# Optimizing a Trainium2 kernel written in Bass

```python
import jax, jax.numpy as jnp
from jax import lax
import numpy as np

D_MODEL = 1024
BATCH = 1
SEQ = 512
DEPTH = 1

N_META = 16
HEAD_DIM = 64
SB_HEADS = D_MODEL // (2 * HEAD_DIM)
RW_HEADS = D_MODEL // (2 * HEAD_DIM)
SB_WIDTH = SB_HEADS * HEAD_DIM
RW_WIDTH = RW_HEADS * HEAD_DIM
DECAY_LORA = 64
AAA_LORA = 64
GATE_LORA = 128
RW_SHIFT_WIDTH = 3 * RW_WIDTH + DECAY_LORA + AAA_LORA + GATE_LORA
P_IN = 3 * SB_WIDTH + RW_SHIFT_WIDTH + 2 * D_MODEL
D_FF = -(-8 * D_MODEL // (3 * 256)) * 256
Q_BLOCK = 128
RMS_EPS = 1e-6
GN_EPS = 64e-5

kernel_name = 'hybrid_stickbreak_rwkv7_block'

def rms_norm(x, g):
    xf = x.astype(jnp.float32)
    y = xf * lax.rsqrt(jnp.mean(xf * xf, axis=-1, keepdims=True) + RMS_EPS)
    return (y * g.astype(jnp.float32)).astype(x.dtype)

def token_shift(p, mu):
    prev = jnp.pad(p, ((0, 0), (1, 0), (0, 0)))[:, :-1]
    return p + mu * (prev - p)

def sb_block(q_blk, q_pos, k, v):
    T = k.shape[2]
    z = jnp.einsum('bhqd,bhsd->bhqs', q_blk, k).astype(jnp.float32) * (HEAD_DIM ** -0.5)
    visible = jnp.arange(T)[None, :] < q_pos[:, None]
    neg_log_1m_beta = jnp.where(visible, jax.nn.softplus(z), 0.0)
    between = lax.cumsum(neg_log_1m_beta, axis=3, reverse=True) - neg_log_1m_beta
    weights = jnp.where(visible, jnp.exp(jax.nn.log_sigmoid(z) - between), 0.0)
    return jnp.einsum('bhqs,bhsd->bhqd', weights.astype(v.dtype), v)

def stick_breaking_attention(q, k, v):
    B, T, _ = q.shape
    S = T - N_META
    nb = S // Q_BLOCK
    to_heads = lambda t: t.reshape(B, T, SB_HEADS, HEAD_DIM).transpose(0, 2, 1, 3)
    q, k, v = to_heads(q), to_heads(k), to_heads(v)
    lead = sb_block(q[:, :, :N_META], jnp.arange(N_META), k, v)
    qb = q[:, :, N_META:].reshape(B, SB_HEADS, nb, Q_BLOCK, HEAD_DIM).transpose(2, 0, 1, 3, 4)
    starts = N_META + Q_BLOCK * jnp.arange(nb)
    body = lambda args: sb_block(args[0], args[1] + jnp.arange(Q_BLOCK), k, v)
    out = lax.map(body, (qb, starts))
    out = out.transpose(1, 2, 0, 3, 4).reshape(B, SB_HEADS, S, HEAD_DIM)
    o = jnp.concatenate([lead, out], axis=2)
    return o.transpose(0, 2, 1, 3).reshape(B, T, SB_WIDTH)

def rwkv7_scan(r, decay, k, v, kk, a):
    B, T, H, N = r.shape

    def step(S, inp):
        r_t, w_t, k_t, v_t, kk_t, a_t = inp
        sa = jnp.einsum('bhvk,bhk->bhv', S, -kk_t)
        S = (S * w_t[:, :, None, :] + sa[..., None] * (kk_t * a_t)[:, :, None, :]
             + v_t[..., None] * k_t[:, :, None, :])
        y = jnp.einsum('bhvk,bhk->bhv', S, r_t)
        return S, y

    xs = tuple(jnp.moveaxis(t, 1, 0) for t in (r, decay, k, v, kk, a))
    S0 = jnp.zeros((B, H, N, N), jnp.float32)
    _, ys = lax.scan(step, S0, xs)
    return jnp.moveaxis(ys, 0, 1)

def rwkv7_time_mix(r, k, v, xw, xa, xg, decay_up, decay_base, aaa_up, aaa_base, gate_up,
                   k_k, k_a, r_k, ln_gain, ln_bias):
    B, T, _ = r.shape
    f32 = jnp.float32
    heads = lambda t: t.astype(f32).reshape(B, T, RW_HEADS, HEAD_DIM)
    w_log = -jax.nn.softplus(-(decay_base + jnp.tanh(xw) @ decay_up)) - 0.5
    decay = jnp.exp(-jnp.exp(w_log.astype(f32)))
    a = jax.nn.sigmoid(aaa_base + xa @ aaa_up)
    g = jax.nn.sigmoid(xg) @ gate_up
    kk = heads(k * k_k)
    kk = kk / jnp.maximum(jnp.sqrt(jnp.sum(kk * kk, axis=-1, keepdims=True)), 1e-12)
    k = k * (1.0 + (a - 1.0) * k_a)
    rh, kh, vh, ah = heads(r), heads(k), heads(v), heads(a)
    y = rwkv7_scan(rh, heads(decay), kh, vh, kk, ah)
    mu = jnp.mean(y, axis=-1, keepdims=True)
    var = jnp.mean(jnp.square(y - mu), axis=-1, keepdims=True)
    y = ((y - mu) * lax.rsqrt(var + GN_EPS)).reshape(B, T, RW_WIDTH)
    y = y * ln_gain.astype(f32) + ln_bias.astype(f32)
    bonus = jnp.sum(rh * kh * r_k.astype(f32), axis=-1, keepdims=True) * vh
    y = (y + bonus.reshape(B, T, RW_WIDTH)) * g.astype(f32)
    return y.astype(r.dtype)

def setup_inputs(seed: int = 0) -> dict:
    key = jax.random.key(seed)
    ks = jax.random.split(key, 26)
    nrm = lambda k, shape, s: jax.random.normal(k, shape, jnp.float32) * s
    L = DEPTH
    return {
        'x': nrm(ks[0], (BATCH, SEQ, D_MODEL), 1.0),
        'meta_tokens': nrm(ks[1], (N_META, D_MODEL), 1.0),
        'norm_mix_pre': 1.0 + nrm(ks[2], (L, D_MODEL), 0.05),
        'norm_mix_post': 1.0 + nrm(ks[3], (L, D_MODEL), 0.05),
        'w_in': nrm(ks[4], (L, D_MODEL, P_IN), D_MODEL ** -0.5),
        'rw_shift_mu': jax.random.uniform(ks[5], (L, RW_SHIFT_WIDTH), jnp.float32),
        'rw_decay_up': nrm(ks[6], (L, DECAY_LORA, RW_WIDTH), 0.5 * DECAY_LORA ** -0.5),
        'rw_decay_base': jax.random.uniform(ks[7], (L, RW_WIDTH), jnp.float32, -6.0, -1.0),
        'rw_aaa_up': nrm(ks[8], (L, AAA_LORA, RW_WIDTH), AAA_LORA ** -0.5),
        'rw_aaa_base': nrm(ks[9], (L, RW_WIDTH), 0.1),
        'rw_gate_up': nrm(ks[10], (L, GATE_LORA, RW_WIDTH), GATE_LORA ** -0.5),
        'rw_k_k': 0.85 + nrm(ks[11], (L, RW_WIDTH), 0.1),
        'rw_k_a': 1.0 + nrm(ks[12], (L, RW_WIDTH), 0.1),
        'rw_r_k': nrm(ks[13], (L, RW_HEADS, HEAD_DIM), 0.1),
        'rw_ln_gain': 1.0 + nrm(ks[14], (L, RW_WIDTH), 0.05),
        'rw_ln_bias': nrm(ks[15], (L, RW_WIDTH), 0.02),
        'w_branch_sb': nrm(ks[16], (L, SB_WIDTH, D_MODEL), SB_WIDTH ** -0.5),
        'w_branch_rw': nrm(ks[17], (L, RW_WIDTH, D_MODEL), RW_WIDTH ** -0.5),
        'w_out': nrm(ks[18], (L, D_MODEL, D_MODEL), D_MODEL ** -0.5),
        'norm_ffn_pre': 1.0 + nrm(ks[19], (L, D_MODEL), 0.05),
        'norm_ffn_post': 1.0 + nrm(ks[20], (L, D_MODEL), 0.05),
        'w_ffn_gate': nrm(ks[21], (L, D_MODEL, D_FF), D_MODEL ** -0.5),
        'w_ffn_up': nrm(ks[22], (L, D_MODEL, D_FF), D_MODEL ** -0.5),
        'w_ffn_down': nrm(ks[23], (L, D_FF, D_MODEL), D_FF ** -0.5),
    }

def reference(x, meta_tokens, norm_mix_pre, norm_mix_post, w_in, rw_shift_mu, rw_decay_up,
              rw_decay_base, rw_aaa_up, rw_aaa_base, rw_gate_up, rw_k_k, rw_k_a, rw_r_k,
              rw_ln_gain, rw_ln_bias, w_branch_sb, w_branch_rw, w_out, norm_ffn_pre,
              norm_ffn_post, w_ffn_gate, w_ffn_up, w_ffn_down):
    B = x.shape[0]
    meta = jnp.broadcast_to(meta_tokens[None].astype(x.dtype), (B, N_META, D_MODEL))
    h = jnp.concatenate([meta, x], axis=1)
    cut = [3 * SB_WIDTH, 3 * SB_WIDTH + RW_SHIFT_WIDTH, 3 * SB_WIDTH + RW_SHIFT_WIDTH + D_MODEL]
    rw_cut = [RW_WIDTH, 2 * RW_WIDTH, 3 * RW_WIDTH, 3 * RW_WIDTH + DECAY_LORA,
              3 * RW_WIDTH + DECAY_LORA + AAA_LORA]
    for l in range(DEPTH):
        u = rms_norm(h, norm_mix_pre[l]) @ w_in[l]
        u_sb, u_rw, gate_sb, gate_rw = jnp.split(u, cut, axis=-1)
        sq, sk, sv = jnp.split(u_sb, 3, axis=-1)
        o_sb = stick_breaking_attention(sq, sk, sv)
        u_rw = token_shift(u_rw, rw_shift_mu[l])
        rr, rk, rv, rxw, rxa, rxg = jnp.split(u_rw, rw_cut, axis=-1)
        o_rw = rwkv7_time_mix(rr, rk, rv, rxw, rxa, rxg, rw_decay_up[l], rw_decay_base[l],
                              rw_aaa_up[l], rw_aaa_base[l], rw_gate_up[l], rw_k_k[l], rw_k_a[l],
                              rw_r_k[l], rw_ln_gain[l], rw_ln_bias[l])
        merged = (jax.nn.sigmoid(gate_sb) * (o_sb @ w_branch_sb[l])
                  + jax.nn.sigmoid(gate_rw) * (o_rw @ w_branch_rw[l]))
        h = h + rms_norm(merged @ w_out[l], norm_mix_post[l])
        f = rms_norm(h, norm_ffn_pre[l])
        f = (jax.nn.silu(f @ w_ffn_gate[l]) * (f @ w_ffn_up[l])) @ w_ffn_down[l]
        h = h + rms_norm(f, norm_ffn_post[l])
    return h[:, N_META:]


_drawn_inputs = setup_inputs


def setup_inputs(seed=0):
    import zlib

    import numpy as np

    out = dict(_drawn_inputs(seed))
    spreads = {}
    factors = {'rw_decay_up': 5.002, 'rw_aaa_base': 2.815, 'rw_ln_bias': 5.548}
    for name, (base, spread) in spreads.items():
        noise = np.random.default_rng([zlib.crc32(name.encode()), seed]).standard_normal(out[name].shape)
        drawn = base * np.exp(spread * noise) if base else spread * noise
        out[name] = __import__('jax').numpy.asarray(drawn.astype(out[name].dtype))
    for name, factor in factors.items():
        out[name] = (out[name] * factor).astype(out[name].dtype)
    return out
```

```python
from contextlib import ExitStack

import concourse.bass as bass
from concourse import mybir

F32 = mybir.dt.float32
F32R = mybir.dt.float32r
U8 = mybir.dt.uint8
ALU = mybir.AluOpType
ACT = mybir.ActivationFunctionType

P = 128
D = 1024
SEQ = 512
META = 16
T = META + SEQ
HALF = T // 2
KT = D // P
HD = 64
PAIRS = 4
C = 64
PAD = C - META
NC_ = 1 + SEQ // C
TP = NC_ * C
LEVELS = 6
DFF = 2816
FT = DFF // P
QB = SEQ // P
RMS_EPS = 1e-6
GN_EPS = 64e-5
DEC = 0.6065306597126334
BIG_Z = 40.0
HIDDEN = -1e30

SQ, SK, SV, RR, RK, RV, XWA, XG, GSB, GRW = 0, 4, 8, 12, 16, 20, 24, 25, 26, 34

V_MU, V_DB, V_AB, V_KK, V_KA, V_RK, V_LG, V_LB = 0, 14, 18, 22, 26, 30, 34, 38
NVEC = 42

K_ID, K_TRI, K_CTRI, K_BLK, K_BDS, K_LE, K_ST, K_RST = 0, 128, 256, 384, 512, 640, 704, 768
NK = K_RST + T
B_X, B_XT, B_BD = 0, LEVELS * C, 2 * LEVELS * C
NB = 4 * LEVELS * C

RAW = 4
SPL = 2

ORDER = [("xwa", XWA, 0), ("xg", XG, 0)]
for _p in range(PAIRS):
    ORDER += [("r", RR + _p, _p), ("k", RK + _p, _p), ("v", RV + _p, _p), ("sk", SK + _p, _p)]
ORDER += [("sv", SV + _p, _p) for _p in range(PAIRS)] + [("sq", SQ + _p, _p) for _p in range(PAIRS)]
N_IN = len(ORDER)
AHEAD = 3
MERGE = []
for _j in range(KT + AHEAD):
    if _j >= AHEAD:
        MERGE += [("branch", _j - AHEAD)]
    if _j < KT:
        MERGE += [("gate_sb", _j), ("gate_rw", _j)]
U_MIX = N_IN
U_OUT = U_MIX + 3 * KT
U_FFN = U_OUT + KT
U_DOWN = U_FFN + 2 * FT
N_UNITS = U_DOWN + FT
N_FFN_LOOP = 2 * FT // RAW
assert U_FFN % SPL == 0 and 2 * FT % RAW == 0 and RAW % SPL == 0

PREP_PE = ["decay", "aaa", "norm", "bonus"]
PREP_ACT = ["sig", "aaa", "ksq", "inc", "inv", "exc", "rnorm"]
PREP_DVE = ["csum", "csum_x", "max", "recip", "kk", "kkn", "a", "bneg", "b", "kmod", "bonus"]
PREP_POOL = ["chunk", "kmod", "k", "r", "rk", "rks"]
_lv = range(1, LEVELS)
SCAN_PE = ["A0", "A1", "A2", "T0", "T1", "T2"] + [f"{s}{j}" for j in _lv for s in ("W", "X", "Y")] + \
          ["Z", "SA", "OUT", "S"]
SCAN_PE.remove(f"X{LEVELS - 1}")
SCAN_ACT = ["bh0", "bh1", "kh0", "kh1", "vs0", "vs1", "vb0", "vb1"] + \
           [f"{s}{j}" for j in _lv for s in ("w", "wb0_", "wb1_")] + ["z", "sa", "sab0", "sab1", "out", "sb0", "sb1"]
SCAN_DVE = ["aab", "xt0", "xtb0", "arb", "aak", "ark", "x0"] + \
           [f"{s}{j}" for j in _lv for s in ("x", "xt", "xtb")] + ["decay", "s"]
SCAN_DVE.remove(f"x{LEVELS - 1}")
SCAN_DVE.remove(f"xt{LEVELS - 1}")
SCAN_POOL = ["b0", "b1", "k0", "k1", "ix", "ixt", "ixtb", "a0", "a1", "kh", "bh"]
ATT_PE = ["Q0", "Q1", "Q2", "Q3", "Q4", "C3", "C2", "C1", "C0", "C4", "O"]
ATT_ACT = ["z0", "z1", "z2", "z3", "z4", "exp", "ln", "w", "wm", "o"]
ATT_DVE = ["min", "max", "s3", "s2", "s1", "s0", "s4"]
ATT_POOL = ["m0", "m1", "m2", "m3"]
POST_PE = ["mean0", "mean1", "var0", "var1", "gate0", "gate1"]
POST_ACT = ["sq0", "sq1", "sqrt0", "sqrt1", "hi0", "hi1"]
POST_DVE = ["centre0", "centre1", "var0", "recip0", "var1", "recip1"] + \
           [f"{s}{i}" for i in range(2) for s in ("norm", "gain", "bonus", "out", "lo")]
TAIL_1 = [f"{s}{b}" for b in range(QB) for s in ("ms", "rec")] + \
         [f"{s}{b}" for b in range(QB) for s in ("z", "res")] + \
         [f"{s}{b}" for b in range(QB) for s in ("ms_f", "rec_f")] + [f"xn{b}" for b in range(QB)]
TAIL_FFN = ["silu", "act", "hi", "lo"]
TAIL_2 = [f"{s}{b}" for b in range(QB) for s in ("ms", "rec")] + \
         [f"{s}{b}" for b in range(QB) for s in ("z", "res")]
FFN_AT = len(TAIL_1)
LAST_AT = FFN_AT + FT * len(TAIL_FFN)


def after(steps, n, step):
    return n * len(steps) + steps.index(step) + 1


def build(nc, x, meta, w_in, w_sb, w_rw, w_out, w_g, w_u, w_d, decay_up, aaa_up, gate_up,
          vecs, g_mix_pre, g_mix_post, g_ffn_pre, g_ffn_post, kf, kb, out):
    with ExitStack() as ctx:
        def sem(name):
            return ctx.enter_context(nc.semaphore(name))

        base = (nc.sbuf_base + 31) // 32 * 32
        end = nc.sbuf_usable_end
        cursor = [base]

        def sb(name, shape, dt=F32):
            size = 1
            for n in shape[1:]:
                size *= n
            size *= 1 if dt == U8 else 4
            t = nc.alloc_sbuf_tensor_at(name, shape, dt, offset=cursor[0])
            cursor[0] += (size + 31) // 32 * 32
            assert cursor[0] <= end, (name, cursor[0], end)
            return t

        raw = [sb(f"w_raw{i}", [P, 1024]) for i in range(RAW)]
        w_hi = [sb(f"w_hi{i}", [P, 1024], F32R) for i in range(SPL)]
        w_lo = [sb(f"w_lo{i}", [P, 1024], F32R) for i in range(SPL)]
        consts = sb("consts", [P, NK])
        bytes_ = sb("byte_masks", [P, NB], U8)
        vrow = sb("vec_rows", [NVEC, P])
        vcol = sb("vec_cols", [P, NVEC + 4])
        small = sb("small", [P, 32])
        lora = sb("lora", [P, 512])
        gup = sb("gate_up_w", [P, 512])
        ident = consts[:, K_ID:K_ID + P]
        tri = consts[:, K_TRI:K_TRI + P]
        ctri = consts[:, K_CTRI:K_CTRI + P]
        blk = consts[:, K_BLK:K_BLK + P]
        bd_strict = consts[:, K_BDS:K_BDS + P]
        st_le = consts[:, K_LE:K_LE + C]
        st_id = consts[:, K_ST:K_ST + C]
        reset = consts[:, K_RST:K_RST + T]

        h_hi = sb("h_hi", [P, KT, T], F32R)
        h_lo = sb("h_lo", [P, KT, T], F32R)
        ffn_at = cursor[0]
        qT = sb("qT", [P, PAIRS, SEQ])
        kv_at = cursor[0]
        kT = sb("kT", [P, PAIRS, T])
        vtok = sb("v_tok", [P, QB, 512])
        vmeta = sb("v_meta", [META, 512])
        ar = sb("a_r", [P, 2, PAIRS, TP])
        bk_at = cursor[0]
        bt = sb("b_t", [P, PAIRS, TP])
        kt = sb("k_t", [P, PAIRS, TP])
        vv = sb("v_t", [P, PAIRS, TP])
        sg = sb("sig_xg", [P, T])
        bonus = sb("bonus", [P, PAIRS, SEQ])
        pc = sb("p_chunk", [P, PAIRS, NC_])
        mix_at = cursor[0]

        xb = [sb(f"x_in{i}", [P, D]) for i in range(5)]
        xn = [sb(f"x_norm{i}", [P, D]) for i in range(5)]
        g_row = sb("g_row", [P, D])
        masks_f = sb("masks_f", [P, NB])

        cursor[0] = mix_at
        stage = [sb(f"shift_in{i}", [P, T + 1]) for i in range(3)]
        diff = sb("shift_diff", [P, T])
        twx = sb("tanh_xw_xa", [P, T])
        rp = [sb(f"r_pair{i}", [P, T]) for i in range(2)]
        kp = [sb(f"k_pair{i}", [P, T]) for i in range(2)]
        vst = [sb(f"v_stage{i}", [P, T]) for i in range(2)]
        sig_w = sb("sig_w", [P, T])
        csum = sb("csum", [P, T])
        csum_x = sb("csum_x", [P, T])
        p_inc = sb("p_inc", [P, T])
        p_inv = sb("p_inv", [P, T])
        p_exc = sb("p_exc", [P, T])
        a_gate = sb("a_gate", [P, T])
        ksq = sb("k_sq", [P, T])
        rnorm = sb("r_norm", [P, T])
        kkn = sb("kk_n", [P, T])
        bneg = sb("b_neg", [P, T])
        kmod = sb("k_mod", [P, T])
        rkp = sb("rk_prod", [P, T])

        cursor[0] = mix_at
        a_bd = sb("a_bd", [P, PAIRS, P])
        b_bd = sb("b_bd", [P, PAIRS, P])
        k_bd = sb("k_bd", [P, PAIRS, P])
        aab_bd = sb("aab_bd", [P, PAIRS, P])
        aak_bd = sb("aak_bd", [P, PAIRS, P])
        arb = sb("arb", [P, PAIRS, C])
        ark = sb("ark", [P, PAIRS, C])
        x_st = sb("x_st", [P, PAIRS, C])
        xt_st = sb("xt_st", [P, PAIRS, C])
        xt_bd = sb("xt_bd", [P, PAIRS, P])
        w_st = sb("w_st", [P, PAIRS, C])
        w_bd = sb("w_bd", [P, PAIRS, P])
        bh_bd = sb("bh_bd", [P, PAIRS, P])
        kh_bd = sb("kh_bd", [P, PAIRS, P])
        v_st = sb("v_st", [P, PAIRS, C])
        v_bd = sb("v_bd", [P, PAIRS, P])
        z_st = sb("z_st", [P, PAIRS, C])
        sa_st = sb("sa_st", [P, PAIRS, C])
        sa_bd = sb("sa_bd", [P, PAIRS, P])
        s_st = sb("s_st", [P, PAIRS, C])
        s_bd = sb("s_bd", [P, PAIRS, P])
        NS = 1280 + SEQ
        zs = sb("scores", [P, NS])
        sp_ = sb("softplus", [P, NS])

        cursor[0] = mix_at
        mg_hi = sb("merged_hi", [P, KT, SEQ], F32R)
        mg_lo = sb("merged_lo", [P, KT, SEQ], F32R)
        sig_t = [sb(f"sig_t{i}", [P, SEQ]) for i in range(2 * AHEAD)]
        mrg_t = [sb(f"merge_t{i}", [P, SEQ]) for i in range(2)]
        mix_end = cursor[0]
        cursor[0] = kv_at
        osb_hi = sb("osb_hi", [P, PAIRS, SEQ], F32R)
        osb_lo = sb("osb_lo", [P, PAIRS, SEQ], F32R)
        cursor[0] = bk_at
        orw_hi = sb("orw_hi", [P, PAIRS, SEQ], F32R)
        orw_lo = sb("orw_lo", [P, PAIRS, SEQ], F32R)
        cursor[0] = mix_at
        ysq = [sb(f"y_sq{i}", [P, SEQ]) for i in range(2)]
        yvar = [sb(f"y_var{i}", [P, SEQ]) for i in range(2)]
        yrec = [sb(f"y_rec{i}", [P, SEQ]) for i in range(2)]
        yrs = [sb(f"y_rs{i}", [P, SEQ]) for i in range(2)]
        yo = [sb(f"y_o{i}", [P, SEQ]) for i in range(2)]

        cursor[0] = ffn_at
        resid = sb("resid", [P, QB, D])
        grows = sb("g_rows", [P, 3, D])
        assert cursor[0] <= mix_at, (cursor[0], mix_at)
        act_at = cursor[0]
        act_hi = sb("act_hi", [P, FT, SEQ], F32R)
        act_lo = sb("act_lo", [P, FT, SEQ], F32R)
        ffn_t = [sb(f"ffn_t{i}", [P, SEQ]) for i in range(2)]
        ffn_u = [sb(f"ffn_u{i}", [P, SEQ]) for i in range(2)]
        cursor[0] = act_at
        ztok = [sb(f"z_tok{b}", [P, D]) for b in range(QB)]
        psum = ctx.enter_context(nc.psum_tensor("psum", [P, 8, 512], F32))

        def bank(b, n=512):
            return psum[:, b, 0:n]

        def both(b):
            return psum[:, b:b + 2, 0:HALF]

        def halves(ap):
            return ap.rearrange("p (a b) -> p a b", a=2)

        def quads(b, n):
            return psum[:, b, 0:PAIRS * n].rearrange("p (q n) -> p q n", q=PAIRS)

        const_in = sem("const_in")
        x_in = [sem(f"x_in{i}") for i in range(5)]
        rows_in = sem("rows_in")
        resid_in = sem("resid_in")
        w_in_raw = [sem(f"w_landed{i}") for i in range(RAW)]
        w_hi_done = sem("w_hi_done")
        w_split = sem("w_split")
        w_used = sem("w_used")
        n_sq = sem("norm_sq")
        n_dve = sem("norm_dve")
        n_rs = sem("norm_rs")
        n_x = sem("norm_x")
        n_tp = sem("norm_transposed")
        n_hi = sem("norm_hi")
        n_lo = sem("norm_lo")
        vec_tp = sem("vec_tp")
        vec_ok = sem("vec_ok")
        edge = sem("edge_zero")
        in_out = sem("in_out")
        sh_diff = sem("shift_diff")
        shifted = sem("shifted")
        lora_act = sem("lora_act")
        v_tp = sem("v_tp")
        v_out = sem("v_out")
        prep_pe, prep_act, prep_dve, prep_pool = (sem(f"prep_{e}") for e in ("pe", "act", "dve", "pool"))
        mix_zero = sem("mix_zero")
        scan_pe, scan_act, scan_dve, scan_pool = (sem(f"scan_{e}") for e in ("pe", "act", "dve", "pool"))
        att_pe, att_act, att_dve, att_pool = (sem(f"att_{e}") for e in ("pe", "act", "dve", "pool"))
        post_pe, post_act, post_dve = (sem(f"post_{e}") for e in ("pe", "act", "dve"))
        osb_h = sem("osb_h")
        osb_l = sem("osb_l")
        gate_out = sem("gate_out")
        mrg_dve = sem("merge_dve")
        mrg_hi = sem("merge_hi")
        tail_sq = sem("tail_sq")
        tail_rs = sem("tail_rs")
        tail_dve = sem("tail_dve")
        f_sig = sem("ffn_sig")
        n_rows = sem("norm_rows_free")
        stored = sem("stored")

        block = ctx.enter_context(nc.Block())

        def tile_of(w, f):
            return w[:, f * P:(f + 1) * P].rearrange("(k p) n -> p k n", p=P)

        def raw3(u, k=KT):
            return raw[u % RAW][:, 0:k * P].rearrange("p (k n) -> p k n", k=k)

        def load_unit(sp, u):
            if u >= RAW:
                sp.wait_ge(w_split, u - RAW + 1)
            if u < U_MIX:
                sp.dma_start(raw3(u), tile_of(w_in, ORDER[u][1])).then_inc(w_in_raw[u % RAW], 16)
            elif u < U_OUT:
                kind, j = MERGE[u - U_MIX]
                if kind == "branch":
                    half = KT // 2
                    sp.dma_start(raw3(u)[:, 0:half], tile_of(w_sb, j)).then_inc(w_in_raw[u % RAW], 16)
                    sp.dma_start(raw3(u)[:, half:KT], tile_of(w_rw, j)).then_inc(w_in_raw[u % RAW], 16)
                else:
                    f = (GSB if kind == "gate_sb" else GRW) + j
                    sp.dma_start(raw3(u), tile_of(w_in, f)).then_inc(w_in_raw[u % RAW], 16)
            elif u < U_FFN:
                k = u - U_OUT
                sp.dma_start(raw[u % RAW][:], w_out[k * P:(k + 1) * P, :]).then_inc(w_in_raw[u % RAW], 16)
            else:
                k = u - U_DOWN
                sp.dma_start(raw[u % RAW][:], w_d[k * P:(k + 1) * P, :]).then_inc(w_in_raw[u % RAW], 16)

        def landed(u):
            n = sum(1 + (U_MIX <= v < U_OUT and MERGE[v - U_MIX][0] == "branch")
                    for v in range(u % RAW, u + 1, RAW))
            return 16 * n

        def hi_unit(act, u):
            act.wait_ge(w_in_raw[u % RAW], landed(u))
            if u >= SPL:
                act.wait_ge(w_used, u - SPL + 1)
            nc.scalar.activation(w_hi[u % SPL][:], raw[u % RAW][:], ACT.Copy).then_inc(w_hi_done, 1)

        def lo_unit(dve, u):
            dve.wait_ge(w_hi_done, u + 1)
            nc.vector.tensor_sub(w_lo[u % SPL][:], raw[u % RAW][:],
                                 w_hi[u % SPL][:].bitcast(F32)).then_inc(w_split, 1)

        def products(u, w0, outs, xh, xl, kts, last=False):
            hi, lo = w_hi[u % SPL], w_lo[u % SPL]
            n = 0
            total = 3 * len(kts)
            for i, k in enumerate(kts):
                for w, xs in ((hi, xh), (hi, xl), (lo, xh)):
                    for o, (c0, c1) in outs:
                        mm = nc.tensor.matmul(o, w[:, (w0 + i) * P:(w0 + i + 1) * P], xs[:, k, c0:c1],
                                              start=(n == 0), stop=(n == total - 1))
                    n += 1
            return mm

        scan_steps = [("scan", c, s) for c in range(NC_)
                      for s in ["A", "T"] + [f"{t}{j}" for j in range(1, LEVELS) for t in ("W", "X")] +
                      ["Z", "SA", "OUT", "S"]]
        att_steps = [("att", h, s) for h in range(2 * PAIRS)
                     for s in ("Q0", "Q1", "Q2", "Q3", "Q4", "P", "C3", "C2", "C1", "C0", "C4", "O")]
        mixing = []
        for i, s in enumerate(scan_steps):
            mixing.append(s)
            mixing += att_steps[i * len(att_steps) // len(scan_steps):(i + 1) * len(att_steps) // len(scan_steps)]

        WIDTH = [SEQ - P * j for j in range(QB)] + [SEQ]
        OFF = [sum(WIDTH[:j]) for j in range(QB + 1)]
        KEYS = [(META + P * j, P) for j in range(QB)] + [(0, META)]
        B0, B1, B2 = 4, 5, 6
        QBANK, CBANK, OBANK = (2, 3), 0, 7

        def cols(c):
            return slice(c * C, (c + 1) * C)

        def top(ap, h):
            return ap[h * C:(h + 1) * C, :, h * C:(h + 1) * C]

        @block.sync
        def _(sp):
            sp.dma_start(xb[4][0:META, :], meta).then_inc(x_in[4], 16)
            sp.dma_start(g_row[:], g_mix_pre.to_broadcast([P, D])).then_inc(x_in[4], 16)
            for b in range(QB):
                sp.dma_start(xb[b][:], x[b * P:(b + 1) * P, :]).then_inc(x_in[b], 16)
            for dst, src in ((consts[:], kf), (masks_f[:], kb), (vrow[:], vecs), (lora[0:64, :], decay_up),
                             (lora[64:P, :], aaa_up), (gup[:], gate_up)):
                sp.dma_start(dst, src).then_inc(const_in, 16)
            for u in range(U_FFN):
                if u == U_OUT + RAW:
                    sp.wait_ge(w_used, U_OUT)
                    for i, g in enumerate((g_mix_post, g_ffn_pre, g_ffn_post)):
                        sp.dma_start(grows[:, i, :], g.to_broadcast([P, D])).then_inc(rows_in, 16)
                    sp.dma_start(resid[:], x.rearrange("(b p) d -> p b d", p=P)).then_inc(resid_in, 16)
                load_unit(sp, u)
            with sp.Fori(0, N_FFN_LOOP) as i:
                for s in range(RAW):
                    sp.wait_ge(w_split, i * RAW + (U_FFN + s - RAW + 1))
                    f = i * (RAW // 2) + s // 2
                    w = (w_g, w_u)[s % 2]
                    sl = (U_FFN + s) % RAW
                    sp.dma_start(raw[sl][:, :].rearrange("p (k n) -> p k n", k=KT),
                                 w.rearrange("(k p) n -> p k n", p=P)[:, :, bass.ds(f * P, P)]
                                 ).then_inc(w_in_raw[sl], 16)
            for u in range(U_DOWN, N_UNITS):
                load_unit(sp, u)
            for b in range(QB):
                sp.wait_ge(tail_dve, LAST_AT + TAIL_2.index(f"res{b}") + 1)
                sp.dma_start(out[b * P:(b + 1) * P, :], resid[:, b, :]).then_inc(stored, 16)
            sp.wait_ge(stored, 16 * QB)

        @block.gpsimd
        def _(pool):
            g = nc.gpsimd
            pool.wait_ge(const_in, 16 * 6)
            g.tensor_copy(bytes_[:], masks_f[:]).then_inc(edge, 1)
            for t in stage:
                pool.wait_ge(n_x, 5)
                g.memset(t[:, 0:1], 0.0).then_inc(edge, 1)
            for t in (ar[:, 0], ar[:, 1], bt, kt, vv):
                g.memset(t[:, :, 0:PAD], 0.0).then_inc(edge, 1)
            for p in range(PAIRS):
                pool.wait_ge(prep_act, after(PREP_ACT, p, "inc"))
                g.tensor_copy(pc[:, p, :], p_inc[:, C - 1 - PAD::C]).then_inc(prep_pool, 1)
                pool.wait_ge(prep_dve, after(PREP_DVE, p, "kmod"))
                g.tensor_tensor(kmod[:], kmod[:], kp[p % 2][:], ALU.mult).then_inc(prep_pool, 1)
                pool.wait_ge(prep_pool, after(PREP_POOL, p, "kmod"))
                pool.wait_ge(prep_act, after(PREP_ACT, p, "inv"))
                g.tensor_tensor(kt[:, p, PAD:TP], kmod[:], p_inv[:], ALU.mult).then_inc(prep_pool, 1)
                g.tensor_tensor(ar[:, 1, p, PAD:TP], rp[p % 2][:], p_inc[:], ALU.mult).then_inc(prep_pool, 1)
                if p >= 1:
                    pool.wait_ge(prep_pe, after(PREP_PE, p - 1, "bonus"))
                g.tensor_tensor(rkp[:], rp[p % 2][:], kmod[:], ALU.mult).then_inc(prep_pool, 1)
                pool.wait_ge(prep_pool, after(PREP_POOL, p, "rk"))
                g.tensor_scalar(rkp[:], rkp[:], vcol[:, V_RK + p:V_RK + p + 1], None,
                                ALU.mult).then_inc(prep_pool, 1)
            pool.wait_ge(prep_dve, after(PREP_DVE, PAIRS - 1, "bonus"))
            pool.wait_ge(prep_act, after(PREP_ACT, PAIRS - 1, "rnorm"))
            pool.wait_ge(prep_pe, after(PREP_PE, PAIRS - 1, "bonus"))
            pool.wait_ge(v_tp, PAIRS)
            for t in (b_bd, k_bd, a_bd, w_bd, bh_bd, kh_bd, v_bd, sa_bd, s_bd, s_st, zs):
                g.memset(t[:], 0.0).then_inc(mix_zero, 1)
            pool.wait_ge(mix_zero, 11)
            heads = 0
            for kind, n, s in mixing:
                if (kind, s) == ("scan", "A"):
                    c = n
                    if c:
                        pool.wait_ge(scan_pool, c * len(SCAN_POOL))
                    if heads:
                        pool.wait_ge(att_pool, heads * len(ATT_POOL))
                        pool.wait_ge(scan_pe, after(SCAN_PE, c - 1, "S"))
                    for src, dst in ((bt, b_bd), (kt, k_bd)):
                        for h in range(2):
                            g.tensor_copy(top(dst, h), src[h * C:(h + 1) * C, :, cols(c)]).then_inc(scan_pool, 1)
                    pool.wait_ge(scan_pool, after(SCAN_POOL, c, "k1"))
                    g.tensor_copy(x_st[:], st_id.unsqueeze(1).to_broadcast([P, PAIRS, C])).then_inc(scan_pool, 1)
                    g.tensor_copy(xt_st[:], st_id.unsqueeze(1).to_broadcast([P, PAIRS, C])).then_inc(scan_pool, 1)
                    g.tensor_copy(xt_bd[:], ident.unsqueeze(1).to_broadcast([P, PAIRS, P])).then_inc(scan_pool, 1)
                    pool.wait_ge(scan_pool, after(SCAN_POOL, c, "ixtb"))
                    for h in range(2):
                        g.tensor_copy(top(a_bd, h), ar[h * C:(h + 1) * C, 0, :, cols(c)]).then_inc(scan_pool, 1)
                    pcb = pc[:, :, c:c + 1].to_broadcast([P, PAIRS, C])
                    pool.wait_ge(scan_pool, after(SCAN_POOL, c, "a1"))
                    g.tensor_tensor(kt[:, :, cols(c)], kt[:, :, cols(c)], pcb, ALU.mult).then_inc(scan_pool, 1)
                    pool.wait_ge(scan_pe, after(SCAN_PE, c, "A2"))
                    g.tensor_tensor(bt[:, :, cols(c)], bt[:, :, cols(c)], pcb, ALU.mult).then_inc(scan_pool, 1)
                if (kind, s) == ("att", "Q4"):
                    for j in range(QB):
                        pool.wait_ge(att_act, after(ATT_ACT, n, f"z{j}"))
                        d = zs[:, OFF[j]:OFF[j] + P]
                        g.affine_select(out=d, in_=d, compare_op=ALU.is_gt, fill=HIDDEN, base=0,
                                        pattern=[[1, P]], channel_multiplier=-1).then_inc(att_pool, 1)
                    heads += 1

        def late_items():
            gates = [m for m in MERGE if m[0] != "branch"][:2 * AHEAD]
            it = iter(range(2 * AHEAD))
            items = [("osb", 0)]
            for r in range(2):
                items += [("mean", r), ("unit", next(it)), ("var", r), ("unit", next(it)), ("gate", r),
                          ("unit", next(it))]
            return items + [("unit", i) for i in range(2 * AHEAD, len(MERGE))]

        LATE = late_items()

        def gate_no(i):
            kind, j = MERGE[i]
            return 2 * j + (kind == "gate_rw")

        def y_of(p):
            return ar[:, 0, p, C:TP]

        def norm_cols(b):
            return (0, META) if b == 4 else (META + P * b, P)

        @block.scalar
        def _(act):
            s_ = nc.scalar

            def norm_hi(n, width, c0):
                for h in range(2):
                    act.wait_ge(n_tp, n + h + 1)
                    s_.activation(h_hi[:, 4 * h:4 * h + 4, c0:c0 + width], quads((n + h) % 4, width),
                                  ACT.Copy).then_inc(n_hi, 1)

            act.wait_ge(n_dve, 1)
            for b in (4, 0, 1, 2, 3):
                n = META if b == 4 else P
                act.wait_ge(x_in[b], 32 if b == 4 else 16)
                s_.activation(xn[b][0:n, :], xb[b][0:n, :], ACT.Square,
                              accum_out=small[0:n, b:b + 1]).then_inc(n_sq, 1)
            act.wait_ge(vec_tp, 1)
            s_.activation(vcol[:, 0:NVEC], psum[:, 7, 0:NVEC], ACT.Copy).then_inc(vec_ok, 1)
            act.wait_ge(n_dve, 3)
            s_.activation(small[:, 24:29], small[:, 16:21], ACT.Sqrt).then_inc(n_rs, 1)
            hi_unit(act, 0)
            for i, b in enumerate((4, 0, 1, 2, 3)):
                c0, width = norm_cols(b)
                norm_hi(2 * i, width, c0)
            hi_unit(act, 1)

            n_shift = 0
            for u, (kind, f, p) in enumerate(ORDER):
                act.wait_ge(w_used, u + 1)
                if u == 0:
                    act.wait_ge(edge, 9)
                ps = both(2 * (u % 2))
                if kind in ("xwa", "xg", "r", "k", "v"):
                    if n_shift >= 3:
                        act.wait_ge(shifted, n_shift - 2)
                    s_.activation(halves(stage[n_shift % 3][:, 1:T + 1]), ps, ACT.Copy).then_inc(in_out, 1)
                    n_shift += 1
                elif kind == "sk":
                    s_.activation(halves(kT[:, p, :]), ps, ACT.Copy).then_inc(in_out, 1)
                elif kind == "sv":
                    if p >= 2:
                        act.wait_ge(v_tp, p - 1)
                    s_.activation(halves(vst[p % 2][:]), ps, ACT.Copy).then_inc(in_out, 1)
                else:
                    s_.activation(qT[:, p, :], bank(2 * (u % 2)), ACT.Copy, scale=HD ** -0.5).then_inc(in_out, 1)
                hi_unit(act, u + 2)
                if u == 1:
                    act.wait_ge(shifted, 1)
                    s_.activation(twx[0:64, :], twx[0:64, :], ACT.Tanh).then_inc(lora_act, 1)
                if u == 2:
                    act.wait_ge(shifted, 2)
                    s_.activation(sg[:], sg[:], ACT.Sigmoid).then_inc(lora_act, 1)
                    act.wait_ge(vec_ok, 2)
                q, step = divmod(u - 5, 4)
                if q in range(PAIRS) and step == 0:
                    act.wait_ge(prep_pe, after(PREP_PE, q, "decay"))
                    if q:
                        act.wait_ge(prep_dve, after(PREP_DVE, q - 1, "kmod"))
                    s_.activation(halves(sig_w[:]), both(4), ACT.Sigmoid,
                                  bias=vcol[:, V_DB + q:V_DB + q + 1]).then_inc(prep_act, 1)
                    act.wait_ge(prep_pe, after(PREP_PE, q, "aaa"))
                    s_.activation(halves(a_gate[:]), both(6), ACT.Sigmoid,
                                  bias=vcol[:, V_AB + q:V_AB + q + 1]).then_inc(prep_act, 1)
                    act.wait_ge(shifted, 2 + 3 * q + 2)
                    s_.activation(ksq[:], kp[q % 2][:], ACT.Square,
                                  scale=vcol[:, V_KK + q:V_KK + q + 1]).then_inc(prep_act, 1)
                if q in range(PAIRS) and step == 1:
                    if q:
                        act.wait_ge(prep_pool, after(PREP_POOL, q - 1, "rks"))
                    act.wait_ge(prep_dve, after(PREP_DVE, q, "csum"))
                    s_.activation(p_inc[:], csum[:], ACT.Exp, scale=-DEC).then_inc(prep_act, 1)
                    s_.activation(p_inv[:], csum[:], ACT.Exp, scale=DEC).then_inc(prep_act, 1)
                    act.wait_ge(prep_dve, after(PREP_DVE, q, "csum_x"))
                    s_.activation(p_exc[:], csum_x[:], ACT.Exp, scale=-DEC).then_inc(prep_act, 1)
                if q in range(PAIRS) and step == 2:
                    act.wait_ge(prep_dve, after(PREP_DVE, q, "recip"))
                    s_.activation(rnorm[:], rnorm[:], ACT.Sqrt).then_inc(prep_act, 1)
                if 19 <= u < 23:
                    act.wait_ge(v_tp, u - 18)
                    o = u - 19
                    s_.activation(vtok[:, :, P * o:P * o + P], quads(4, P), ACT.Copy).then_inc(v_out, 1)
                    s_.activation(vmeta[:, P * o:P * o + P], psum[0:META, 5, 0:P], ACT.Copy).then_inc(v_out, 1)

            act.wait_ge(mix_zero, 11)
            for kind, n, s in mixing:
                if kind == "scan":
                    c = n
                    if s == "T":
                        for name, bnk, dst in (("T0", B0, bh_bd), ("T1", B1, kh_bd)):
                            act.wait_ge(scan_pe, after(SCAN_PE, c, name))
                            for h in range(2):
                                s_.activation(top(dst, h), quads(bnk, P)[0:C, :, h * C:(h + 1) * C],
                                              ACT.Copy).then_inc(scan_act, 1)
                        act.wait_ge(scan_pe, after(SCAN_PE, c, "T2"))
                        for h in range(2):
                            s_.activation(v_st[h * C:(h + 1) * C], quads(B2, P)[0:C, :, h * C:(h + 1) * C],
                                          ACT.Copy).then_inc(scan_act, 1)
                        for h in range(2):
                            s_.activation(top(v_bd, h), quads(B2, P)[0:C, :, h * C:(h + 1) * C],
                                          ACT.Copy).then_inc(scan_act, 1)
                    if s[0] == "W":
                        act.wait_ge(scan_pe, after(SCAN_PE, c, s))
                        s_.activation(w_st[:], quads(B0, C), ACT.Copy).then_inc(scan_act, 1)
                        for h in range(2):
                            s_.activation(top(w_bd, h), quads(B0, C)[h * C:(h + 1) * C],
                                          ACT.Copy).then_inc(scan_act, 1)
                    if s == "Z":
                        act.wait_ge(scan_pe, after(SCAN_PE, c, "Z"))
                        if c:
                            act.wait_ge(scan_dve, after(SCAN_DVE, c - 1, "s"))
                        s_.activation(z_st[:], quads(B0, C), ACT.Copy).then_inc(scan_act, 1)
                    if s == "SA":
                        act.wait_ge(scan_pe, after(SCAN_PE, c, "SA"))
                        s_.activation(sa_st[:], quads(B1, C), ACT.Copy).then_inc(scan_act, 1)
                        for h in range(2):
                            s_.activation(top(sa_bd, h), quads(B1, C)[h * C:(h + 1) * C],
                                          ACT.Copy).then_inc(scan_act, 1)
                    if s == "OUT":
                        act.wait_ge(scan_pe, after(SCAN_PE, c, "OUT"))
                        s_.activation(ar[:, 0, :, cols(c)], quads(B2, C), ACT.Copy).then_inc(scan_act, 1)
                    if s == "S":
                        act.wait_ge(scan_dve, after(SCAN_DVE, c, "s"))
                        for h in range(2):
                            s_.activation(top(s_bd, h), s_st[h * C:(h + 1) * C], ACT.Copy).then_inc(scan_act, 1)
                else:
                    h = n
                    hp, hr = h // 2, h % 2
                    if s[0] == "Q":
                        j = int(s[1])
                        rows = META if j == 4 else P
                        act.wait_ge(att_pe, after(ATT_PE, h, s))
                        if j == 0 and h:
                            act.wait_ge(att_pe, after(ATT_PE, h - 1, "O"))
                        s_.activation(zs[0:rows, OFF[j]:OFF[j] + WIDTH[j]], psum[0:rows, QBANK[j % 2], 0:WIDTH[j]],
                                      ACT.Copy).then_inc(att_act, 1)
                    if s == "P":
                        act.wait_ge(att_dve, after(ATT_DVE, h, "min"))
                        s_.activation(sp_[:], sp_[:], ACT.Exp).then_inc(att_act, 1)
                        act.wait_ge(att_act, after(ATT_ACT, h, "exp"))
                        s_.activation(sp_[:], sp_[:], ACT.Ln, bias=1.0).then_inc(att_act, 1)
                    if s == "O":
                        act.wait_ge(att_dve, after(ATT_DVE, h, "s0"))
                        s_.activation(zs[:, 0:OFF[4]], zs[:, 0:OFF[4]], ACT.Exp).then_inc(att_act, 1)
                        act.wait_ge(att_dve, after(ATT_DVE, h, "s4"))
                        s_.activation(zs[0:META, OFF[4]:NS], zs[0:META, OFF[4]:NS], ACT.Exp).then_inc(att_act, 1)
                        act.wait_ge(att_pe, after(ATT_PE, h, "O"))
                        s_.activation(qT[hr * HD:(hr + 1) * HD, hp, :], psum[hr * HD:(hr + 1) * HD, OBANK, :],
                                      ACT.Copy).then_inc(att_act, 1)

            for kind, i in LATE:
                if kind == "osb":
                    act.wait_ge(att_act, 2 * PAIRS * len(ATT_ACT))
                    act.wait_ge(att_pe, 2 * PAIRS * len(ATT_PE))
                    s_.activation(osb_hi[:], qT[:], ACT.Copy).then_inc(osb_h, 1)
                if kind == "mean":
                    for q in range(2):
                        act.wait_ge(post_dve, after(POST_DVE, i, f"centre{q}"))
                        s_.activation(ysq[q][:], y_of(2 * i + q), ACT.Square).then_inc(post_act, 1)
                if kind == "gate":
                    for q in range(2):
                        act.wait_ge(post_dve, after(POST_DVE, i, f"recip{q}"))
                        s_.activation(yrs[q][:], yrec[q][:], ACT.Sqrt).then_inc(post_act, 1)
                    for q in range(2):
                        act.wait_ge(post_dve, after(POST_DVE, i, f"out{q}"))
                        s_.activation(orw_hi[:, 2 * i + q, :], yo[q][:], ACT.Copy).then_inc(post_act, 1)
                if kind == "unit":
                    u = U_MIX + i
                    what, j = MERGE[i]
                    act.wait_ge(w_used, u + 1)
                    if what == "branch":
                        hi_unit(act, u + 2)
                        act.wait_ge(mrg_dve, 4 * j + 3)
                        s_.activation(mg_hi[:, j, :], mrg_t[0][:], ACT.Copy).then_inc(mrg_hi, 1)
                    else:
                        n = gate_no(i)
                        if j >= AHEAD:
                            act.wait_ge(mrg_dve, 4 * (j - AHEAD) + 2)
                        s_.activation(sig_t[n % (2 * AHEAD)][:], bank(n % 2), ACT.Sigmoid).then_inc(gate_out, 1)
                        hi_unit(act, u + 2)

            for k in range(KT):
                hi_unit(act, U_OUT + k + 2)

            def tail_squares(n):
                for b in range(QB):
                    s_.activation(ztok[b][:], psum[:, 2 * b:2 * b + 2, :], ACT.Square,
                                  accum_out=small[:, b:b + 1]).then_inc(tail_sq, 1)

            act.wait_ge(w_used, U_FFN)
            tail_squares(0)
            for b in range(QB):
                act.wait_ge(tail_dve, TAIL_1.index(f"rec{b}") + 1)
                s_.activation(small[:, 24 + b:25 + b], small[:, 16 + b:17 + b], ACT.Sqrt).then_inc(tail_rs, 1)
            for b in range(QB):
                act.wait_ge(tail_dve, TAIL_1.index(f"res{b}") + 1)
                s_.activation(ztok[b][:], resid[:, b, :], ACT.Square,
                              accum_out=small[:, b:b + 1]).then_inc(tail_sq, 1)
            for b in range(QB):
                act.wait_ge(tail_dve, TAIL_1.index(f"rec_f{b}") + 1)
                s_.activation(small[:, 24 + b:25 + b], small[:, 16 + b:17 + b], ACT.Sqrt).then_inc(tail_rs, 1)
            for b in range(QB):
                norm_hi(10 + 2 * b, P, P * b)

            with act.Fori(0, N_FFN_LOOP) as i:
                for s in range(RAW):
                    u0 = U_FFN + s
                    act.wait_ge(w_used, i * RAW + (u0 + 1))
                    if s % 2 == 0:
                        t = s // 2
                        act.wait_ge(tail_dve, i * (2 * len(TAIL_FFN)) + (FFN_AT + (t - 2) * len(TAIL_FFN) + 1))
                        s_.activation(ffn_t[t][:], bank(2 * t), ACT.Sigmoid).then_inc(f_sig, 1)
                    v = u0 + 2
                    act.wait_ge(w_in_raw[v % RAW], i * 16 + landed(v))
                    s_.activation(w_hi[v % SPL][:], raw[v % RAW][:], ACT.Copy).then_inc(w_hi_done, 1)
            for k in range(2, FT):
                hi_unit(act, U_DOWN + k)
            act.wait_ge(w_used, N_UNITS)
            tail_squares(1)
            for b in range(QB):
                act.wait_ge(tail_dve, LAST_AT + TAIL_2.index(f"rec{b}") + 1)
                s_.activation(small[:, 24 + b:25 + b], small[:, 16 + b:17 + b], ACT.Sqrt).then_inc(tail_rs, 1)

        @block.vector
        def _(dve):
            v_ = nc.vector

            def norm_lo(n, width, c0):
                for h in range(2):
                    dve.wait_ge(n_hi, n + h + 1)
                    v_.tensor_sub(h_lo[:, 4 * h:4 * h + 4, c0:c0 + width], quads((n + h) % 4, width),
                                  h_hi[:, 4 * h:4 * h + 4, c0:c0 + width].bitcast(F32)).then_inc(n_lo, 1)

            v_.memset(small[:, 0:5], 1.0).then_inc(n_dve, 1)
            dve.wait_ge(n_sq, 5)
            v_.tensor_scalar(small[:, 8:13], small[:, 0:5], 1.0 / D, RMS_EPS, ALU.mult, ALU.add).then_inc(n_dve, 1)
            dve.wait_ge(n_dve, 2)
            v_.reciprocal(small[:, 16:21], small[:, 8:13]).then_inc(n_dve, 1)
            dve.wait_ge(n_rs, 1)
            for b in (4, 0, 1, 2, 3):
                n = META if b == 4 else P
                if b == 4:
                    dve.wait_ge(x_in[4], 32)
                v_.scalar_tensor_tensor(xn[b][0:n, :], xb[b][0:n, :], small[0:n, 24 + b:25 + b],
                                        g_row[0:n, :], ALU.mult, ALU.mult).then_inc(n_x, 1)
            lo_unit(dve, 0)
            for i, b in enumerate((4, 0, 1, 2, 3)):
                c0, width = norm_cols(b)
                norm_lo(2 * i, width, c0)
            lo_unit(dve, 1)
            dve.wait_ge(vec_ok, 1)
            v_.tensor_scalar(vcol[:, NVEC:NVEC + PAIRS], vcol[:, V_KA:V_KA + PAIRS], -1.0, 1.0,
                             ALU.mult, ALU.add).then_inc(vec_ok, 1)
            dve.wait_ge(vec_ok, 2)
            dve.wait_ge(edge, 9)

            n_shift = 0
            for u, (kind, f, p) in enumerate(ORDER):
                if kind in ("xwa", "xg", "r", "k", "v"):
                    st = stage[n_shift % 3]
                    dst = {"xwa": twx[:], "xg": sg[:], "r": rp[p % 2][:], "k": kp[p % 2][:],
                           "v": vv[:, p, PAD:TP]}[kind]
                    dve.wait_ge(in_out, u + 1)
                    if n_shift:
                        dve.wait_ge(shifted, n_shift)
                    v_.tensor_sub(diff[:], st[:, 0:T], st[:, 1:T + 1]).then_inc(sh_diff, 1)
                    dve.wait_ge(sh_diff, n_shift + 1)
                    if kind in ("r", "k") and p >= 2:
                        dve.wait_ge(prep_pool, after(PREP_POOL, p - 2, "rks"))
                    mu = V_MU + f - RR
                    v_.scalar_tensor_tensor(dst, diff[:], vcol[:, mu:mu + 1], st[:, 1:T + 1],
                                            ALU.mult, ALU.add).then_inc(shifted, 1)
                    n_shift += 1
                lo_unit(dve, u + 2)
                q, step = divmod(u - 9, 4)
                if q in range(PAIRS) and step == 0:
                    dve.wait_ge(prep_pe, after(PREP_PE, q, "bonus"))
                    m = HALF - META
                    v_.tensor_mul(bonus[:, q, 0:m], psum[:, 6, META:HALF], vv[:, q, C:C + m])
                    v_.tensor_mul(bonus[:, q, m:SEQ], psum[:, 7, 0:HALF], vv[:, q, C + m:TP]).then_inc(prep_dve, 1)
                q, step = divmod(u - 5, 4)
                if q in range(PAIRS) and step == 0:
                    dve.wait_ge(prep_act, after(PREP_ACT, q, "sig"))
                    if q:
                        dve.wait_ge(prep_act, after(PREP_ACT, q - 1, "exc"))
                    v_.tensor_tensor_scan(csum[:], reset, sig_w[:], 0.0, ALU.mult, ALU.add).then_inc(prep_dve, 1)
                    dve.wait_ge(prep_dve, after(PREP_DVE, q, "csum"))
                    v_.tensor_sub(csum_x[:], csum[:], sig_w[:]).then_inc(prep_dve, 1)
                if q in range(PAIRS) and step == 1:
                    dve.wait_ge(prep_pe, after(PREP_PE, q, "norm"))
                    v_.tensor_scalar(halves(ksq[:]), both(4), 1e-24, None, ALU.max).then_inc(prep_dve, 1)
                    dve.wait_ge(prep_dve, after(PREP_DVE, q, "max"))
                    v_.reciprocal(rnorm[:], ksq[:]).then_inc(prep_dve, 1)
                    v_.tensor_scalar(kkn[:], kp[q % 2][:], vcol[:, V_KK + q:V_KK + q + 1], None,
                                     ALU.mult).then_inc(prep_dve, 1)
                if q in range(PAIRS) and step == 2:
                    dve.wait_ge(prep_dve, after(PREP_DVE, q, "kk"))
                    dve.wait_ge(prep_act, after(PREP_ACT, q, "rnorm"))
                    v_.tensor_mul(kkn[:], kkn[:], rnorm[:]).then_inc(prep_dve, 1)
                    dve.wait_ge(prep_dve, after(PREP_DVE, q, "kkn"))
                    v_.tensor_mul(ar[:, 0, q, PAD:TP], kkn[:], p_exc[:]).then_inc(prep_dve, 1)
                    v_.scalar_tensor_tensor(bneg[:], kkn[:], -1.0, a_gate[:], ALU.mult, ALU.mult).then_inc(prep_dve, 1)
                    dve.wait_ge(prep_dve, after(PREP_DVE, q, "bneg"))
                    v_.tensor_mul(bt[:, q, PAD:TP], bneg[:], p_inv[:]).then_inc(prep_dve, 1)
                    if q:
                        dve.wait_ge(prep_pool, after(PREP_POOL, q - 1, "rks"))
                    v_.tensor_scalar(kmod[:], a_gate[:], vcol[:, V_KA + q:V_KA + q + 1],
                                     vcol[:, NVEC + q:NVEC + q + 1], ALU.mult, ALU.add).then_inc(prep_dve, 1)

            dve.wait_ge(mix_zero, 11)

            def pairs_of(ap):
                return ap.unsqueeze(1).to_broadcast([P, PAIRS, ap.shape[1]])

            def twice(ap):
                return ap.unsqueeze(2).to_broadcast([P, PAIRS, 2, C])

            def bd4(ap):
                return ap.rearrange("p q (h n) -> p q h n", h=2)

            def mask4(ap):
                return ap.rearrange("p (h n) -> p h n", h=2).unsqueeze(1).to_broadcast([P, PAIRS, 2, C])

            for kind, n, s in mixing:
                if kind == "scan":
                    c = n
                    if s == "A":
                        dve.wait_ge(scan_pe, after(SCAN_PE, c, "A0"))
                        ab, rb = quads(B0, P)[:, :, 0:C], quads(B0, P)[:, :, C:P]
                        v_.tensor_tensor(bd4(aab_bd), twice(ab), mask4(bd_strict), ALU.mult).then_inc(scan_dve, 1)
                        dve.wait_ge(scan_pool, after(SCAN_POOL, c, "ixtb"))
                        v_.copy_predicated(xt_st[:], pairs_of(bytes_[:, B_XT:B_XT + C]), ab).then_inc(scan_dve, 1)
                        v_.copy_predicated(bd4(xt_bd), mask4(bytes_[:, B_BD:B_BD + P]), twice(ab)).then_inc(scan_dve, 1)
                        v_.tensor_tensor(arb[:], rb, pairs_of(st_le), ALU.mult).then_inc(scan_dve, 1)
                        dve.wait_ge(scan_pe, after(SCAN_PE, c, "A1"))
                        ak, rk = quads(B1, P)[:, :, 0:C], quads(B1, P)[:, :, C:P]
                        v_.tensor_tensor(bd4(aak_bd), twice(ak), mask4(bd_strict), ALU.mult).then_inc(scan_dve, 1)
                        v_.tensor_tensor(ark[:], rk, pairs_of(st_le), ALU.mult).then_inc(scan_dve, 1)
                        dve.wait_ge(scan_pe, after(SCAN_PE, c, "A2"))
                        v_.copy_predicated(x_st[:], pairs_of(bytes_[:, B_X:B_X + C]), quads(B2, C)).then_inc(scan_dve, 1)
                    if s[0] == "X":
                        j = int(s[1])
                        if j < LEVELS - 1:
                            dve.wait_ge(scan_pe, after(SCAN_PE, c, f"X{j}"))
                            m = B_X + j * C
                            v_.copy_predicated(x_st[:], pairs_of(bytes_[:, m:m + C]), quads(B1, C)).then_inc(scan_dve, 1)
                        dve.wait_ge(scan_pe, after(SCAN_PE, c, f"Y{j}"))
                        if j < LEVELS - 1:
                            m = B_XT + j * C
                            v_.copy_predicated(xt_st[:], pairs_of(bytes_[:, m:m + C]), quads(B2, C)).then_inc(scan_dve, 1)
                        m = B_BD + j * P
                        v_.copy_predicated(bd4(xt_bd), mask4(bytes_[:, m:m + P]), twice(quads(B2, C))).then_inc(scan_dve, 1)
                    if s == "S":
                        dve.wait_ge(scan_pe, after(SCAN_PE, c, "S"))
                        pcb = pc[:, :, c:c + 1].to_broadcast([P, PAIRS, C])
                        v_.tensor_tensor(z_st[:], s_st[:], pcb, ALU.mult).then_inc(scan_dve, 1)
                        dve.wait_ge(scan_dve, after(SCAN_DVE, c, "decay"))
                        v_.tensor_tensor(s_st[:], quads(B0, C), z_st[:], ALU.add).then_inc(scan_dve, 1)
                else:
                    h = n
                    if s == "P":
                        dve.wait_ge(att_act, after(ATT_ACT, h, "z4"))
                        dve.wait_ge(att_pool, after(ATT_POOL, h, "m3"))
                        v_.tensor_scalar(sp_[:], zs[:], BIG_Z, None, ALU.min).then_inc(att_dve, 1)
                        dve.wait_ge(att_act, after(ATT_ACT, h, "ln"))
                        v_.tensor_tensor(sp_[:], sp_[:], zs[:], ALU.max).then_inc(att_dve, 1)
                    if s[0] == "C":
                        j = int(s[1])
                        rows = META if j == 4 else P
                        dve.wait_ge(att_pe, after(ATT_PE, h, s))
                        d = zs[0:rows, OFF[j]:OFF[j] + WIDTH[j]]
                        v_.tensor_tensor(d, d, psum[0:rows, CBANK, SEQ - WIDTH[j]:SEQ],
                                         ALU.subtract).then_inc(att_dve, 1)

            for kind, i in LATE:
                if kind == "osb":
                    dve.wait_ge(osb_h, 1)
                    v_.tensor_sub(osb_lo[:], qT[:], osb_hi[:].bitcast(F32)).then_inc(osb_l, 1)
                if kind == "mean":
                    for q in range(2):
                        dve.wait_ge(post_pe, after(POST_PE, i, f"mean{q}"))
                        y = y_of(2 * i + q)
                        v_.scalar_tensor_tensor(y, bank(4 + q), -1.0 / HD, y, ALU.mult, ALU.add).then_inc(post_dve, 1)
                if kind == "var":
                    for q in range(2):
                        dve.wait_ge(post_pe, after(POST_PE, i, f"var{q}"))
                        if i:
                            dve.wait_ge(post_act, after(POST_ACT, i - 1, f"sqrt{q}"))
                        v_.tensor_scalar(yvar[q][:], bank(6 + q), 1.0 / HD, GN_EPS, ALU.mult, ALU.add).then_inc(post_dve, 1)
                        dve.wait_ge(post_dve, after(POST_DVE, i, f"var{q}"))
                        v_.reciprocal(yrec[q][:], yvar[q][:]).then_inc(post_dve, 1)
                if kind == "gate":
                    for q in range(2):
                        p = 2 * i + q
                        y = y_of(p)
                        dve.wait_ge(post_act, after(POST_ACT, i, f"sqrt{q}"))
                        v_.tensor_mul(y, y, yrs[q][:]).then_inc(post_dve, 1)
                        dve.wait_ge(post_dve, after(POST_DVE, i, f"norm{q}"))
                        v_.tensor_scalar(y, y, vcol[:, V_LG + p:V_LG + p + 1], vcol[:, V_LB + p:V_LB + p + 1],
                                         ALU.mult, ALU.add).then_inc(post_dve, 1)
                        dve.wait_ge(post_dve, after(POST_DVE, i, f"gain{q}"))
                        v_.tensor_add(y, y, bonus[:, p, :]).then_inc(post_dve, 1)
                        dve.wait_ge(post_dve, after(POST_DVE, i, f"bonus{q}"))
                        dve.wait_ge(post_pe, after(POST_PE, i, f"gate{q}"))
                        v_.tensor_mul(yo[q][:], bank(4 + q), y).then_inc(post_dve, 1)
                        dve.wait_ge(post_act, after(POST_ACT, i, f"hi{q}"))
                        v_.tensor_sub(orw_lo[:, p, :], yo[q][:], orw_hi[:, p, :].bitcast(F32)).then_inc(post_dve, 1)
                if kind == "unit":
                    u = U_MIX + i
                    what, j = MERGE[i]
                    lo_unit(dve, u + 2)
                    if what == "branch":
                        n = 2 * j
                        dve.wait_ge(w_used, u + 1)
                        dve.wait_ge(gate_out, n + 2)
                        if j:
                            dve.wait_ge(mrg_dve, 4 * j)
                        v_.tensor_mul(mrg_t[0][:], bank(2), sig_t[n % (2 * AHEAD)][:]).then_inc(mrg_dve, 1)
                        v_.tensor_mul(mrg_t[1][:], bank(3), sig_t[(n + 1) % (2 * AHEAD)][:]).then_inc(mrg_dve, 1)
                        dve.wait_ge(mrg_dve, 4 * j + 2)
                        v_.tensor_add(mrg_t[0][:], mrg_t[0][:], mrg_t[1][:]).then_inc(mrg_dve, 1)
                        dve.wait_ge(mrg_hi, j + 1)
                        v_.tensor_sub(mg_lo[:, j, :], mrg_t[0][:], mg_hi[:, j, :].bitcast(F32)).then_inc(mrg_dve, 1)

            for k in range(KT):
                lo_unit(dve, U_OUT + k + 2)

            def mean_square(at, steps, b, name, squares):
                dve.wait_ge(tail_sq, squares)
                v_.tensor_scalar(small[:, 8 + b:9 + b], small[:, b:b + 1], 1.0 / D, RMS_EPS,
                                 ALU.mult, ALU.add).then_inc(tail_dve, 1)
                dve.wait_ge(tail_dve, at + steps.index(f"ms{name}{b}") + 1)
                v_.reciprocal(small[:, 16 + b:17 + b], small[:, 8 + b:9 + b]).then_inc(tail_dve, 1)

            def add_normed(at, steps, b, row, roots):
                dve.wait_ge(tail_rs, roots)
                v_.scalar_tensor_tensor(ztok[b][:].rearrange("p (a n) -> p a n", a=2), psum[:, 2 * b:2 * b + 2, :],
                                        small[:, 24 + b:25 + b], grows[:, row, :].rearrange("p (a n) -> p a n", a=2),
                                        ALU.mult, ALU.mult).then_inc(tail_dve, 1)
                dve.wait_ge(tail_dve, at + steps.index(f"z{b}") + 1)
                v_.tensor_add(resid[:, b, :], resid[:, b, :], ztok[b][:]).then_inc(tail_dve, 1)

            for b in range(QB):
                mean_square(0, TAIL_1, b, "", b + 1)
            dve.wait_ge(rows_in, 48)
            dve.wait_ge(resid_in, 16)
            for b in range(QB):
                add_normed(0, TAIL_1, b, 0, b + 1)
            for b in range(QB):
                mean_square(0, TAIL_1, b, "_f", QB + b + 1)
            for b in range(QB):
                dve.wait_ge(tail_rs, QB + b + 1)
                v_.scalar_tensor_tensor(ztok[b][:], resid[:, b, :], small[:, 24 + b:25 + b],
                                        grows[:, 1, :], ALU.mult, ALU.mult).then_inc(tail_dve, 1)
            for b in range(QB):
                norm_lo(10 + 2 * b, P, P * b)

            with dve.Fori(0, N_FFN_LOOP) as i:
                per = 2 * len(TAIL_FFN)
                for s in range(RAW):
                    u0 = U_FFN + s
                    v = u0 + 2
                    dve.wait_ge(w_hi_done, i * RAW + (v + 1))
                    v_.tensor_sub(w_lo[v % SPL][:], raw[v % RAW][:], w_hi[v % SPL][:].bitcast(F32)).then_inc(w_split, 1)
                    if s % 2 == 1:
                        t = s // 2
                        at = FFN_AT + t * len(TAIL_FFN)
                        dve.wait_ge(f_sig, i * 2 + (t + 1))
                        v_.tensor_mul(ffn_t[t][:], bank(2 * t), ffn_t[t][:]).then_inc(tail_dve, 1)
                        dve.wait_ge(tail_dve, i * per + (at + 1))
                        v_.tensor_mul(ffn_u[t][:], bank(2 * t + 1), ffn_t[t][:]).then_inc(tail_dve, 1)
                        dve.wait_ge(tail_dve, i * per + (at + 2))
                        tile = i * 2 + t
                        v_.tensor_scalar(act_hi[:, bass.ds(tile, 1), :], ffn_u[t][:].unsqueeze(1), 1.0, None,
                                         ALU.mult).then_inc(tail_dve, 1)
                        dve.wait_ge(tail_dve, i * per + (at + 3))
                        v_.tensor_tensor(act_lo[:, bass.ds(tile, 1), :], ffn_u[t][:].unsqueeze(1),
                                         act_hi[:, bass.ds(tile, 1), :].bitcast(F32),
                                         ALU.subtract).then_inc(tail_dve, 1)
            for k in range(2, FT):
                lo_unit(dve, U_DOWN + k)
            for b in range(QB):
                mean_square(LAST_AT, TAIL_2, b, "", 2 * QB + b + 1)
            for b in range(QB):
                add_normed(LAST_AT, TAIL_2, b, 2, 2 * QB + b + 1)

        @block.tensor
        def _(pe):
            t_ = nc.tensor

            def norm_transpose(n, src, width):
                for h in range(2):
                    if n + h >= 4:
                        pe.wait_ge(n_lo, n + h - 3)
                    for k in range(4):
                        f = (4 * h + k) * P
                        mm = t_.transpose(quads((n + h) % 4, width)[:, k, :], src[0:width, f:f + P],
                                          ident[0:width, 0:width])
                    mm.then_inc(n_tp, 1)

            pe.wait_ge(const_in, 16 * 6)
            t_.transpose(psum[:, 7, 0:NVEC], vrow[:], ident[0:NVEC, 0:NVEC]).then_inc(vec_tp, 1)
            for i, b in enumerate((4, 0, 1, 2, 3)):
                pe.wait_ge(n_x, i + 1)
                norm_transpose(2 * i, xn[b][:, :], META if b == 4 else P)
            pe.wait_ge(n_lo, 10)
            pe.wait_ge(vec_ok, 2)

            for u, (kind, f, p) in enumerate(ORDER):
                pe.wait_ge(w_split, u + 1)
                if u >= 2:
                    pe.wait_ge(in_out, u - 1)
                b = 2 * (u % 2)
                if kind == "sq":
                    outs = [(bank(b), (META, T))]
                else:
                    outs = [(bank(b, HALF), (0, HALF)), (bank(b + 1, HALF), (HALF, T))]
                products(u, 0, outs, h_hi, h_lo, range(KT)).then_inc(w_used, 1)

                q, step = divmod(u - 5, 4)
                hv = ((0, HALF), (HALF, T))
                if q in range(PAIRS) and step == 0:
                    f0 = q * P
                    pe.wait_ge(lora_act, 1)
                    if q:
                        pe.wait_ge(prep_dve, after(PREP_DVE, q - 1, "max"))
                    for i, (c0, c1) in enumerate(hv):
                        mm = t_.matmul(bank(4 + i, HALF), lora[0:64, f0:f0 + P], twx[0:64, c0:c1], start=True, stop=True)
                    mm.then_inc(prep_pe, 1)
                    if q:
                        pe.wait_ge(prep_dve, after(PREP_DVE, q - 1, "bonus"))
                    pe.wait_ge(shifted, 1)
                    for i, (c0, c1) in enumerate(hv):
                        mm = t_.matmul(bank(6 + i, HALF), lora[64:P, f0:f0 + P], twx[64:P, c0:c1], start=True, stop=True)
                    mm.then_inc(prep_pe, 1)
                if q in range(PAIRS) and step == 1:
                    pe.wait_ge(prep_act, after(PREP_ACT, q, "ksq"))
                    for i, (c0, c1) in enumerate(hv):
                        mm = t_.matmul(bank(4 + i, HALF), blk, ksq[:, c0:c1], start=True, stop=True)
                    mm.then_inc(prep_pe, 1)
                if q in range(PAIRS) and step == 3:
                    pe.wait_ge(prep_pool, after(PREP_POOL, q, "rks"))
                    for i, (c0, c1) in enumerate(hv):
                        mm = t_.matmul(bank(6 + i, HALF), blk, rkp[:, c0:c1], start=True, stop=True)
                    mm.then_inc(prep_pe, 1)
                if 19 <= u < 23:
                    o = u - 19
                    pe.wait_ge(in_out, u)
                    if o == 0:
                        pe.wait_ge(prep_dve, after(PREP_DVE, PAIRS - 1, "max"))
                    else:
                        pe.wait_ge(v_out, 2 * o)
                    for b4 in range(QB):
                        t_.transpose(quads(4, P)[:, b4, :], vst[o % 2][:, META + P * b4:META + P * b4 + P], ident)
                    t_.transpose(psum[0:META, 5, 0:P], vst[o % 2][:, 0:META], ident).then_inc(v_tp, 1)

            pe.wait_ge(in_out, N_IN)
            pe.wait_ge(v_out, 2 * PAIRS)
            pe.wait_ge(prep_dve, PAIRS * len(PREP_DVE))
            pe.wait_ge(mix_zero, 11)

            def pairs(outs, terms):
                for p in range(PAIRS):
                    for i, (w, m) in enumerate(terms):
                        mm = t_.matmul(outs[:, p, :], w(p), m(p), start=(i == 0), stop=(i == len(terms) - 1))
                return mm

            def whole(t):
                return lambda p: t[:, p, :]

            for kind, n, s in mixing:
                if kind == "scan":
                    c = n
                    at_c = lambda t: lambda p: t[:, p, cols(c)]
                    if s == "A":
                        pe.wait_ge(scan_pool, after(SCAN_POOL, c, "k1"))
                        if c:
                            pe.wait_ge(scan_dve, after(SCAN_DVE, c - 1, "s"))
                            pe.wait_ge(scan_act, after(SCAN_ACT, c - 1, "out"))
                        a_and_r = lambda p: ar[:, :, p, cols(c)]
                        pairs(quads(B0, P), [(whole(b_bd), a_and_r)]).then_inc(scan_pe, 1)
                        pairs(quads(B1, P), [(whole(k_bd), a_and_r)]).then_inc(scan_pe, 1)
                        pe.wait_ge(scan_pool, after(SCAN_POOL, c, "a1"))
                        pairs(quads(B2, C), [(whole(a_bd), at_c(bt))]).then_inc(scan_pe, 1)
                    if s == "T":
                        pe.wait_ge(scan_pool, after(SCAN_POOL, c, "bh"))
                        for src, bnk, last in ((bt, B0, "arb"), (kt, B1, "ark"), (vv, B2, "x0")):
                            pe.wait_ge(scan_dve, after(SCAN_DVE, c, last))
                            for p in range(PAIRS):
                                mm = t_.transpose(quads(bnk, P)[0:C, p, :], src[:, p, cols(c)], ident)
                            mm.then_inc(scan_pe, 1)
                    if s[0] == "W":
                        j = int(s[1])
                        if j == 1:
                            pe.wait_ge(scan_act, after(SCAN_ACT, c, "bh1"))
                            pe.wait_ge(scan_dve, after(SCAN_DVE, c, "x0"))
                        else:
                            pe.wait_ge(scan_dve, after(SCAN_DVE, c, f"x{j - 1}"))
                        pairs(quads(B0, C), [(whole(aab_bd), whole(x_st))]).then_inc(scan_pe, 1)
                    if s[0] == "X":
                        j = int(s[1])
                        prev = after(SCAN_DVE, c, "x0" if j == 1 else f"xtb{j - 1}")
                        if j < LEVELS - 1:
                            pe.wait_ge(scan_act, after(SCAN_ACT, c, f"w{j}"))
                            pe.wait_ge(scan_dve, prev)
                            pairs(quads(B1, C), [(whole(xt_bd), whole(w_st))]).then_inc(scan_pe, 1)
                        pe.wait_ge(scan_act, after(SCAN_ACT, c, f"wb1_{j}"))
                        pe.wait_ge(scan_dve, prev)
                        pairs(quads(B2, C), [(whole(w_bd), whole(xt_st))]).then_inc(scan_pe, 1)
                    if s == "Z":
                        pe.wait_ge(scan_act, after(SCAN_ACT, c, f"wb1_{LEVELS - 1}"))
                        pairs(quads(B0, C), [(whole(a_bd), whole(s_st)), (whole(aak_bd), whole(v_st))]).then_inc(scan_pe, 1)
                    if s == "SA":
                        pe.wait_ge(scan_act, after(SCAN_ACT, c, "z"))
                        pe.wait_ge(scan_dve, after(SCAN_DVE, c, f"xtb{LEVELS - 1}"))
                        pairs(quads(B1, C), [(whole(xt_bd), whole(z_st))]).then_inc(scan_pe, 1)
                    if s == "OUT":
                        pe.wait_ge(scan_act, after(SCAN_ACT, c, "sab1"))
                        r_c = lambda p: ar[:, 1, p, cols(c)]
                        pairs(quads(B2, C), [(whole(s_bd), r_c), (whole(v_bd), whole(ark)),
                                             (whole(sa_bd), whole(arb))]).then_inc(scan_pe, 1)
                    if s == "S":
                        pairs(quads(B0, C), [(whole(bh_bd), whole(sa_st)), (whole(kh_bd), whole(v_st))]).then_inc(scan_pe, 1)
                else:
                    h = n
                    hp, hr = h // 2, h % 2
                    rows = slice(hr * HD, (hr + 1) * HD)
                    if s[0] == "Q":
                        j = int(s[1])
                        k0, kn = KEYS[j]
                        if j >= 2:
                            pe.wait_ge(att_act, after(ATT_ACT, h, f"z{j - 2}"))
                        elif h:
                            pe.wait_ge(att_act, after(ATT_ACT, h - 1, f"z{4 - j}"))
                        q0 = SEQ - WIDTH[j]
                        t_.matmul(psum[0:kn, QBANK[j % 2], 0:WIDTH[j]], kT[rows, hp, k0:k0 + kn],
                                  qT[rows, hp, q0:SEQ], start=True, stop=True).then_inc(att_pe, 1)
                    if s[0] == "C":
                        j = int(s[1])
                        kn = KEYS[j][1]
                        q0 = SEQ - WIDTH[j]
                        if j == 3:
                            pe.wait_ge(att_dve, after(ATT_DVE, h, "max"))
                        mv = sp_[0:kn, OFF[j]:OFF[j] + WIDTH[j]]
                        t_.matmul(psum[0:kn, CBANK, q0:SEQ], tri[0:kn, 0:kn], mv, start=(j == 3), stop=(j == 4),
                                  skip_group_check=True).then_inc(att_pe, 1)
                        if j != 4:
                            pe.wait_ge(att_dve, after(ATT_DVE, h, f"s{j}"))
                            t_.matmul(psum[:, CBANK, q0:SEQ], ctri, mv, start=False, stop=False,
                                      skip_group_check=True)
                    if s == "O":
                        ps = psum[rows, OBANK, :]
                        pe.wait_ge(att_act, after(ATT_ACT, h, "wm"))
                        vc = slice(h * HD, (h + 1) * HD)
                        t_.matmul(ps, vmeta[:, vc], zs[0:META, OFF[4]:NS], start=True, stop=False)
                        for j in range(QB):
                            mm = t_.matmul(ps[:, SEQ - WIDTH[j]:SEQ], vtok[:, j, vc], zs[:, OFF[j]:OFF[j] + WIDTH[j]],
                                           start=False, stop=(j == QB - 1))
                        mm.then_inc(att_pe, 1)

            for kind, i in LATE:
                if kind == "osb":
                    pe.wait_ge(scan_act, NC_ * len(SCAN_ACT))
                    pe.wait_ge(scan_dve, NC_ * len(SCAN_DVE))
                    pe.wait_ge(att_act, 2 * PAIRS * len(ATT_ACT))
                    pe.wait_ge(att_dve, 2 * PAIRS * len(ATT_DVE))
                if kind == "mean":
                    for q in range(2):
                        if i:
                            pe.wait_ge(post_dve, after(POST_DVE, i - 1, f"out{q}"))
                        t_.matmul(bank(4 + q), blk, y_of(2 * i + q), start=True, stop=True).then_inc(post_pe, 1)
                if kind == "var":
                    for q in range(2):
                        pe.wait_ge(post_act, after(POST_ACT, i, f"sq{q}"))
                        t_.matmul(bank(6 + q), blk, ysq[q][:], start=True, stop=True).then_inc(post_pe, 1)
                if kind == "gate":
                    for q in range(2):
                        pe.wait_ge(post_dve, after(POST_DVE, i, f"centre{q}"))
                        f0 = (2 * i + q) * P
                        t_.matmul(bank(4 + q), gup[:, f0:f0 + P], sg[:, META:T], start=True, stop=True).then_inc(post_pe, 1)
                if kind == "unit":
                    u = U_MIX + i
                    what, j = MERGE[i]
                    pe.wait_ge(w_split, u + 1)
                    if what == "branch":
                        if j == 0:
                            pe.wait_ge(osb_l, 1)
                            pe.wait_ge(post_dve, 2 * len(POST_DVE))
                        else:
                            pe.wait_ge(mrg_dve, 4 * j - 2)
                        products(u, 0, [(bank(2), (0, SEQ))], osb_hi, osb_lo, range(PAIRS))
                        products(u, PAIRS, [(bank(3), (0, SEQ))], orw_hi, orw_lo, range(PAIRS)).then_inc(w_used, 1)
                    else:
                        n = gate_no(i)
                        if n >= 2:
                            pe.wait_ge(gate_out, n - 1)
                        products(u, 0, [(bank(n % 2), (META, T))], h_hi, h_lo, range(KT)).then_inc(w_used, 1)

            def token_major(u0, n, hi, lo):
                for k in range(n):
                    u = u0 + k
                    pe.wait_ge(w_split, u + 1)
                    passes = ((hi, w_hi[u % SPL]), (hi, w_lo[u % SPL]), (lo, w_hi[u % SPL]))
                    for b in range(QB):
                        for i, (xs, w) in enumerate(passes):
                            for h in range(2):
                                mm = t_.matmul(bank(2 * b + h), xs[:, k, P * b:P * b + P], w[:, 512 * h:512 * h + 512],
                                               start=(k == 0 and i == 0), stop=(k == n - 1 and i == 2))
                    mm.then_inc(w_used, 1)

            pe.wait_ge(mrg_dve, 4 * KT)
            pe.wait_ge(gate_out, 2 * KT)
            token_major(U_OUT, KT, mg_hi, mg_lo)

            for b in range(QB):
                pe.wait_ge(tail_dve, TAIL_1.index(f"xn{b}") + 1)
                norm_transpose(10 + 2 * b, ztok[b][:, :], P)
            pe.wait_ge(n_lo, 18)
            with pe.Fori(0, N_FFN_LOOP) as i:
                per = 2 * len(TAIL_FFN)
                for s in range(RAW):
                    u = U_FFN + s
                    t = s // 2
                    pe.wait_ge(w_split, i * RAW + (u + 1))
                    step = 1 + s % 2
                    pe.wait_ge(tail_dve, i * per + (FFN_AT + (t - 2) * len(TAIL_FFN) + step))
                    products(u, 0, [(bank(s), (0, SEQ))], h_hi, h_lo, range(KT)).then_inc(w_used, 1)
            pe.wait_ge(tail_dve, LAST_AT)
            token_major(U_DOWN, FT, act_hi, act_lo)


def tables():
    import numpy as np

    i = np.arange(P)
    row, col = i[:, None], i[None, :]
    f = np.zeros((P, NK), np.float32)
    f[:, K_ID:K_ID + P] = row == col
    f[:, K_TRI:K_TRI + P] = row >= col
    f[:, K_CTRI:K_CTRI + P] = row < col
    head = row // C == col // C
    f[:, K_BLK:K_BLK + P] = head
    f[:, K_BDS:K_BDS + P] = head & (row < col)
    s, t = i[:, None] % C, np.arange(C)[None, :]
    f[:, K_LE:K_LE + C] = s <= t
    f[:, K_ST:K_ST + C] = s == t
    f[:, K_RST:K_RST + T] = (np.arange(T)[None, :] + PAD) % C != 0
    b = np.zeros((P, NB), np.float32)
    for j in range(LEVELS):
        def joins(t, s):
            return (t >> (j + 1) == s >> (j + 1)) & (t >> j & 1 == 1) & (s >> j & 1 == 0)
        b[:, B_X + j * C:B_X + (j + 1) * C] = joins(i[:, None] % C, np.arange(C)[None, :])
        b[:, B_XT + j * C:B_XT + (j + 1) * C] = joins(np.arange(C)[None, :], i[:, None] % C)
        b[:, B_BD + j * P:B_BD + (j + 1) * P] = head & joins(col % C, row % C)
    return f, b


def kernel(**inputs):
    import numpy as np
    import concourse.bacc as bacc
    from concourse.bass_utils import run_bass_kernel_spmd

    a = {k: np.ascontiguousarray(v) for k, v in inputs.items()}
    vecs = np.concatenate([a[k].reshape(-1, P) for k in (
        "rw_shift_mu", "rw_decay_base", "rw_aaa_base", "rw_k_k", "rw_k_a", "rw_r_k", "rw_ln_gain", "rw_ln_bias")])
    kf, kb = tables()
    arrays = {
        "x": a["x"][0], "meta": a["meta_tokens"], "w_in": a["w_in"][0], "w_sb": a["w_branch_sb"][0],
        "w_rw": a["w_branch_rw"][0], "w_out": a["w_out"][0], "w_g": a["w_ffn_gate"][0],
        "w_u": a["w_ffn_up"][0], "w_d": a["w_ffn_down"][0], "decay_up": a["rw_decay_up"][0],
        "aaa_up": a["rw_aaa_up"][0], "gate_up": a["rw_gate_up"][0], "vecs": vecs,
        "g_mix_pre": a["norm_mix_pre"], "g_mix_post": a["norm_mix_post"],
        "g_ffn_pre": a["norm_ffn_pre"], "g_ffn_post": a["norm_ffn_post"], "kf": kf, "kb": kb,
    }
    nc = bacc.Bacc("TRN2", target_bir_lowering=False, num_devices=1)
    args = [nc.dram_tensor(f"in_{n}", v.shape, mybir.dt.from_np(v.dtype), kind="ExternalInput").ap()
            for n, v in arrays.items()]
    out = nc.dram_tensor("out", (SEQ, D), F32, kind="ExternalOutput").ap()
    build(nc, *args, out)
    r = run_bass_kernel_spmd(nc, [{f"in_{n}": np.ascontiguousarray(v) for n, v in arrays.items()}], core_ids=[0])
    return r.results[0]["out"].reshape(1, SEQ, D)
```

```python
from contextlib import ExitStack

import concourse.bass as bass
from concourse import mybir

F32 = mybir.dt.float32
F32R = mybir.dt.float32r
U8 = mybir.dt.uint8
ALU = mybir.AluOpType
ACT = mybir.ActivationFunctionType

P = 128
D = 1024
SEQ = 512
META = 16
T = META + SEQ
HALF = T // 2
KT = D // P
HD = 64
PAIRS = 4
C = 64
PAD = C - META
NC_ = 1 + SEQ // C
TP = NC_ * C
LEVELS = 6
DFF = 2816
FT = DFF // P
QB = SEQ // P
RMS_EPS = 1e-6
GN_EPS = 64e-5
DEC = 0.6065306597126334
BIG_Z = 40.0
N_ZERO = 13
HIDDEN = -1e30

SQ, SK, SV, RR, RK, RV, XWA, XG, GSB, GRW = 0, 4, 8, 12, 16, 20, 24, 25, 26, 34

V_MU, V_DB, V_AB, V_KK, V_KA, V_RK, V_LG, V_LB = 0, 14, 18, 22, 26, 30, 34, 38
NVEC = 42

K_ID, K_TRI, K_CTRI, K_BLK, K_BDS, K_LE, K_ST, K_RST = 0, 128, 256, 384, 512, 640, 704, 768
NK = K_RST + T
B_X, B_XT, B_BD = 0, LEVELS * C, 2 * LEVELS * C
NB = 4 * LEVELS * C

RAW = 4
SPL = 2

ORDER = [("xwa", XWA, 0), ("xg", XG, 0)]
for _p in range(PAIRS):
    ORDER += [("r", RR + _p, _p), ("k", RK + _p, _p), ("v", RV + _p, _p), ("sk", SK + _p, _p)]
ORDER += [("sv", SV + _p, _p) for _p in range(PAIRS)] + [("sq", SQ + _p, _p) for _p in range(PAIRS)]
N_IN = len(ORDER)
AHEAD = 3
MERGE = []
for _j in range(KT + AHEAD):
    if _j >= AHEAD:
        MERGE += [("branch", _j - AHEAD)]
    if _j < KT:
        MERGE += [("gate_sb", _j), ("gate_rw", _j)]
U_MIX = N_IN
U_OUT = U_MIX + 3 * KT
U_FFN = U_OUT + KT
U_DOWN = U_FFN + 2 * FT
N_UNITS = U_DOWN + FT
N_FFN_LOOP = 2 * FT // RAW
assert U_FFN % SPL == 0 and 2 * FT % RAW == 0 and RAW % SPL == 0

PREP_PE = ["decay", "aaa", "norm", "bonus"]
PREP_ACT = ["sig", "aaa", "ksq", "inc", "inv", "exc", "rnorm"]
PREP_DVE = ["csum", "csum_x", "max", "recip", "kk", "kkn", "a", "bneg", "b", "k_a", "kmod", "rk", "bonus"]
PREP_POOL = ["chunk", "r", "k"]
INV_ITEMS = {"B": ([], [], [], ["b0", "b1"]),
             "A": (["A"], [], ["aab", "xt0", "xtb0", "arb"], ["ix", "ixt", "ixtb"]),
             "AT": (["AT"], [], ["x0"], [])}
for _j in range(1, LEVELS):
    INV_ITEMS[f"W{_j}"] = ([f"W{_j}"], [f"w{_j}", f"wb0_{_j}", f"wb1_{_j}"], [], [])
    INV_ITEMS[f"X{_j}"] = ([f"X{_j}", f"Y{_j}"], [], [f"x{_j}", f"xt{_j}", f"xtb{_j}"], [])
INV_ITEMS[f"X{LEVELS - 1}"] = ([f"Y{LEVELS - 1}"], [], [f"xtb{LEVELS - 1}"], [])
SEQ_ITEMS = {"K": ([], [], [], ["k0", "k1", "a0", "a1", "kh", "bh"]),
             "F": (["F", "T0"], ["bh0", "bh1"], ["aak", "ark"], []),
             "T": (["T1", "T2"], ["kh0", "kh1"], ["vs0", "vs1", "vb0", "vb1"], []),
             "Z": (["Z"], ["z"], [], []),
             "SA": (["SA"], ["sa"], ["decay"], ["sab0", "sab1"]),
             "S": (["S", "OUT"], ["out"], ["s"], ["sb0", "sb1"])}
ATT_ITEMS = {**{f"Q{_j}": ([f"Q{_j}"], [f"z{_j}"], [], [f"m{_j}"] if _j < 4 else []) for _j in range(5)},
             "M": ([], [], ["min1", "min0"], []),
             "E1": ([], ["exp1"], [], []), "E0": ([], ["exp0"], [], []),
             "L1": ([], ["ln1"], ["max1"], []), "L0": ([], ["ln0"], ["max0"], []),
             **{f"C{_j}": ([f"C{_j}"], [], [f"s{_j}"], []) for _j in range(5)},
             "V1": ([], ["w1"], [], []), "V0": ([], ["w0", "wm"], [], []),
             "O": (["O"], ["o"], [], [])}
ITEMS = {"inv": INV_ITEMS, "seq": SEQ_ITEMS, "att": ATT_ITEMS}
POST_PE = ["mean0", "mean1", "var0", "var1", "gate0", "gate1"]
POST_ACT = ["sq0", "sq1", "sqrt0", "sqrt1", "hi0", "hi1"]
POST_DVE = ["centre0", "centre1", "var0", "recip0", "var1", "recip1"] + \
           [f"{s}{i}" for i in range(2) for s in ("norm", "gain", "bonus", "out", "lo")]
TAIL_1 = [f"{s}{b}" for b in range(QB) for s in ("ms", "rec")] + \
         [f"{s}{b}" for b in range(QB) for s in ("z", "res")] + \
         [f"{s}{b}" for b in range(QB) for s in ("ms_f", "rec_f")] + [f"xn{b}" for b in range(QB)]
TAIL_FFN = ["silu", "act", "hi", "lo"]
TAIL_2 = [f"{s}{b}" for b in range(QB) for s in ("ms", "rec")] + \
         [f"{s}{b}" for b in range(QB) for s in ("z", "res")]
FFN_AT = len(TAIL_1)
LAST_AT = FFN_AT + FT * len(TAIL_FFN)


def after(steps, n, step):
    return n * len(steps) + steps.index(step) + 1


def mixing_order():
    heads = 2 * PAIRS
    att = [("att", 0, f"Q{j}") for j in range(5)]
    for h in range(heads):
        nxt = [("att", h + 1, f"Q{j}") if h + 1 < heads else None for j in range(5)]
        own = [("att", h, s) for s in ("M", "E1", "E0", "L1", "L0", "C3", "C2", "C1", "C0", "C4", "V1", "V0", "O")]
        att += own[:5] + [i for j in range(5) for i in (nxt[j], own[5 + j]) if i] + own[10:]
    inverse = ["A", "AT"] + [f"{s}{j}" for j in range(1, LEVELS) for s in ("W", "X")]
    half = len(inverse) // 2
    rounds = half * (NC_ - 1) + len(inverse) + 2
    order = [("inv", 0, "B")]
    taken = 0
    for r in range(rounds):
        seq = []
        for c in range(NC_):
            for at, item in ((6, "K"), (8, "F"), (9, "T"), (10, "Z"), (12, "SA"), (13, "S")):
                if r == half * c + at:
                    seq.append(("seq", c, item))
            if c and r == half * c - 2:
                seq.append(("inv", c, "B"))
        lots = [[("inv", c, inverse[r - half * c]) for c in range(e, NC_, 2) if 0 <= r - half * c < len(inverse)]
                for e in range(2)] + [seq]
        for i, lot in enumerate(lots):
            order += lot
            upto = (3 * r + i + 1) * len(att) // (3 * rounds)
            order += att[taken:upto]
            taken = upto
    return order


MIXING = mixing_order()
MIX_PE, MIX_ACT, MIX_DVE, MIX_POOL = (
    [(kind, n, step) for kind, n, item in MIXING for step in ITEMS[kind][item][e]] for e in range(4))


def upto(steps, kind, n, step):
    return steps.index((kind, n, step)) + 1


def build(nc, x, meta, w_in, w_sb, w_rw, w_out, w_g, w_u, w_d, decay_up, aaa_up, gate_up,
          vecs, g_mix_pre, g_mix_post, g_ffn_pre, g_ffn_post, kf, kb, out):
    with ExitStack() as ctx:
        def sem(name):
            return ctx.enter_context(nc.semaphore(name))

        base = (nc.sbuf_base + 31) // 32 * 32
        end = nc.sbuf_usable_end
        cursor = [base]

        def sb(name, shape, dt=F32):
            size = 1
            for n in shape[1:]:
                size *= n
            size *= 1 if dt == U8 else 4
            t = nc.alloc_sbuf_tensor_at(name, shape, dt, offset=cursor[0])
            cursor[0] += (size + 31) // 32 * 32
            assert cursor[0] <= end, (name, cursor[0], end)
            return t

        raw_at = cursor[0]
        raw = [sb(f"w_raw{i}", [P, 1024]) for i in range(RAW)]
        w_hi, w_lo, split_at = [], [], []
        for i in range(SPL):
            split_at.append(cursor[0])
            w_hi.append(sb(f"w_hi{i}", [P, 1024], F32R))
            w_lo.append(sb(f"w_lo{i}", [P, 1024], F32R))
        consts = sb("consts", [P, NK])
        bytes_ = sb("byte_masks", [P, NB], U8)
        vcol = sb("vec_cols", [P, NVEC + 4])
        small = sb("small", [P, 32])
        gup = sb("gate_up_w", [P, 512])
        ident = consts[:, K_ID:K_ID + P]
        tri = consts[:, K_TRI:K_TRI + P]
        ctri = consts[:, K_CTRI:K_CTRI + P]
        blk = consts[:, K_BLK:K_BLK + P]
        bd_strict = consts[:, K_BDS:K_BDS + P]
        st_le = consts[:, K_LE:K_LE + C]
        st_id = consts[:, K_ST:K_ST + C]
        reset = consts[:, K_RST:K_RST + T]

        h_hi = sb("h_hi", [P, KT, T], F32R)
        h_lo = sb("h_lo", [P, KT, T], F32R)
        ffn_at = cursor[0]
        qT = sb("qT", [P, PAIRS, SEQ])
        kv_at = cursor[0]
        kT = sb("kT", [P, PAIRS, T])
        vtok = sb("v_tok", [P, QB, 512])
        vmeta = sb("v_meta", [META, 512])
        ar = sb("a_r", [P, 2, PAIRS, TP])
        bk_at = cursor[0]
        bt = sb("b_t", [P, PAIRS, TP])
        kt = sb("k_t", [P, PAIRS, TP])
        vv = sb("v_t", [P, PAIRS, TP])
        sg = sb("sig_xg", [P, T])
        bonus = sb("bonus", [P, PAIRS, SEQ])
        pc = sb("p_chunk", [P, PAIRS, NC_])
        mix_at = cursor[0]

        xb = [sb(f"x_in{i}", [P, D]) for i in range(5)]
        xn = [sb(f"x_norm{i}", [P, D]) for i in range(5)]
        g_row = sb("g_row", [P, D])
        masks_f = sb("masks_f", [P, NB])
        vrow = sb("vec_rows", [NVEC, P])
        lora = sb("lora", [P, 512])

        cursor[0] = mix_at
        stage = [sb(f"shift_in{i}", [P, T + 1]) for i in range(3)]
        diff = sb("shift_diff", [P, T])
        twx = sb("tanh_xw_xa", [P, T])
        rp = [sb(f"r_pair{i}", [P, T]) for i in range(2)]
        kp = [sb(f"k_pair{i}", [P, T]) for i in range(2)]
        vst = [sb(f"v_stage{i}", [P, T]) for i in range(2)]
        sig_w = sb("sig_w", [P, T])
        csum = sb("csum", [P, T])
        csum_x = sb("csum_x", [P, T])
        p_inc = sb("p_inc", [P, T])
        p_inv = sb("p_inv", [P, T])
        p_exc = sb("p_exc", [P, T])
        a_gate = sb("a_gate", [P, T])
        ksq = sb("k_sq", [P, T])
        rnorm = sb("r_norm", [P, T])
        kkn = sb("kk_n", [P, T])
        bneg = sb("b_neg", [P, T])
        kmod = sb("k_mod", [P, T])
        rkp = sb("rk_prod", [P, T])

        cursor[0] = mix_at
        def bd(name):
            return sb(name, [P, PAIRS, P])

        def st(name):
            return sb(name, [P, PAIRS, C])

        b_bd = bd("b_bd")
        xt_bd = [bd(f"xt_bd{i}") for i in range(3)]
        arb = [st(f"arb{i}") for i in range(3)]
        xt_st = [st(f"xt_st{i}") for i in range(2)]
        w_st = [st(f"w_st{i}") for i in range(2)]
        w_bd = [bd(f"w_bd{i}") for i in range(2)]
        x_st1 = st("x_st1")
        a_bd, k_bd, aak_bd, bh_bd, kh_bd, v_bd, sa_bd, s_bd = (
            bd(n) for n in ("a_bd", "k_bd", "aak_bd", "bh_bd", "kh_bd", "v_bd", "sa_bd", "s_bd"))
        ark = st("ark")
        s_st = st("s_st")
        NS = 1280 + SEQ
        zs0 = sb("scores0", [P, NS])
        sp_ = sb("softplus", [P, NS])
        cursor[0] = raw_at + 2 * 4 * 1024
        aab_bd = [bd(f"aab_bd{i}") for i in range(2)]
        cursor[0] = split_at[1]
        zs = [zs0, sb("scores1", [P, NS])]
        x_st = [st("x_st0"), x_st1]

        cursor[0] = mix_at
        mg_hi = sb("merged_hi", [P, KT, SEQ], F32R)
        mg_lo = sb("merged_lo", [P, KT, SEQ], F32R)
        sig_t = [sb(f"sig_t{i}", [P, SEQ]) for i in range(2 * AHEAD)]
        mrg_t = [sb(f"merge_t{i}", [P, SEQ]) for i in range(2)]
        mix_end = cursor[0]
        cursor[0] = kv_at
        osb_hi = sb("osb_hi", [P, PAIRS, SEQ], F32R)
        osb_lo = sb("osb_lo", [P, PAIRS, SEQ], F32R)
        cursor[0] = bk_at
        orw_hi = sb("orw_hi", [P, PAIRS, SEQ], F32R)
        orw_lo = sb("orw_lo", [P, PAIRS, SEQ], F32R)
        cursor[0] = mix_at
        ysq = [sb(f"y_sq{i}", [P, SEQ]) for i in range(2)]
        yvar = [sb(f"y_var{i}", [P, SEQ]) for i in range(2)]
        yrec = [sb(f"y_rec{i}", [P, SEQ]) for i in range(2)]
        yrs = [sb(f"y_rs{i}", [P, SEQ]) for i in range(2)]
        yo = [sb(f"y_o{i}", [P, SEQ]) for i in range(2)]

        cursor[0] = ffn_at
        resid = sb("resid", [P, QB, D])
        grows = sb("g_rows", [P, 3, D])
        assert cursor[0] <= mix_at, (cursor[0], mix_at)
        act_at = cursor[0]
        act_hi = sb("act_hi", [P, FT, SEQ], F32R)
        act_lo = sb("act_lo", [P, FT, SEQ], F32R)
        ffn_t = [sb(f"ffn_t{i}", [P, SEQ]) for i in range(2)]
        ffn_u = [sb(f"ffn_u{i}", [P, SEQ]) for i in range(2)]
        cursor[0] = act_at
        ztok = [sb(f"z_tok{b}", [P, D]) for b in range(QB)]
        psum = ctx.enter_context(nc.psum_tensor("psum", [P, 8, 512], F32))

        def bank(b, n=512):
            return psum[:, b, 0:n]

        def both(b):
            return psum[:, b:b + 2, 0:HALF]

        def halves(ap):
            return ap.rearrange("p (a b) -> p a b", a=2)

        def quads(b, n):
            return psum[:, b, 0:PAIRS * n].rearrange("p (q n) -> p q n", q=PAIRS)

        const_in = sem("const_in")
        x_in = [sem(f"x_in{i}") for i in range(5)]
        rows_in = sem("rows_in")
        resid_in = sem("resid_in")
        w_in_raw = [sem(f"w_landed{i}") for i in range(RAW)]
        w_hi_done = sem("w_hi_done")
        w_split = sem("w_split")
        w_used = sem("w_used")
        n_sq = sem("norm_sq")
        n_dve = sem("norm_dve")
        n_rs = sem("norm_rs")
        n_x = sem("norm_x")
        n_tp = sem("norm_transposed")
        n_hi = sem("norm_hi")
        n_lo = sem("norm_lo")
        vec_tp = sem("vec_tp")
        vec_ok = sem("vec_ok")
        edge = sem("edge_zero")
        in_out = sem("in_out")
        sh_diff = sem("shift_diff")
        shifted = sem("shifted")
        lora_act = sem("lora_act")
        v_tp = sem("v_tp")
        v_out = sem("v_out")
        prep_pe, prep_act, prep_dve, prep_pool = (sem(f"prep_{e}") for e in ("pe", "act", "dve", "pool"))
        mix_zero = sem("mix_zero")
        mix_pe, mix_act, mix_dve, mix_pool = (sem(f"mix_{e}") for e in ("pe", "act", "dve", "pool"))
        post_pe, post_act, post_dve = (sem(f"post_{e}") for e in ("pe", "act", "dve"))
        osb_h = sem("osb_h")
        osb_l = sem("osb_l")
        gate_out = sem("gate_out")
        mrg_dve = sem("merge_dve")
        mrg_hi = sem("merge_hi")
        tail_sq = sem("tail_sq")
        tail_rs = sem("tail_rs")
        tail_dve = sem("tail_dve")
        f_sig = sem("ffn_sig")
        n_rows = sem("norm_rows_free")
        stored = sem("stored")

        block = ctx.enter_context(nc.Block())

        def tile_of(w, f):
            return w[:, f * P:(f + 1) * P].rearrange("(k p) n -> p k n", p=P)

        def raw3(u, k=KT):
            return raw[u % RAW][:, 0:k * P].rearrange("p (k n) -> p k n", k=k)

        def load_unit(sp, u):
            if u >= RAW:
                sp.wait_ge(w_split, u - RAW + 1)
            if u < U_MIX:
                sp.dma_start(raw3(u), tile_of(w_in, ORDER[u][1])).then_inc(w_in_raw[u % RAW], 16)
            elif u < U_OUT:
                kind, j = MERGE[u - U_MIX]
                if kind == "branch":
                    half = KT // 2
                    sp.dma_start(raw3(u)[:, 0:half], tile_of(w_sb, j)).then_inc(w_in_raw[u % RAW], 16)
                    sp.dma_start(raw3(u)[:, half:KT], tile_of(w_rw, j)).then_inc(w_in_raw[u % RAW], 16)
                else:
                    f = (GSB if kind == "gate_sb" else GRW) + j
                    sp.dma_start(raw3(u), tile_of(w_in, f)).then_inc(w_in_raw[u % RAW], 16)
            elif u < U_FFN:
                k = u - U_OUT
                sp.dma_start(raw[u % RAW][:], w_out[k * P:(k + 1) * P, :]).then_inc(w_in_raw[u % RAW], 16)
            else:
                k = u - U_DOWN
                sp.dma_start(raw[u % RAW][:], w_d[k * P:(k + 1) * P, :]).then_inc(w_in_raw[u % RAW], 16)

        def landed(u):
            n = sum(1 + (U_MIX <= v < U_OUT and MERGE[v - U_MIX][0] == "branch")
                    for v in range(u % RAW, u + 1, RAW))
            return 16 * n

        def hi_unit(act, u):
            act.wait_ge(w_in_raw[u % RAW], landed(u))
            if u >= SPL:
                act.wait_ge(w_used, u - SPL + 1)
            nc.scalar.activation(w_hi[u % SPL][:], raw[u % RAW][:], ACT.Copy).then_inc(w_hi_done, 1)

        def lo_unit(dve, u):
            dve.wait_ge(w_hi_done, u + 1)
            nc.vector.tensor_sub(w_lo[u % SPL][:], raw[u % RAW][:],
                                 w_hi[u % SPL][:].bitcast(F32)).then_inc(w_split, 1)

        def products(u, w0, outs, xh, xl, kts, last=False):
            hi, lo = w_hi[u % SPL], w_lo[u % SPL]
            n = 0
            total = 3 * len(kts)
            for i, k in enumerate(kts):
                for w, xs in ((hi, xh), (hi, xl), (lo, xh)):
                    for o, (c0, c1) in outs:
                        mm = nc.tensor.matmul(o, w[:, (w0 + i) * P:(w0 + i + 1) * P], xs[:, k, c0:c1],
                                              start=(n == 0), stop=(n == total - 1))
                    n += 1
            return mm

        WIDTH = [SEQ - P * j for j in range(QB)] + [SEQ]
        OFF = [sum(WIDTH[:j]) for j in range(QB + 1)]
        KEYS = [(META + P * j, P) for j in range(QB)] + [(0, META)]
        PART = (slice(0, NS // 2), slice(NS // 2, NS))
        I0, I1 = (0, 2), (1, 3)
        S0, S1 = 4, 5
        CBANK, QBANK = 6, 7

        def cols(c):
            return slice(c * C, (c + 1) * C)

        def top(ap, h):
            return ap[h * C:(h + 1) * C, :, h * C:(h + 1) * C]

        @block.sync
        def _(sp):
            sp.dma_start(xb[4][0:META, :], meta).then_inc(x_in[4], 16)
            sp.dma_start(g_row[:], g_mix_pre.to_broadcast([P, D])).then_inc(x_in[4], 16)
            for b in range(QB):
                sp.dma_start(xb[b][:], x[b * P:(b + 1) * P, :]).then_inc(x_in[b], 16)
            for dst, src in ((consts[:], kf), (masks_f[:], kb), (vrow[:], vecs), (lora[0:64, :], decay_up),
                             (lora[64:P, :], aaa_up), (gup[:], gate_up)):
                sp.dma_start(dst, src).then_inc(const_in, 16)
            for u in range(U_FFN):
                if u == U_OUT + RAW:
                    sp.wait_ge(w_used, U_OUT)
                    for i, g in enumerate((g_mix_post, g_ffn_pre, g_ffn_post)):
                        sp.dma_start(grows[:, i, :], g.to_broadcast([P, D])).then_inc(rows_in, 16)
                    sp.dma_start(resid[:], x.rearrange("(b p) d -> p b d", p=P)).then_inc(resid_in, 16)
                if u == U_MIX + RAW:
                    sp.wait_ge(mix_pe, len(MIX_PE))
                load_unit(sp, u)
            with sp.Fori(0, N_FFN_LOOP) as i:
                for s in range(RAW):
                    sp.wait_ge(w_split, i * RAW + (U_FFN + s - RAW + 1))
                    f = i * (RAW // 2) + s // 2
                    w = (w_g, w_u)[s % 2]
                    sl = (U_FFN + s) % RAW
                    sp.dma_start(raw[sl][:, :].rearrange("p (k n) -> p k n", k=KT),
                                 w.rearrange("(k p) n -> p k n", p=P)[:, :, bass.ds(f * P, P)]
                                 ).then_inc(w_in_raw[sl], 16)
            for u in range(U_DOWN, N_UNITS):
                load_unit(sp, u)
            for b in range(QB):
                sp.wait_ge(tail_dve, LAST_AT + TAIL_2.index(f"res{b}") + 1)
                sp.dma_start(out[b * P:(b + 1) * P, :], resid[:, b, :]).then_inc(stored, 16)
            sp.wait_ge(stored, 16 * QB)

        @block.gpsimd
        def _(pool):
            g = nc.gpsimd
            pool.wait_ge(const_in, 16 * 6)
            g.tensor_copy(bytes_[:], masks_f[:]).then_inc(edge, 1)
            for t in stage:
                pool.wait_ge(n_x, 5)
                g.memset(t[:, 0:1], 0.0).then_inc(edge, 1)
            for t in (ar[:, 0], ar[:, 1], bt, kt, vv):
                g.memset(t[:, :, 0:PAD], 0.0).then_inc(edge, 1)
            for p in range(PAIRS):
                pool.wait_ge(prep_act, after(PREP_ACT, p, "inc"))
                g.tensor_copy(pc[:, p, :], p_inc[:, C - 1 - PAD::C]).then_inc(prep_pool, 1)
                g.tensor_tensor(ar[:, 1, p, PAD:TP], rp[p % 2][:], p_inc[:], ALU.mult).then_inc(prep_pool, 1)
                pool.wait_ge(prep_dve, after(PREP_DVE, p, "kmod"))
                pool.wait_ge(prep_act, after(PREP_ACT, p, "inv"))
                g.tensor_tensor(kt[:, p, PAD:TP], kmod[:], p_inv[:], ALU.mult).then_inc(prep_pool, 1)
            pool.wait_ge(prep_pool, PAIRS * len(PREP_POOL))
            pool.wait_ge(prep_dve, after(PREP_DVE, PAIRS - 1, "bonus"))
            pool.wait_ge(prep_act, after(PREP_ACT, PAIRS - 1, "rnorm"))
            pool.wait_ge(prep_pe, after(PREP_PE, PAIRS - 1, "bonus"))
            pool.wait_ge(v_tp, PAIRS)
            for t in (b_bd, k_bd, a_bd, *w_bd, bh_bd, kh_bd, v_bd, sa_bd, s_st, s_bd):
                g.memset(t[:], 0.0).then_inc(mix_zero, 1)
            g.memset(zs[0][:, OFF[4]:NS], 0.0).then_inc(mix_zero, 1)
            pool.wait_ge(w_used, N_IN)
            g.memset(zs[1][:, OFF[4]:NS], 0.0).then_inc(mix_zero, 1)
            pool.wait_ge(mix_zero, N_ZERO)
            steps = 0
            for kind, n, item in MIXING:
                if ITEMS[kind][item][3] and steps:
                    pool.wait_ge(mix_pool, steps)
                steps += len(ITEMS[kind][item][3])
                c = h = n
                e = c % 2
                if (kind, item) == ("inv", "B"):
                    if c:
                        pool.wait_ge(mix_pe, upto(MIX_PE, "inv", c - 1, "A"))
                    for i in range(2):
                        g.tensor_copy(top(b_bd, i), bt[i * C:(i + 1) * C, :, cols(c)]).then_inc(mix_pool, 1)
                if (kind, item) == ("inv", "A"):
                    if c >= 2:
                        pool.wait_ge(mix_pe, upto(MIX_PE, "inv", c - 2, f"Y{LEVELS - 1}"))
                    else:
                        pool.wait_ge(w_used, N_IN)
                    one = st_id.unsqueeze(1).to_broadcast([P, PAIRS, C])
                    g.tensor_copy(x_st[e][:], one).then_inc(mix_pool, 1)
                    g.tensor_copy(xt_st[e][:], one).then_inc(mix_pool, 1)
                    if c >= 3:
                        pool.wait_ge(mix_pe, upto(MIX_PE, "seq", c - 3, "SA"))
                    g.tensor_copy(xt_bd[c % 3][:], ident.unsqueeze(1).to_broadcast([P, PAIRS, P])).then_inc(mix_pool, 1)
                if (kind, item) == ("seq", "K"):
                    pcb = pc[:, :, c:c + 1].to_broadcast([P, PAIRS, C])
                    if c:
                        pool.wait_ge(mix_pe, upto(MIX_PE, "seq", c - 1, "Z"))
                    for src, dst in ((kt, k_bd), (ar[:, 0], a_bd)):
                        for i in range(2):
                            g.tensor_copy(top(dst, i), src[i * C:(i + 1) * C, :, cols(c)]).then_inc(mix_pool, 1)
                    pool.wait_ge(mix_pool, upto(MIX_POOL, "seq", c, "a1"))
                    g.tensor_tensor(kt[:, :, cols(c)], kt[:, :, cols(c)], pcb, ALU.mult).then_inc(mix_pool, 1)
                    g.tensor_tensor(bt[:, :, cols(c)], bt[:, :, cols(c)], pcb, ALU.mult).then_inc(mix_pool, 1)
                if (kind, item) == ("seq", "SA"):
                    pool.wait_ge(mix_act, upto(MIX_ACT, "seq", c, "sa"))
                    for i in range(2):
                        g.tensor_copy(top(sa_bd, i), kt[i * C:(i + 1) * C, :, cols(c)]).then_inc(mix_pool, 1)
                if (kind, item) == ("seq", "S"):
                    pool.wait_ge(mix_dve, upto(MIX_DVE, "seq", c, "s"))
                    pool.wait_ge(mix_pe, upto(MIX_PE, "seq", c, "OUT"))
                    for i in range(2):
                        g.tensor_copy(top(s_bd, i), s_st[i * C:(i + 1) * C]).then_inc(mix_pool, 1)
                if kind == "att" and item[0] == "Q" and item != "Q4":
                    j = int(item[1])
                    pool.wait_ge(mix_act, upto(MIX_ACT, "att", h, f"z{j}"))
                    d = zs[h % 2][:, OFF[j]:OFF[j] + P]
                    g.affine_select(out=d, in_=d, compare_op=ALU.is_gt, fill=HIDDEN, base=0,
                                    pattern=[[1, P]], channel_multiplier=-1).then_inc(mix_pool, 1)

        def late_items():
            gates = [m for m in MERGE if m[0] != "branch"][:2 * AHEAD]
            it = iter(range(2 * AHEAD))
            items = [("osb", 0)]
            for r in range(2):
                items += [("mean", r), ("unit", next(it)), ("var", r), ("unit", next(it)), ("gate", r),
                          ("unit", next(it))]
            return items + [("unit", i) for i in range(2 * AHEAD, len(MERGE))]

        LATE = late_items()

        def gate_no(i):
            kind, j = MERGE[i]
            return 2 * j + (kind == "gate_rw")

        def y_of(p):
            return ar[:, 0, p, C:TP]

        def norm_cols(b):
            return (0, META) if b == 4 else (META + P * b, P)

        @block.scalar
        def _(act):
            s_ = nc.scalar

            def norm_hi(n, width, c0):
                for h in range(2):
                    act.wait_ge(n_tp, n + h + 1)
                    s_.activation(h_hi[:, 4 * h:4 * h + 4, c0:c0 + width], quads((n + h) % 4, width),
                                  ACT.Copy).then_inc(n_hi, 1)

            act.wait_ge(n_dve, 1)
            for b in (4, 0, 1, 2, 3):
                n = META if b == 4 else P
                act.wait_ge(x_in[b], 32 if b == 4 else 16)
                s_.activation(xn[b][0:n, :], xb[b][0:n, :], ACT.Square,
                              accum_out=small[0:n, b:b + 1]).then_inc(n_sq, 1)
            act.wait_ge(vec_tp, 1)
            s_.activation(vcol[:, 0:NVEC], psum[:, 7, 0:NVEC], ACT.Copy).then_inc(vec_ok, 1)
            act.wait_ge(n_dve, 3)
            s_.activation(small[:, 24:29], small[:, 16:21], ACT.Sqrt).then_inc(n_rs, 1)
            hi_unit(act, 0)
            for i, b in enumerate((4, 0, 1, 2, 3)):
                c0, width = norm_cols(b)
                norm_hi(2 * i, width, c0)
            hi_unit(act, 1)

            n_shift = 0
            for u, (kind, f, p) in enumerate(ORDER):
                act.wait_ge(w_used, u + 1)
                if u == 0:
                    act.wait_ge(edge, 9)
                ps = both(2 * (u % 2))
                if kind in ("xwa", "xg", "r", "k", "v"):
                    if n_shift >= 3:
                        act.wait_ge(shifted, n_shift - 2)
                    s_.activation(halves(stage[n_shift % 3][:, 1:T + 1]), ps, ACT.Copy).then_inc(in_out, 1)
                    n_shift += 1
                elif kind == "sk":
                    s_.activation(halves(kT[:, p, :]), ps, ACT.Copy).then_inc(in_out, 1)
                elif kind == "sv":
                    if p >= 2:
                        act.wait_ge(v_tp, p - 1)
                    s_.activation(halves(vst[p % 2][:]), ps, ACT.Copy).then_inc(in_out, 1)
                else:
                    s_.activation(qT[:, p, :], bank(2 * (u % 2)), ACT.Copy, scale=HD ** -0.5).then_inc(in_out, 1)
                if u + 2 != U_MIX + 1:
                    hi_unit(act, u + 2)
                if u == 1:
                    act.wait_ge(shifted, 1)
                    s_.activation(twx[0:64, :], twx[0:64, :], ACT.Tanh).then_inc(lora_act, 1)
                if u == 2:
                    act.wait_ge(shifted, 2)
                    s_.activation(sg[:], sg[:], ACT.Sigmoid).then_inc(lora_act, 1)
                    act.wait_ge(vec_ok, 2)
                q, step = divmod(u - 5, 4)
                if q in range(PAIRS) and step == 0:
                    act.wait_ge(prep_pe, after(PREP_PE, q, "decay"))
                    if q:
                        act.wait_ge(prep_dve, after(PREP_DVE, q - 1, "kmod"))
                    s_.activation(halves(sig_w[:]), both(4), ACT.Sigmoid,
                                  bias=vcol[:, V_DB + q:V_DB + q + 1]).then_inc(prep_act, 1)
                    act.wait_ge(prep_pe, after(PREP_PE, q, "aaa"))
                    s_.activation(halves(a_gate[:]), both(6), ACT.Sigmoid,
                                  bias=vcol[:, V_AB + q:V_AB + q + 1]).then_inc(prep_act, 1)
                    act.wait_ge(shifted, 2 + 3 * q + 2)
                    s_.activation(ksq[:], kp[q % 2][:], ACT.Square,
                                  scale=vcol[:, V_KK + q:V_KK + q + 1]).then_inc(prep_act, 1)
                if q in range(PAIRS) and step == 1:
                    if q:
                        act.wait_ge(prep_pool, after(PREP_POOL, q - 1, "k"))
                    act.wait_ge(prep_dve, after(PREP_DVE, q, "csum"))
                    s_.activation(p_inc[:], csum[:], ACT.Exp, scale=-DEC).then_inc(prep_act, 1)
                    s_.activation(p_inv[:], csum[:], ACT.Exp, scale=DEC).then_inc(prep_act, 1)
                    act.wait_ge(prep_dve, after(PREP_DVE, q, "csum_x"))
                    s_.activation(p_exc[:], csum_x[:], ACT.Exp, scale=-DEC).then_inc(prep_act, 1)
                if q in range(PAIRS) and step == 2:
                    act.wait_ge(prep_dve, after(PREP_DVE, q, "recip"))
                    s_.activation(rnorm[:], rnorm[:], ACT.Sqrt).then_inc(prep_act, 1)
                if 19 <= u < 23:
                    act.wait_ge(v_tp, u - 18)
                    o = u - 19
                    s_.activation(vtok[:, :, P * o:P * o + P], quads(4, P), ACT.Copy).then_inc(v_out, 1)
                    s_.activation(vmeta[:, P * o:P * o + P], psum[0:META, 5, 0:P], ACT.Copy).then_inc(v_out, 1)

            act.wait_ge(mix_zero, N_ZERO)
            for kind, n, s in MIXING:
                c = h = n
                e = c % 2
                if kind == "inv" and s[0] == "W":
                    act.wait_ge(mix_pe, upto(MIX_PE, "inv", c, s))
                    s_.activation(w_st[e][:], quads(I0[e], C), ACT.Copy).then_inc(mix_act, 1)
                    for i in range(2):
                        s_.activation(top(w_bd[e], i), quads(I0[e], C)[i * C:(i + 1) * C],
                                      ACT.Copy).then_inc(mix_act, 1)
                if kind == "seq":
                    for name, it, bnk, dst in (("T0", "F", S1, bh_bd), ("T1", "T", S0, kh_bd)):
                        if s == it:
                            act.wait_ge(mix_pe, upto(MIX_PE, "seq", c, name))
                            for i in range(2):
                                s_.activation(top(dst, i), quads(bnk, P)[0:C, :, i * C:(i + 1) * C],
                                              ACT.Copy).then_inc(mix_act, 1)
                    if s == "Z":
                        act.wait_ge(mix_pe, upto(MIX_PE, "seq", c, "Z"))
                        s_.activation(bt[:, :, cols(c)], quads(S0, C), ACT.Copy).then_inc(mix_act, 1)
                    if s == "SA":
                        act.wait_ge(mix_pe, upto(MIX_PE, "seq", c, "SA"))
                        s_.activation(kt[:, :, cols(c)], quads(S1, C), ACT.Copy).then_inc(mix_act, 1)
                    if s == "S":
                        act.wait_ge(mix_pe, upto(MIX_PE, "seq", c, "OUT"))
                        s_.activation(ar[:, 0, :, cols(c)], quads(S0, C), ACT.Copy).then_inc(mix_act, 1)
                if kind == "att":
                    hp, hr = h // 2, h % 2
                    z_h = zs[h % 2]
                    if s[0] == "Q":
                        j = int(s[1])
                        rows = META if j == 4 else P
                        act.wait_ge(mix_pe, upto(MIX_PE, "att", h, s))
                        s_.activation(z_h[0:rows, OFF[j]:OFF[j] + WIDTH[j]], psum[0:rows, QBANK, 0:WIDTH[j]],
                                      ACT.Copy).then_inc(mix_act, 1)
                    if s[0] == "E":
                        act.wait_ge(mix_dve, upto(MIX_DVE, "att", h, f"min{s[1]}"))
                        part = sp_[:, PART[int(s[1])]]
                        s_.activation(part, part, ACT.Exp).then_inc(mix_act, 1)
                    if s[0] == "L":
                        act.wait_ge(mix_act, upto(MIX_ACT, "att", h, f"exp{s[1]}"))
                        part = sp_[:, PART[int(s[1])]]
                        s_.activation(part, part, ACT.Ln, bias=1.0).then_inc(mix_act, 1)
                    if s == "V1":
                        act.wait_ge(mix_dve, upto(MIX_DVE, "att", h, "s2"))
                        w = z_h[:, OFF[2]:OFF[4]]
                        s_.activation(w, w, ACT.Exp).then_inc(mix_act, 1)
                    if s == "V0":
                        act.wait_ge(mix_dve, upto(MIX_DVE, "att", h, "s0"))
                        w = z_h[:, 0:OFF[2]]
                        s_.activation(w, w, ACT.Exp).then_inc(mix_act, 1)
                        act.wait_ge(mix_dve, upto(MIX_DVE, "att", h, "s4"))
                        w = z_h[0:META, OFF[4]:NS]
                        s_.activation(w, w, ACT.Exp).then_inc(mix_act, 1)
                    if s == "O":
                        act.wait_ge(mix_pe, upto(MIX_PE, "att", h, "O"))
                        s_.activation(qT[hr * HD:(hr + 1) * HD, hp, :], psum[hr * HD:(hr + 1) * HD, QBANK, :],
                                      ACT.Copy).then_inc(mix_act, 1)

            for kind, i in LATE:
                if kind == "osb":
                    act.wait_ge(mix_act, len(MIX_ACT))
                    act.wait_ge(mix_pool, len(MIX_POOL))
                    act.wait_ge(mix_pe, len(MIX_PE))
                    hi_unit(act, U_MIX + 1)
                    s_.activation(osb_hi[:], qT[:], ACT.Copy).then_inc(osb_h, 1)
                if kind == "mean":
                    for q in range(2):
                        act.wait_ge(post_dve, after(POST_DVE, i, f"centre{q}"))
                        s_.activation(ysq[q][:], y_of(2 * i + q), ACT.Square).then_inc(post_act, 1)
                if kind == "gate":
                    for q in range(2):
                        act.wait_ge(post_dve, after(POST_DVE, i, f"recip{q}"))
                        s_.activation(yrs[q][:], yrec[q][:], ACT.Sqrt).then_inc(post_act, 1)
                    for q in range(2):
                        act.wait_ge(post_dve, after(POST_DVE, i, f"out{q}"))
                        s_.activation(orw_hi[:, 2 * i + q, :], yo[q][:], ACT.Copy).then_inc(post_act, 1)
                if kind == "unit":
                    u = U_MIX + i
                    what, j = MERGE[i]
                    act.wait_ge(w_used, u + 1)
                    if what == "branch":
                        hi_unit(act, u + 2)
                        act.wait_ge(mrg_dve, 4 * j + 3)
                        s_.activation(mg_hi[:, j, :], mrg_t[0][:], ACT.Copy).then_inc(mrg_hi, 1)
                    else:
                        n = gate_no(i)
                        if j >= AHEAD:
                            act.wait_ge(mrg_dve, 4 * (j - AHEAD) + 2)
                        s_.activation(sig_t[n % (2 * AHEAD)][:], bank(n % 2), ACT.Sigmoid).then_inc(gate_out, 1)
                        hi_unit(act, u + 2)

            for k in range(KT):
                hi_unit(act, U_OUT + k + 2)

            def tail_squares(n):
                for b in range(QB):
                    s_.activation(ztok[b][:], psum[:, 2 * b:2 * b + 2, :], ACT.Square,
                                  accum_out=small[:, b:b + 1]).then_inc(tail_sq, 1)

            act.wait_ge(w_used, U_FFN)
            tail_squares(0)
            for b in range(QB):
                act.wait_ge(tail_dve, TAIL_1.index(f"rec{b}") + 1)
                s_.activation(small[:, 24 + b:25 + b], small[:, 16 + b:17 + b], ACT.Sqrt).then_inc(tail_rs, 1)
            for b in range(QB):
                act.wait_ge(tail_dve, TAIL_1.index(f"res{b}") + 1)
                s_.activation(ztok[b][:], resid[:, b, :], ACT.Square,
                              accum_out=small[:, b:b + 1]).then_inc(tail_sq, 1)
            for b in range(QB):
                act.wait_ge(tail_dve, TAIL_1.index(f"rec_f{b}") + 1)
                s_.activation(small[:, 24 + b:25 + b], small[:, 16 + b:17 + b], ACT.Sqrt).then_inc(tail_rs, 1)
            for b in range(QB):
                norm_hi(10 + 2 * b, P, P * b)

            with act.Fori(0, N_FFN_LOOP) as i:
                for s in range(RAW):
                    u0 = U_FFN + s
                    act.wait_ge(w_used, i * RAW + (u0 + 1))
                    if s % 2 == 0:
                        t = s // 2
                        act.wait_ge(tail_dve, i * (2 * len(TAIL_FFN)) + (FFN_AT + (t - 2) * len(TAIL_FFN) + 1))
                        s_.activation(ffn_t[t][:], bank(2 * t), ACT.Sigmoid).then_inc(f_sig, 1)
                    v = u0 + 2
                    act.wait_ge(w_in_raw[v % RAW], i * 16 + landed(v))
                    s_.activation(w_hi[v % SPL][:], raw[v % RAW][:], ACT.Copy).then_inc(w_hi_done, 1)
            for k in range(2, FT):
                hi_unit(act, U_DOWN + k)
            act.wait_ge(w_used, N_UNITS)
            tail_squares(1)
            for b in range(QB):
                act.wait_ge(tail_dve, LAST_AT + TAIL_2.index(f"rec{b}") + 1)
                s_.activation(small[:, 24 + b:25 + b], small[:, 16 + b:17 + b], ACT.Sqrt).then_inc(tail_rs, 1)

        @block.vector
        def _(dve):
            v_ = nc.vector

            def norm_lo(n, width, c0):
                for h in range(2):
                    dve.wait_ge(n_hi, n + h + 1)
                    v_.tensor_sub(h_lo[:, 4 * h:4 * h + 4, c0:c0 + width], quads((n + h) % 4, width),
                                  h_hi[:, 4 * h:4 * h + 4, c0:c0 + width].bitcast(F32)).then_inc(n_lo, 1)

            v_.memset(small[:, 0:5], 1.0).then_inc(n_dve, 1)
            dve.wait_ge(n_sq, 5)
            v_.tensor_scalar(small[:, 8:13], small[:, 0:5], 1.0 / D, RMS_EPS, ALU.mult, ALU.add).then_inc(n_dve, 1)
            dve.wait_ge(n_dve, 2)
            v_.reciprocal(small[:, 16:21], small[:, 8:13]).then_inc(n_dve, 1)
            dve.wait_ge(n_rs, 1)
            for b in (4, 0, 1, 2, 3):
                n = META if b == 4 else P
                if b == 4:
                    dve.wait_ge(x_in[4], 32)
                v_.scalar_tensor_tensor(xn[b][0:n, :], xb[b][0:n, :], small[0:n, 24 + b:25 + b],
                                        g_row[0:n, :], ALU.mult, ALU.mult).then_inc(n_x, 1)
            lo_unit(dve, 0)
            for i, b in enumerate((4, 0, 1, 2, 3)):
                c0, width = norm_cols(b)
                norm_lo(2 * i, width, c0)
            lo_unit(dve, 1)
            dve.wait_ge(vec_ok, 1)
            v_.tensor_scalar(vcol[:, NVEC:NVEC + PAIRS], vcol[:, V_KA:V_KA + PAIRS], -1.0, 1.0,
                             ALU.mult, ALU.add).then_inc(vec_ok, 1)
            dve.wait_ge(vec_ok, 2)
            dve.wait_ge(edge, 9)

            n_shift = 0
            for u, (kind, f, p) in enumerate(ORDER):
                if kind in ("xwa", "xg", "r", "k", "v"):
                    st = stage[n_shift % 3]
                    dst = {"xwa": twx[:], "xg": sg[:], "r": rp[p % 2][:], "k": kp[p % 2][:],
                           "v": vv[:, p, PAD:TP]}[kind]
                    dve.wait_ge(in_out, u + 1)
                    if n_shift:
                        dve.wait_ge(shifted, n_shift)
                    v_.tensor_sub(diff[:], st[:, 0:T], st[:, 1:T + 1]).then_inc(sh_diff, 1)
                    dve.wait_ge(sh_diff, n_shift + 1)
                    if kind in ("r", "k") and p >= 2:
                        dve.wait_ge(prep_pool, after(PREP_POOL, p - 2, "r"))
                    mu = V_MU + f - RR
                    v_.scalar_tensor_tensor(dst, diff[:], vcol[:, mu:mu + 1], st[:, 1:T + 1],
                                            ALU.mult, ALU.add).then_inc(shifted, 1)
                    n_shift += 1
                if u + 2 != U_MIX + 1:
                    lo_unit(dve, u + 2)
                q, step = divmod(u - 5, 4)
                if q in range(PAIRS) and step == 0:
                    dve.wait_ge(prep_act, after(PREP_ACT, q, "sig"))
                    if q:
                        dve.wait_ge(prep_act, after(PREP_ACT, q - 1, "exc"))
                    v_.tensor_tensor_scan(csum[:], reset, sig_w[:], 0.0, ALU.mult, ALU.add).then_inc(prep_dve, 1)
                    dve.wait_ge(prep_dve, after(PREP_DVE, q, "csum"))
                    v_.tensor_sub(csum_x[:], csum[:], sig_w[:]).then_inc(prep_dve, 1)
                if q in range(PAIRS) and step == 1:
                    dve.wait_ge(prep_pe, after(PREP_PE, q, "norm"))
                    v_.tensor_scalar(halves(ksq[:]), both(4), 1e-24, None, ALU.max).then_inc(prep_dve, 1)
                    dve.wait_ge(prep_dve, after(PREP_DVE, q, "max"))
                    v_.reciprocal(rnorm[:], ksq[:]).then_inc(prep_dve, 1)
                    v_.tensor_scalar(kkn[:], kp[q % 2][:], vcol[:, V_KK + q:V_KK + q + 1], None,
                                     ALU.mult).then_inc(prep_dve, 1)
                if q in range(PAIRS) and step == 2:
                    dve.wait_ge(prep_dve, after(PREP_DVE, q, "kk"))
                    dve.wait_ge(prep_act, after(PREP_ACT, q, "rnorm"))
                    v_.tensor_mul(kkn[:], kkn[:], rnorm[:]).then_inc(prep_dve, 1)
                    dve.wait_ge(prep_dve, after(PREP_DVE, q, "kkn"))
                    v_.tensor_mul(ar[:, 0, q, PAD:TP], kkn[:], p_exc[:]).then_inc(prep_dve, 1)
                    v_.scalar_tensor_tensor(bneg[:], kkn[:], -1.0, a_gate[:], ALU.mult, ALU.mult).then_inc(prep_dve, 1)
                    dve.wait_ge(prep_dve, after(PREP_DVE, q, "bneg"))
                    v_.tensor_mul(bt[:, q, PAD:TP], bneg[:], p_inv[:]).then_inc(prep_dve, 1)
                    if q:
                        dve.wait_ge(prep_pool, after(PREP_POOL, q - 1, "k"))
                        dve.wait_ge(prep_pe, after(PREP_PE, q - 1, "bonus"))
                    v_.tensor_scalar(kmod[:], a_gate[:], vcol[:, V_KA + q:V_KA + q + 1],
                                     vcol[:, NVEC + q:NVEC + q + 1], ALU.mult, ALU.add).then_inc(prep_dve, 1)
                    dve.wait_ge(prep_dve, after(PREP_DVE, q, "k_a"))
                    v_.tensor_mul(kmod[:], kmod[:], kp[q % 2][:]).then_inc(prep_dve, 1)
                    dve.wait_ge(prep_dve, after(PREP_DVE, q, "kmod"))
                    v_.scalar_tensor_tensor(rkp[:], rp[q % 2][:], vcol[:, V_RK + q:V_RK + q + 1], kmod[:],
                                            ALU.mult, ALU.mult).then_inc(prep_dve, 1)
                if q in range(PAIRS) and step == 3:
                    dve.wait_ge(prep_pe, after(PREP_PE, q, "bonus"))
                    m = HALF - META
                    v_.tensor_mul(bonus[:, q, 0:m], psum[:, 6, META:HALF], vv[:, q, C:C + m])
                    v_.tensor_mul(bonus[:, q, m:SEQ], psum[:, 7, 0:HALF], vv[:, q, C + m:TP]).then_inc(prep_dve, 1)

            dve.wait_ge(mix_zero, N_ZERO)
            dve.wait_ge(w_split, U_MIX + 1)

            def pairs_of(ap):
                return ap.unsqueeze(1).to_broadcast([P, PAIRS, ap.shape[1]])

            def twice(ap):
                return ap.unsqueeze(2).to_broadcast([P, PAIRS, 2, C])

            def bd4(ap):
                return ap.rearrange("p q (h n) -> p q h n", h=2)

            def mask4(ap):
                return ap.rearrange("p (h n) -> p h n", h=2).unsqueeze(1).to_broadcast([P, PAIRS, 2, C])

            for kind, n, s in MIXING:
                c = h = n
                e = c % 2
                x_t = xt_bd[c % 3]
                if kind == "inv" and s == "A":
                    dve.wait_ge(mix_pe, upto(MIX_PE, "inv", c, "A"))
                    ab, rb = quads(I0[e], P)[:, :, 0:C], quads(I0[e], P)[:, :, C:P]
                    v_.tensor_tensor(bd4(aab_bd[e]), twice(ab), mask4(bd_strict), ALU.mult).then_inc(mix_dve, 1)
                    dve.wait_ge(mix_pool, upto(MIX_POOL, "inv", c, "ixtb"))
                    v_.copy_predicated(xt_st[e][:], pairs_of(bytes_[:, B_XT:B_XT + C]), ab).then_inc(mix_dve, 1)
                    v_.copy_predicated(bd4(x_t), mask4(bytes_[:, B_BD:B_BD + P]), twice(ab)).then_inc(mix_dve, 1)
                    v_.tensor_tensor(arb[c % 3][:], rb, pairs_of(st_le), ALU.mult).then_inc(mix_dve, 1)
                if kind == "inv" and s == "AT":
                    dve.wait_ge(mix_pe, upto(MIX_PE, "inv", c, "AT"))
                    v_.copy_predicated(x_st[e][:], pairs_of(bytes_[:, B_X:B_X + C]), quads(I1[e], C)).then_inc(mix_dve, 1)
                if kind == "inv" and s[0] == "X":
                    j = int(s[1])
                    dve.wait_ge(mix_pe, upto(MIX_PE, "inv", c, f"Y{j}"))
                    y = psum[:, I1[e], PAIRS * C:2 * PAIRS * C].rearrange("p (q n) -> p q n", q=PAIRS)
                    if j < LEVELS - 1:
                        m = B_X + j * C
                        v_.copy_predicated(x_st[e][:], pairs_of(bytes_[:, m:m + C]), quads(I1[e], C)).then_inc(mix_dve, 1)
                        m = B_XT + j * C
                        v_.copy_predicated(xt_st[e][:], pairs_of(bytes_[:, m:m + C]), y).then_inc(mix_dve, 1)
                    m = B_BD + j * P
                    v_.copy_predicated(bd4(x_t), mask4(bytes_[:, m:m + P]), twice(y)).then_inc(mix_dve, 1)
                if kind == "seq" and s == "F":
                    dve.wait_ge(mix_pe, upto(MIX_PE, "seq", c, "F"))
                    ak, rk = quads(S0, P)[:, :, 0:C], quads(S0, P)[:, :, C:P]
                    v_.tensor_tensor(bd4(aak_bd), twice(ak), mask4(bd_strict), ALU.mult).then_inc(mix_dve, 1)
                    v_.tensor_tensor(ark[:], rk, pairs_of(st_le), ALU.mult).then_inc(mix_dve, 1)
                if kind == "seq" and s == "T":
                    dve.wait_ge(mix_pe, upto(MIX_PE, "seq", c, "T2"))
                    for i in range(2):
                        v_.tensor_copy(vv[i * C:(i + 1) * C, :, cols(c)],
                                       quads(S1, P)[0:C, :, i * C:(i + 1) * C]).then_inc(mix_dve, 1)
                    for i in range(2):
                        v_.tensor_copy(top(v_bd, i), quads(S1, P)[0:C, :, i * C:(i + 1) * C]).then_inc(mix_dve, 1)
                if kind == "seq" and s == "SA":
                    dve.wait_ge(mix_pe, upto(MIX_PE, "seq", c, "SA"))
                    pcb = pc[:, :, c:c + 1].to_broadcast([P, PAIRS, C])
                    v_.tensor_tensor(bt[:, :, cols(c)], s_st[:], pcb, ALU.mult).then_inc(mix_dve, 1)
                if kind == "seq" and s == "S":
                    dve.wait_ge(mix_pe, upto(MIX_PE, "seq", c, "S"))
                    dve.wait_ge(mix_dve, upto(MIX_DVE, "seq", c, "decay"))
                    if c:
                        dve.wait_ge(mix_pool, upto(MIX_POOL, "seq", c - 1, "sb1"))
                    v_.tensor_tensor(s_st[:], quads(S1, C), bt[:, :, cols(c)], ALU.add).then_inc(mix_dve, 1)
                if kind == "att" and s == "M":
                    dve.wait_ge(mix_act, upto(MIX_ACT, "att", h, "z4"))
                    dve.wait_ge(mix_pool, upto(MIX_POOL, "att", h, "m3"))
                    if h:
                        dve.wait_ge(mix_pe, upto(MIX_PE, "att", h - 1, "C4"))
                    for i in (1, 0):
                        v_.tensor_scalar(sp_[:, PART[i]], zs[h % 2][:, PART[i]], BIG_Z, None,
                                         ALU.min).then_inc(mix_dve, 1)
                if kind == "att" and s[0] == "L":
                    dve.wait_ge(mix_act, upto(MIX_ACT, "att", h, f"ln{s[1]}"))
                    part = PART[int(s[1])]
                    v_.tensor_tensor(sp_[:, part], sp_[:, part], zs[h % 2][:, part], ALU.max).then_inc(mix_dve, 1)
                if kind == "att" and s[0] == "C":
                    j = int(s[1])
                    rows = META if j == 4 else P
                    dve.wait_ge(mix_pe, upto(MIX_PE, "att", h, s))
                    d = zs[h % 2][0:rows, OFF[j]:OFF[j] + WIDTH[j]]
                    v_.tensor_tensor(d, d, psum[0:rows, CBANK, SEQ - WIDTH[j]:SEQ],
                                     ALU.subtract).then_inc(mix_dve, 1)

            for kind, i in LATE:
                if kind == "osb":
                    lo_unit(dve, U_MIX + 1)
                    dve.wait_ge(osb_h, 1)
                    v_.tensor_sub(osb_lo[:], qT[:], osb_hi[:].bitcast(F32)).then_inc(osb_l, 1)
                if kind == "mean":
                    for q in range(2):
                        dve.wait_ge(post_pe, after(POST_PE, i, f"mean{q}"))
                        y = y_of(2 * i + q)
                        v_.scalar_tensor_tensor(y, bank(4 + q), -1.0 / HD, y, ALU.mult, ALU.add).then_inc(post_dve, 1)
                if kind == "var":
                    for q in range(2):
                        dve.wait_ge(post_pe, after(POST_PE, i, f"var{q}"))
                        if i:
                            dve.wait_ge(post_act, after(POST_ACT, i - 1, f"sqrt{q}"))
                        v_.tensor_scalar(yvar[q][:], bank(6 + q), 1.0 / HD, GN_EPS, ALU.mult, ALU.add).then_inc(post_dve, 1)
                        dve.wait_ge(post_dve, after(POST_DVE, i, f"var{q}"))
                        v_.reciprocal(yrec[q][:], yvar[q][:]).then_inc(post_dve, 1)
                if kind == "gate":
                    for q in range(2):
                        p = 2 * i + q
                        y = y_of(p)
                        dve.wait_ge(post_act, after(POST_ACT, i, f"sqrt{q}"))
                        v_.tensor_mul(y, y, yrs[q][:]).then_inc(post_dve, 1)
                        dve.wait_ge(post_dve, after(POST_DVE, i, f"norm{q}"))
                        v_.tensor_scalar(y, y, vcol[:, V_LG + p:V_LG + p + 1], vcol[:, V_LB + p:V_LB + p + 1],
                                         ALU.mult, ALU.add).then_inc(post_dve, 1)
                        dve.wait_ge(post_dve, after(POST_DVE, i, f"gain{q}"))
                        v_.tensor_add(y, y, bonus[:, p, :]).then_inc(post_dve, 1)
                        dve.wait_ge(post_dve, after(POST_DVE, i, f"bonus{q}"))
                        dve.wait_ge(post_pe, after(POST_PE, i, f"gate{q}"))
                        v_.tensor_mul(yo[q][:], bank(4 + q), y).then_inc(post_dve, 1)
                        dve.wait_ge(post_act, after(POST_ACT, i, f"hi{q}"))
                        v_.tensor_sub(orw_lo[:, p, :], yo[q][:], orw_hi[:, p, :].bitcast(F32)).then_inc(post_dve, 1)
                if kind == "unit":
                    u = U_MIX + i
                    what, j = MERGE[i]
                    lo_unit(dve, u + 2)
                    if what == "branch":
                        n = 2 * j
                        dve.wait_ge(w_used, u + 1)
                        dve.wait_ge(gate_out, n + 2)
                        if j:
                            dve.wait_ge(mrg_dve, 4 * j)
                        v_.tensor_mul(mrg_t[0][:], bank(2), sig_t[n % (2 * AHEAD)][:]).then_inc(mrg_dve, 1)
                        v_.tensor_mul(mrg_t[1][:], bank(3), sig_t[(n + 1) % (2 * AHEAD)][:]).then_inc(mrg_dve, 1)
                        dve.wait_ge(mrg_dve, 4 * j + 2)
                        v_.tensor_add(mrg_t[0][:], mrg_t[0][:], mrg_t[1][:]).then_inc(mrg_dve, 1)
                        dve.wait_ge(mrg_hi, j + 1)
                        v_.tensor_sub(mg_lo[:, j, :], mrg_t[0][:], mg_hi[:, j, :].bitcast(F32)).then_inc(mrg_dve, 1)

            for k in range(KT):
                lo_unit(dve, U_OUT + k + 2)

            def mean_square(at, steps, b, name, squares):
                dve.wait_ge(tail_sq, squares)
                v_.tensor_scalar(small[:, 8 + b:9 + b], small[:, b:b + 1], 1.0 / D, RMS_EPS,
                                 ALU.mult, ALU.add).then_inc(tail_dve, 1)
                dve.wait_ge(tail_dve, at + steps.index(f"ms{name}{b}") + 1)
                v_.reciprocal(small[:, 16 + b:17 + b], small[:, 8 + b:9 + b]).then_inc(tail_dve, 1)

            def add_normed(at, steps, b, row, roots):
                dve.wait_ge(tail_rs, roots)
                v_.scalar_tensor_tensor(ztok[b][:].rearrange("p (a n) -> p a n", a=2), psum[:, 2 * b:2 * b + 2, :],
                                        small[:, 24 + b:25 + b], grows[:, row, :].rearrange("p (a n) -> p a n", a=2),
                                        ALU.mult, ALU.mult).then_inc(tail_dve, 1)
                dve.wait_ge(tail_dve, at + steps.index(f"z{b}") + 1)
                v_.tensor_add(resid[:, b, :], resid[:, b, :], ztok[b][:]).then_inc(tail_dve, 1)

            for b in range(QB):
                mean_square(0, TAIL_1, b, "", b + 1)
            dve.wait_ge(rows_in, 48)
            dve.wait_ge(resid_in, 16)
            for b in range(QB):
                add_normed(0, TAIL_1, b, 0, b + 1)
            for b in range(QB):
                mean_square(0, TAIL_1, b, "_f", QB + b + 1)
            for b in range(QB):
                dve.wait_ge(tail_rs, QB + b + 1)
                v_.scalar_tensor_tensor(ztok[b][:], resid[:, b, :], small[:, 24 + b:25 + b],
                                        grows[:, 1, :], ALU.mult, ALU.mult).then_inc(tail_dve, 1)
            for b in range(QB):
                norm_lo(10 + 2 * b, P, P * b)

            with dve.Fori(0, N_FFN_LOOP) as i:
                per = 2 * len(TAIL_FFN)
                for s in range(RAW):
                    u0 = U_FFN + s
                    v = u0 + 2
                    dve.wait_ge(w_hi_done, i * RAW + (v + 1))
                    v_.tensor_sub(w_lo[v % SPL][:], raw[v % RAW][:], w_hi[v % SPL][:].bitcast(F32)).then_inc(w_split, 1)
                    if s % 2 == 1:
                        t = s // 2
                        at = FFN_AT + t * len(TAIL_FFN)
                        dve.wait_ge(f_sig, i * 2 + (t + 1))
                        v_.tensor_mul(ffn_t[t][:], bank(2 * t), ffn_t[t][:]).then_inc(tail_dve, 1)
                        dve.wait_ge(tail_dve, i * per + (at + 1))
                        v_.tensor_mul(ffn_u[t][:], bank(2 * t + 1), ffn_t[t][:]).then_inc(tail_dve, 1)
                        dve.wait_ge(tail_dve, i * per + (at + 2))
                        tile = i * 2 + t
                        v_.tensor_scalar(act_hi[:, bass.ds(tile, 1), :], ffn_u[t][:].unsqueeze(1), 1.0, None,
                                         ALU.mult).then_inc(tail_dve, 1)
                        dve.wait_ge(tail_dve, i * per + (at + 3))
                        v_.tensor_tensor(act_lo[:, bass.ds(tile, 1), :], ffn_u[t][:].unsqueeze(1),
                                         act_hi[:, bass.ds(tile, 1), :].bitcast(F32),
                                         ALU.subtract).then_inc(tail_dve, 1)
            for k in range(2, FT):
                lo_unit(dve, U_DOWN + k)
            for b in range(QB):
                mean_square(LAST_AT, TAIL_2, b, "", 2 * QB + b + 1)
            for b in range(QB):
                add_normed(LAST_AT, TAIL_2, b, 2, 2 * QB + b + 1)

        @block.tensor
        def _(pe):
            t_ = nc.tensor

            def norm_transpose(n, src, width):
                for h in range(2):
                    if n + h >= 4:
                        pe.wait_ge(n_lo, n + h - 3)
                    for k in range(4):
                        f = (4 * h + k) * P
                        mm = t_.transpose(quads((n + h) % 4, width)[:, k, :], src[0:width, f:f + P],
                                          ident[0:width, 0:width])
                    mm.then_inc(n_tp, 1)

            pe.wait_ge(const_in, 16 * 6)
            t_.transpose(psum[:, 7, 0:NVEC], vrow[:], ident[0:NVEC, 0:NVEC]).then_inc(vec_tp, 1)
            for i, b in enumerate((4, 0, 1, 2, 3)):
                pe.wait_ge(n_x, i + 1)
                norm_transpose(2 * i, xn[b][:, :], META if b == 4 else P)
            pe.wait_ge(n_lo, 10)
            pe.wait_ge(vec_ok, 2)

            for u, (kind, f, p) in enumerate(ORDER):
                pe.wait_ge(w_split, u + 1)
                if u >= 2:
                    pe.wait_ge(in_out, u - 1)
                b = 2 * (u % 2)
                if kind == "sq":
                    outs = [(bank(b), (META, T))]
                else:
                    outs = [(bank(b, HALF), (0, HALF)), (bank(b + 1, HALF), (HALF, T))]
                products(u, 0, outs, h_hi, h_lo, range(KT)).then_inc(w_used, 1)

                q, step = divmod(u - 5, 4)
                hv = ((0, HALF), (HALF, T))
                if q in range(PAIRS) and step == 0:
                    f0 = q * P
                    pe.wait_ge(lora_act, 1)
                    if q:
                        pe.wait_ge(prep_dve, after(PREP_DVE, q - 1, "max"))
                    for i, (c0, c1) in enumerate(hv):
                        mm = t_.matmul(bank(4 + i, HALF), lora[0:64, f0:f0 + P], twx[0:64, c0:c1], start=True, stop=True)
                    mm.then_inc(prep_pe, 1)
                    if q:
                        pe.wait_ge(prep_dve, after(PREP_DVE, q - 1, "bonus"))
                    pe.wait_ge(shifted, 1)
                    for i, (c0, c1) in enumerate(hv):
                        mm = t_.matmul(bank(6 + i, HALF), lora[64:P, f0:f0 + P], twx[64:P, c0:c1], start=True, stop=True)
                    mm.then_inc(prep_pe, 1)
                if q in range(PAIRS) and step == 1:
                    pe.wait_ge(prep_act, after(PREP_ACT, q, "ksq"))
                    for i, (c0, c1) in enumerate(hv):
                        mm = t_.matmul(bank(4 + i, HALF), blk, ksq[:, c0:c1], start=True, stop=True)
                    mm.then_inc(prep_pe, 1)
                if q in range(PAIRS) and step == 3:
                    pe.wait_ge(prep_dve, after(PREP_DVE, q, "rk"))
                    for i, (c0, c1) in enumerate(hv):
                        mm = t_.matmul(bank(6 + i, HALF), blk, rkp[:, c0:c1], start=True, stop=True)
                    mm.then_inc(prep_pe, 1)
                if 19 <= u < 23:
                    o = u - 19
                    pe.wait_ge(in_out, u)
                    if o == 0:
                        pe.wait_ge(prep_dve, after(PREP_DVE, PAIRS - 1, "max"))
                    else:
                        pe.wait_ge(v_out, 2 * o)
                    for b4 in range(QB):
                        t_.transpose(quads(4, P)[:, b4, :], vst[o % 2][:, META + P * b4:META + P * b4 + P], ident)
                    t_.transpose(psum[0:META, 5, 0:P], vst[o % 2][:, 0:META], ident).then_inc(v_tp, 1)

            pe.wait_ge(in_out, N_IN)
            pe.wait_ge(v_out, 2 * PAIRS)
            pe.wait_ge(prep_dve, PAIRS * len(PREP_DVE))
            pe.wait_ge(mix_zero, N_ZERO)

            def pairs(outs, terms):
                for p in range(PAIRS):
                    for i, (w, m) in enumerate(terms):
                        mm = t_.matmul(outs[:, p, :], w(p), m(p), start=(i == 0), stop=(i == len(terms) - 1))
                return mm

            def whole(t):
                return lambda p: t[:, p, :]

            LAST = LEVELS - 1
            for kind, n, s in MIXING:
                c = h = n
                e = c % 2
                at_c = lambda t: lambda p: t[:, p, cols(c)]
                a_and_r = lambda p: ar[:, :, p, cols(c)]
                if kind == "inv" and s == "A":
                    pe.wait_ge(mix_pool, upto(MIX_POOL, "inv", c, "b1"))
                    if c >= 2:
                        pe.wait_ge(mix_act, upto(MIX_ACT, "inv", c - 2, f"wb1_{LAST}"))
                    pairs(quads(I0[e], P), [(whole(b_bd), a_and_r)]).then_inc(mix_pe, 1)
                if kind == "inv" and s == "AT":
                    pe.wait_ge(mix_dve, upto(MIX_DVE, "inv", c, "aab"))
                    pairs(quads(I1[e], C), [(whole(aab_bd[e]), lambda p: st_id)]).then_inc(mix_pe, 1)
                if kind == "inv" and s[0] == "W":
                    j = int(s[1])
                    pe.wait_ge(mix_dve, upto(MIX_DVE, "inv", c, f"x{j - 1}"))
                    pairs(quads(I0[e], C), [(whole(aab_bd[e]), whole(x_st[e]))]).then_inc(mix_pe, 1)
                if kind == "inv" and s[0] == "X":
                    j = int(s[1])
                    pe.wait_ge(mix_dve, upto(MIX_DVE, "inv", c, "x0" if j == 1 else f"xtb{j - 1}"))
                    if j < LAST:
                        pe.wait_ge(mix_act, upto(MIX_ACT, "inv", c, f"w{j}"))
                        pairs(quads(I1[e], C), [(whole(xt_bd[c % 3]), whole(w_st[e]))]).then_inc(mix_pe, 1)
                    pe.wait_ge(mix_act, upto(MIX_ACT, "inv", c, f"wb1_{j}"))
                    y = psum[:, I1[e], PAIRS * C:2 * PAIRS * C].rearrange("p (q n) -> p q n", q=PAIRS)
                    pairs(y, [(whole(w_bd[e]), whole(xt_st[e]))]).then_inc(mix_pe, 1)
                if kind == "seq" and s in ("F", "T"):
                    if s == "F":
                        pe.wait_ge(mix_pool, upto(MIX_POOL, "seq", c, "k1"))
                        if c:
                            pe.wait_ge(mix_act, upto(MIX_ACT, "seq", c - 1, "out"))
                        pairs(quads(S0, P), [(whole(k_bd), a_and_r)]).then_inc(mix_pe, 1)
                        pe.wait_ge(mix_pool, upto(MIX_POOL, "seq", c, "bh"))
                        if c:
                            pe.wait_ge(mix_dve, upto(MIX_DVE, "seq", c - 1, "s"))
                        turns = ((bt, S1),)
                    else:
                        pe.wait_ge(mix_dve, upto(MIX_DVE, "seq", c, "ark"))
                        turns = ((kt, S0), (vv, S1))
                    for src, bnk in turns:
                        if src is vv:
                            pe.wait_ge(mix_act, upto(MIX_ACT, "seq", c, "bh1"))
                        for p in range(PAIRS):
                            mm = t_.transpose(quads(bnk, P)[0:C, p, :], src[:, p, cols(c)], ident)
                        mm.then_inc(mix_pe, 1)
                if kind == "seq" and s == "Z":
                    pe.wait_ge(mix_act, upto(MIX_ACT, "seq", c, "kh1"))
                    pe.wait_ge(mix_dve, upto(MIX_DVE, "seq", c, "vb1"))
                    pairs(quads(S0, C), [(whole(a_bd), whole(s_st)), (whole(aak_bd), at_c(vv))]).then_inc(mix_pe, 1)
                if kind == "seq" and s == "SA":
                    pe.wait_ge(mix_act, upto(MIX_ACT, "seq", c, "z"))
                    pe.wait_ge(mix_dve, upto(MIX_DVE, "inv", c, f"xtb{LAST}"))
                    pairs(quads(S1, C), [(whole(xt_bd[c % 3]), at_c(bt))]).then_inc(mix_pe, 1)
                if kind == "seq" and s == "S":
                    pe.wait_ge(mix_act, upto(MIX_ACT, "seq", c, "sa"))
                    pairs(quads(S1, C), [(whole(bh_bd), at_c(kt)), (whole(kh_bd), at_c(vv))]).then_inc(mix_pe, 1)
                    pe.wait_ge(mix_pool, upto(MIX_POOL, "seq", c, "sab1"))
                    r_c = lambda p: ar[:, 1, p, cols(c)]
                    pairs(quads(S0, C), [(whole(s_bd), r_c), (whole(v_bd), whole(ark)),
                                         (whole(sa_bd), whole(arb[c % 3]))]).then_inc(mix_pe, 1)
                if kind == "att":
                    hp, hr = h // 2, h % 2
                    rows = slice(hr * HD, (hr + 1) * HD)
                    if s[0] == "Q":
                        j = int(s[1])
                        k0, kn = KEYS[j]
                        if j:
                            pe.wait_ge(mix_act, upto(MIX_ACT, "att", h, f"z{j - 1}"))
                        elif h >= 2:
                            pe.wait_ge(mix_act, upto(MIX_ACT, "att", h - 2, "o"))
                        elif h:
                            pe.wait_ge(mix_act, upto(MIX_ACT, "att", 0, "z4"))
                        t_.matmul(psum[0:kn, QBANK, 0:WIDTH[j]], kT[rows, hp, k0:k0 + kn],
                                  qT[rows, hp, SEQ - WIDTH[j]:SEQ], start=True, stop=True).then_inc(mix_pe, 1)
                    if s[0] == "C":
                        j = int(s[1])
                        if j == 3:
                            pe.wait_ge(mix_dve, upto(MIX_DVE, "att", h, "max1"))
                        else:
                            i = 0 if j == 4 else j + 1
                            pe.wait_ge(mix_dve, upto(MIX_DVE, "att", h, f"s{i}"))
                            if i != 0:
                                pe.wait_ge(mix_dve, upto(MIX_DVE, "att", h, "max0"))
                            t_.matmul(psum[:, CBANK, SEQ - WIDTH[i]:SEQ], ctri, sp_[:, OFF[i]:OFF[i] + WIDTH[i]],
                                      start=False, stop=False, skip_group_check=True)
                        kn = KEYS[j][1]
                        t_.matmul(psum[0:kn, CBANK, SEQ - WIDTH[j]:SEQ], tri[0:kn, 0:kn],
                                  sp_[0:kn, OFF[j]:OFF[j] + WIDTH[j]], start=(j == 3), stop=(j == 4),
                                  skip_group_check=True).then_inc(mix_pe, 1)
                    if s == "O":
                        ps = psum[rows, QBANK, :]
                        z_h = zs[h % 2]
                        pe.wait_ge(mix_act, upto(MIX_ACT, "att", h, "wm"))
                        vc = slice(h * HD, (h + 1) * HD)
                        t_.matmul(ps, vmeta[:, vc], z_h[0:META, OFF[4]:NS], start=True, stop=False)
                        for j in range(QB):
                            mm = t_.matmul(ps[:, SEQ - WIDTH[j]:SEQ], vtok[:, j, vc], z_h[:, OFF[j]:OFF[j] + WIDTH[j]],
                                           start=False, stop=(j == QB - 1))
                        mm.then_inc(mix_pe, 1)

            for kind, i in LATE:
                if kind == "osb":
                    pe.wait_ge(mix_act, len(MIX_ACT))
                    pe.wait_ge(mix_dve, len(MIX_DVE))
                if kind == "mean":
                    for q in range(2):
                        if i:
                            pe.wait_ge(post_dve, after(POST_DVE, i - 1, f"out{q}"))
                        t_.matmul(bank(4 + q), blk, y_of(2 * i + q), start=True, stop=True).then_inc(post_pe, 1)
                if kind == "var":
                    for q in range(2):
                        pe.wait_ge(post_act, after(POST_ACT, i, f"sq{q}"))
                        t_.matmul(bank(6 + q), blk, ysq[q][:], start=True, stop=True).then_inc(post_pe, 1)
                if kind == "gate":
                    for q in range(2):
                        pe.wait_ge(post_dve, after(POST_DVE, i, f"centre{q}"))
                        f0 = (2 * i + q) * P
                        t_.matmul(bank(4 + q), gup[:, f0:f0 + P], sg[:, META:T], start=True, stop=True).then_inc(post_pe, 1)
                if kind == "unit":
                    u = U_MIX + i
                    what, j = MERGE[i]
                    pe.wait_ge(w_split, u + 1)
                    if what == "branch":
                        if j == 0:
                            pe.wait_ge(osb_l, 1)
                            pe.wait_ge(post_dve, 2 * len(POST_DVE))
                        else:
                            pe.wait_ge(mrg_dve, 4 * j - 2)
                        products(u, 0, [(bank(2), (0, SEQ))], osb_hi, osb_lo, range(PAIRS))
                        products(u, PAIRS, [(bank(3), (0, SEQ))], orw_hi, orw_lo, range(PAIRS)).then_inc(w_used, 1)
                    else:
                        n = gate_no(i)
                        if n >= 2:
                            pe.wait_ge(gate_out, n - 1)
                        products(u, 0, [(bank(n % 2), (META, T))], h_hi, h_lo, range(KT)).then_inc(w_used, 1)

            def token_major(u0, n, hi, lo):
                for k in range(n):
                    u = u0 + k
                    pe.wait_ge(w_split, u + 1)
                    passes = ((hi, w_hi[u % SPL]), (hi, w_lo[u % SPL]), (lo, w_hi[u % SPL]))
                    for b in range(QB):
                        for i, (xs, w) in enumerate(passes):
                            for h in range(2):
                                mm = t_.matmul(bank(2 * b + h), xs[:, k, P * b:P * b + P], w[:, 512 * h:512 * h + 512],
                                               start=(k == 0 and i == 0), stop=(k == n - 1 and i == 2))
                    mm.then_inc(w_used, 1)

            pe.wait_ge(mrg_dve, 4 * KT)
            pe.wait_ge(gate_out, 2 * KT)
            token_major(U_OUT, KT, mg_hi, mg_lo)

            for b in range(QB):
                pe.wait_ge(tail_dve, TAIL_1.index(f"xn{b}") + 1)
                norm_transpose(10 + 2 * b, ztok[b][:, :], P)
            pe.wait_ge(n_lo, 18)
            with pe.Fori(0, N_FFN_LOOP) as i:
                per = 2 * len(TAIL_FFN)
                for s in range(RAW):
                    u = U_FFN + s
                    t = s // 2
                    pe.wait_ge(w_split, i * RAW + (u + 1))
                    step = 1 + s % 2
                    pe.wait_ge(tail_dve, i * per + (FFN_AT + (t - 2) * len(TAIL_FFN) + step))
                    products(u, 0, [(bank(s), (0, SEQ))], h_hi, h_lo, range(KT)).then_inc(w_used, 1)
            pe.wait_ge(tail_dve, LAST_AT)
            token_major(U_DOWN, FT, act_hi, act_lo)


def tables():
    import numpy as np

    i = np.arange(P)
    row, col = i[:, None], i[None, :]
    f = np.zeros((P, NK), np.float32)
    f[:, K_ID:K_ID + P] = row == col
    f[:, K_TRI:K_TRI + P] = row >= col
    f[:, K_CTRI:K_CTRI + P] = row < col
    head = row // C == col // C
    f[:, K_BLK:K_BLK + P] = head
    f[:, K_BDS:K_BDS + P] = head & (row < col)
    s, t = i[:, None] % C, np.arange(C)[None, :]
    f[:, K_LE:K_LE + C] = s <= t
    f[:, K_ST:K_ST + C] = s == t
    f[:, K_RST:K_RST + T] = (np.arange(T)[None, :] + PAD) % C != 0
    b = np.zeros((P, NB), np.float32)
    for j in range(LEVELS):
        def joins(t, s):
            return (t >> (j + 1) == s >> (j + 1)) & (t >> j & 1 == 1) & (s >> j & 1 == 0)
        b[:, B_X + j * C:B_X + (j + 1) * C] = joins(i[:, None] % C, np.arange(C)[None, :])
        b[:, B_XT + j * C:B_XT + (j + 1) * C] = joins(np.arange(C)[None, :], i[:, None] % C)
        b[:, B_BD + j * P:B_BD + (j + 1) * P] = head & joins(col % C, row % C)
    return f, b


def kernel(**inputs):
    import numpy as np
    import concourse.bacc as bacc
    from concourse.bass_utils import run_bass_kernel_spmd

    a = {k: np.ascontiguousarray(v) for k, v in inputs.items()}
    vecs = np.concatenate([a[k].reshape(-1, P) for k in (
        "rw_shift_mu", "rw_decay_base", "rw_aaa_base", "rw_k_k", "rw_k_a", "rw_r_k", "rw_ln_gain", "rw_ln_bias")])
    kf, kb = tables()
    arrays = {
        "x": a["x"][0], "meta": a["meta_tokens"], "w_in": a["w_in"][0], "w_sb": a["w_branch_sb"][0],
        "w_rw": a["w_branch_rw"][0], "w_out": a["w_out"][0], "w_g": a["w_ffn_gate"][0],
        "w_u": a["w_ffn_up"][0], "w_d": a["w_ffn_down"][0], "decay_up": a["rw_decay_up"][0],
        "aaa_up": a["rw_aaa_up"][0], "gate_up": a["rw_gate_up"][0], "vecs": vecs,
        "g_mix_pre": a["norm_mix_pre"], "g_mix_post": a["norm_mix_post"],
        "g_ffn_pre": a["norm_ffn_pre"], "g_ffn_post": a["norm_ffn_post"], "kf": kf, "kb": kb,
    }
    nc = bacc.Bacc("TRN2", target_bir_lowering=False, num_devices=1)
    args = [nc.dram_tensor(f"in_{n}", v.shape, mybir.dt.from_np(v.dtype), kind="ExternalInput").ap()
            for n, v in arrays.items()]
    out = nc.dram_tensor("out", (SEQ, D), F32, kind="ExternalOutput").ap()
    build(nc, *args, out)
    r = run_bass_kernel_spmd(nc, [{f"in_{n}": np.ascontiguousarray(v) for n, v in arrays.items()}], core_ids=[0])
    return r.results[0]["out"].reshape(1, SEQ, D)
```

```python
from contextlib import ExitStack

import concourse.bass as bass
from concourse import mybir

F32 = mybir.dt.float32
F32R = mybir.dt.float32r
U8 = mybir.dt.uint8
ALU = mybir.AluOpType
ACT = mybir.ActivationFunctionType

P = 128
D = 1024
SEQ = 512
META = 16
T = META + SEQ
HALF = T // 2
KT = D // P
HD = 64
PAIRS = 4
C = 64
PAD = C - META
NC_ = 1 + SEQ // C
TP = NC_ * C
LEVELS = 6
DFF = 2816
FT = DFF // P
QB = SEQ // P
RMS_EPS = 1e-6
GN_EPS = 64e-5
DEC = 0.6065306597126334
BIG_Z = 40.0
N_ZERO = 8
HIDDEN = -1e30

SQ, SK, SV, RR, RK, RV, XWA, XG, GSB, GRW = 0, 4, 8, 12, 16, 20, 24, 25, 26, 34

V_MU, V_DB, V_AB, V_KK, V_KA, V_RK, V_LG, V_LB = 0, 14, 18, 22, 26, 30, 34, 38
NVEC = 42

K_ID, K_TRI, K_CTRI, K_BLK, K_BDS, K_LE, K_RST = 0, 128, 256, 384, 512, 640, 704
NK = K_RST + T
NB = LEVELS * P

RAW = 4
SPL = 2

BLOCKS = (4, 0, 1, 2, 3)

ORDER = [("xwa", XWA, 0), ("xg", XG, 0)]
for _p in range(PAIRS):
    ORDER += [("r", RR + _p, _p), ("k", RK + _p, _p), ("v", RV + _p, _p), ("sk", SK + _p, _p)]
ORDER += [("sv", SV + _p, _p) for _p in range(PAIRS)] + [("sq", SQ + _p, _p) for _p in range(PAIRS)]
N_IN = len(ORDER)
AHEAD = 3
MERGE = []
for _j in range(KT + AHEAD):
    if _j >= AHEAD:
        MERGE += [("branch", _j - AHEAD)]
    if _j < KT:
        MERGE += [("gate_sb", _j), ("gate_rw", _j)]
U_MIX = N_IN
U_OUT = U_MIX + 3 * KT
U_FFN = U_OUT + KT
U_DOWN = U_FFN + 2 * FT
N_UNITS = U_DOWN + FT
N_FFN_LOOP = 2 * FT // RAW
assert U_FFN % SPL == 0 and 2 * FT % RAW == 0 and RAW % SPL == 0

PREP_PE = ["decay", "aaa", "norm"]
PREP_ACT = ["sig", "ksq", "aaa", "inc", "inv", "exc", "rnorm"]
PREP_DVE = ["csum", "max", "recip", "kkn", "a", "bneg", "b", "k_a", "kmod", "rk"]
PREP_POOL = ["csum_x", "kk", "chunk", "r", "k"]
INV_ITEMS = {"B": ([], [], [], ["b0", "b1"]),
             "A": (["A"], [], ["aab", "xt0", "arb"], ["ixt"]),
             **{f"W{_j}": ([f"W{_j}"], [f"w{_j}"], [], []) for _j in range(1, LEVELS)},
             **{f"Y{_j}": ([f"Y{_j}"], [], [f"xt{_j}"], []) for _j in range(1, LEVELS)},
             **{f"R{_j}": ([f"R{_j}"], [f"x{_j}"], [], []) for _j in range(LEVELS - 1)}}
SEQ_ITEMS = {"K": ([], [], [], ["k0", "k1", "a0", "a1", "kh", "bh"]),
             "F": (["F", "T0"], ["bh0", "bh1"], ["aak", "ark"], []),
             "T": (["T1", "T2"], ["kh0", "kh1"], ["v0", "v1"], []),
             "Z": (["Z"], ["z"], [], []),
             "SA": (["SA"], ["sa"], ["decay"], []),
             "S": (["OUT", "S"], ["out"], ["s"], [])}
ATT_ITEMS = {**{f"Q{_j}": ([f"Q{_j}"], [f"z{_j}"], [], [f"m{_j}"] if _j < 4 else []) for _j in range(5)},
             "M": ([], [], ["min1", "min0"], []),
             "E1": ([], ["exp1"], [], []), "E0": ([], ["exp0"], [], []),
             "L1": ([], ["ln1"], ["max1"], []), "L0": ([], ["ln0"], ["max0"], []),
             "H1": ([], [], ["hi1", "lo1"], []), "H0": ([], [], ["hi0", "lo0"], []),
             **{f"C{_j}": ([f"C{_j}"], [], [f"s{_j}"], []) for _j in range(5)},
             "V1": ([], ["w1"], [], []), "V0": ([], ["w0", "wm"], [], []),
             "O": (["O"], ["o"], [], [])}
ITEMS = {"inv": INV_ITEMS, "seq": SEQ_ITEMS, "att": ATT_ITEMS}
POST_ITEMS = {"mean": (["mean0", "mean1"], ["sq0", "sq1"], ["centre0", "centre1"], []),
              "var": (["var0", "var1"], ["root0", "root1"], ["recip0", "recip1"], []),
              "gate": (["gate0", "gate1"], ["gain0", "gain1"], ["norm0", "norm1"], ["bonus0", "bonus1"]),
              "out": ([], ["hi0", "hi1"], ["out0", "out1"], ["lo0", "lo1"])}
LATE = [("osb", 0), ("mean", 0), ("unit", 0), ("unit", 1), ("var", 0), ("mean", 1), ("unit", 2), ("gate", 0),
        ("out", 0), ("unit", 3), ("var", 1), ("unit", 4), ("gate", 1), ("out", 1), ("unit", 5)]
LATE += [("unit", i) for i in range(2 * AHEAD, len(MERGE))]
POST_PE, POST_ACT, POST_DVE, POST_POOL = (
    [("post", r, step) for item, r in LATE if item in POST_ITEMS for step in POST_ITEMS[item][e]] for e in range(4))
OUT_ORDER = (3, 0, 1, 2)
DOWN_ORDER = (2, 3, 0, 1)


def tail_steps(lists):
    return [f"{s}{t - i}" for t in range(QB + len(lists) - 1) for i, steps in enumerate(lists)
            if 0 <= t - i < QB for s in steps]


TAIL_1_ACT = [f"{s}{n}" for t in range(QB + 1) for s, n in (("sq", t), ("root", t), ("sq_f", t - 1), ("root_f", t - 1))
              if 0 <= n < QB]
TAIL_1 = [s for s in tail_steps([["rec", "z", "res"], ["rec_f", "xn"]])
          if s not in ("res0", "res1", "res2")]
TAIL_FFN = ["silu", "act", "hi", "lo"]
TAIL_2_ACT = tail_steps([["sq", "root"]])
TAIL_2 = tail_steps([["rec", "z", "res"]])
FFN_AT = len(TAIL_1)
LAST_AT = FFN_AT + FT * len(TAIL_FFN)


def after(steps, n, step):
    return n * len(steps) + steps.index(step) + 1


def mixing_order():
    heads = 2 * PAIRS
    att = [("att", 0, f"Q{j}") for j in range(5)]
    for h in range(heads):
        for s in ("M", "E1", "O-", "E0", "L1", "L0", "H1", "Q0", "H0", "C3", "Q1", "C2", "Q2", "C1", "Q3", "V1",
                  "C0", "Q4", "C4", "V0"):
            if s == "O-":
                att += [("att", h - 1, "O")] if h else []
            elif s[0] == "Q":
                att += [("att", h + 1, s)] if h + 1 < heads else []
            else:
                att += [("att", h, s)]
    att += [("att", heads - 1, "O")]
    inverse = ["A", "R0"] + [f"{s}{j}" for j in range(1, LEVELS) for s in ("W", "Y", "R")][:-1]
    half = len(inverse) // 2
    rounds = half * (NC_ - 1) + len(inverse) + 2
    order = [("inv", 0, "B")]
    taken = 0
    for r in range(rounds):
        seq = []
        for c in range(NC_):
            for at, item in ((-7, "K"), (-5, "F"), (-4, "T"), (-3, "Z"), (0, "SA"), (1, "S")):
                if r == half * c + len(inverse) + at:
                    seq.append(("seq", c, item))
            if c and r == half * c - 2:
                seq.append(("inv", c, "B"))
        lots = [[("inv", c, inverse[r - half * c]) for c in range(e, NC_, 2) if 0 <= r - half * c < len(inverse)]
                for e in range(2)] + [seq]
        for i, lot in enumerate(lots):
            order += lot
            upto = (3 * r + i + 1) * len(att) // (3 * rounds)
            order += att[taken:upto]
            taken = upto
    return order


MIXING = mixing_order()
LAST_C = NC_ - 1
LEFT_OUT = [("seq", LAST_C, s) for s in ("T0", "T1", "S", "bh0", "bh1", "kh0", "kh1", "decay", "s", "kh", "bh")]
MIX_PE, MIX_ACT, MIX_DVE, MIX_POOL = (
    [(kind, n, step) for kind, n, item in MIXING for step in ITEMS[kind][item][e] if (kind, n, step) not in LEFT_OUT]
    for e in range(4))


def upto(steps, kind, n, step):
    return steps.index((kind, n, step)) + 1


def build(nc, x, meta, w_in, w_sb, w_rw, w_out, w_g, w_u, w_d, decay_up, aaa_up, gate_up,
          vecs, g_mix_pre, g_mix_post, g_ffn_pre, g_ffn_post, kf, kb, out):
    with ExitStack() as ctx:
        def sem(name):
            return ctx.enter_context(nc.semaphore(name))

        base = (nc.sbuf_base + 31) // 32 * 32
        end = nc.sbuf_usable_end
        cursor = [base]

        def sb(name, shape, dt=F32):
            size = 1
            for n in shape[1:]:
                size *= n
            size *= 1 if dt == U8 else 4
            t = nc.alloc_sbuf_tensor_at(name, shape, dt, offset=cursor[0])
            cursor[0] += (size + 31) // 32 * 32
            assert cursor[0] <= end, (name, cursor[0], end)
            return t

        raw_at = cursor[0]
        raw = [sb(f"w_raw{i}", [P, 1024]) for i in range(RAW)]
        w_hi, w_lo, split_at = [], [], []
        for i in range(SPL):
            split_at.append(cursor[0])
            w_hi.append(sb(f"w_hi{i}", [P, 1024], F32R))
            w_lo.append(sb(f"w_lo{i}", [P, 1024], F32R))
        consts = sb("consts", [P, NK])
        bytes_ = sb("byte_masks", [P, NB], U8)
        vcol = sb("vec_cols", [P, NVEC + 4])
        small = sb("small", [P, 32])
        gup = sb("gate_up_w", [P, 512])
        ident = consts[:, K_ID:K_ID + P]
        blk = consts[:, K_BLK:K_BLK + P]
        bd_strict = consts[:, K_BDS:K_BDS + P]
        st_le = consts[:, K_LE:K_LE + C]
        reset = consts[:, K_RST:K_RST + T]

        h_hi = sb("h_hi", [P, KT, T], F32R)
        h_lo = sb("h_lo", [P, KT, T], F32R)
        ffn_at = cursor[0]
        qT = sb("qT", [P, PAIRS, SEQ])
        kv_at = cursor[0]
        kT = sb("kT", [P, PAIRS, T])
        vtok = sb("v_tok", [P, QB, 512])
        vmeta = sb("v_meta", [META, 512])
        ar = sb("a_r", [P, 2, PAIRS, TP])
        bk_at = cursor[0]
        bt = sb("b_t", [P, PAIRS, TP])
        kt = sb("k_t", [P, PAIRS, TP])
        vv = sb("v_t", [P, PAIRS, TP])
        sg = sb("sig_xg", [P, T])
        bonus = sb("bonus", [P, PAIRS, SEQ])
        pc = sb("p_chunk", [P, PAIRS, NC_])
        mix_at = cursor[0]

        xb = [sb(f"x_in{i}", [P, D]) for i in range(5)]
        xn = [sb(f"x_norm{i}", [P, D]) for i in range(5)]
        g_row = sb("g_row", [P, D])
        masks_f = sb("masks_f", [P, NB])
        norm_end = cursor[0]

        cursor[0] = mix_at
        stage = [sb(f"shift_in{i}", [P, T + 1]) for i in range(3)]
        diff = sb("shift_diff", [P, T])
        twx = sb("tanh_xw_xa", [P, T])
        rp = [sb(f"r_pair{i}", [P, T]) for i in range(2)]
        kp = [sb(f"k_pair{i}", [P, T]) for i in range(2)]
        vst = [sb(f"v_stage{i}", [P, T]) for i in range(2)]
        sig_w = sb("sig_w", [P, T])
        csum = sb("csum", [P, T])
        csum_x = sb("csum_x", [P, T])
        p_inc = sb("p_inc", [P, T])
        p_inv = sb("p_inv", [P, T])
        p_exc = sb("p_exc", [P, T])
        a_gate = sb("a_gate", [P, T])
        ksq = sb("k_sq", [P, T])
        rnorm = sb("r_norm", [P, T])
        kkn = sb("kk_n", [P, T])
        bneg = sb("b_neg", [P, T])
        kmod = sb("k_mod", [P, T])
        rkp = sb("rk_prod", [P, T])
        cursor[0] = max(cursor[0], norm_end)
        vrow = sb("vec_rows", [NVEC, P])
        lora = sb("lora", [P, 512])

        cursor[0] = mix_at
        def bd(name):
            return sb(name, [P, PAIRS, P])

        def st(name):
            return sb(name, [P, PAIRS, C])

        b_bd = bd("b_bd")
        xt_bd = [bd(f"xt_bd{i}") for i in range(3)]
        arb = [st(f"arb{i}") for i in range(3)]
        x_bd = [bd(f"x_bd{i}") for i in range(2)]
        w_bd = [bd(f"w_bd{i}") for i in range(2)]
        a_bd, k_bd, aak_bd, bh_bd, kh_bd, v_bd, z_bd, sa_bd, s_bd = (
            bd(n) for n in ("a_bd", "k_bd", "aak_bd", "bh_bd", "kh_bd", "v_bd", "z_bd", "sa_bd", "s_bd"))
        ark = st("ark")
        NS = 1280 + SEQ
        zs0 = sb("scores0", [P, NS])
        sp_at = cursor[0]
        sp_ = sb("softplus", [P, NS])
        cursor[0] = sp_at
        sp_lo = sb("softplus_lo", [P, NS], F32R)
        cursor[0] = raw_at + 4 * 1024
        tri_r = sb("tri_r", [P, 2 * P], F32R)
        sp_hi = sb("softplus_hi", [P, NS], F32R)
        aab_bd = [bd(f"aab_bd{i}") for i in range(2)]
        cursor[0] = split_at[1]
        zs = [zs0, sb("scores1", [P, NS])]

        cursor[0] = mix_at
        mg_hi = sb("merged_hi", [P, KT, SEQ], F32R)
        mg_lo = sb("merged_lo", [P, KT, SEQ], F32R)
        sig_t = [sb(f"sig_t{i}", [P, SEQ]) for i in range(2 * AHEAD)]
        mrg_t = [sb(f"merge_t{i}", [P, SEQ]) for i in range(2)]
        cursor[0] = kv_at
        osb_hi = sb("osb_hi", [P, PAIRS, SEQ], F32R)
        osb_lo = sb("osb_lo", [P, PAIRS, SEQ], F32R)
        cursor[0] = bk_at
        orw_hi = sb("orw_hi", [P, PAIRS, SEQ], F32R)
        orw_lo = sb("orw_lo", [P, PAIRS, SEQ], F32R)
        cursor[0] = mix_at
        ysq = [sb(f"y_sq{i}", [P, SEQ]) for i in range(2)]
        yrec = [sb(f"y_rec{i}", [P, SEQ]) for i in range(2)]
        yrs = [sb(f"y_rs{i}", [P, SEQ]) for i in range(2)]
        yo = [sb(f"y_o{i}", [P, SEQ]) for i in range(2)]

        cursor[0] = ffn_at
        resid = sb("resid", [P, QB, D])
        grows = sb("g_rows", [P, 3, D])
        assert cursor[0] <= mix_at, (cursor[0], mix_at)
        act_at = cursor[0]
        act_hi = sb("act_hi", [P, FT, SEQ], F32R)
        act_lo = sb("act_lo", [P, FT, SEQ], F32R)
        ffn_t = [sb(f"ffn_t{i}", [P, SEQ]) for i in range(2)]
        ffn_u = [sb(f"ffn_u{i}", [P, SEQ]) for i in range(2)]
        cursor[0] = act_at
        ztok = [sb(f"z_tok{b}", [P, D]) for b in range(QB)]
        psum = ctx.enter_context(nc.psum_tensor("psum", [P, 8, 512], F32))

        def bank(b, n=512):
            return psum[:, b, 0:n]

        def both(b):
            return psum[:, b:b + 2, 0:HALF]

        def halves(ap):
            return ap.rearrange("p (a b) -> p a b", a=2)

        def quads(b, n):
            return psum[:, b, 0:PAIRS * n].rearrange("p (q n) -> p q n", q=PAIRS)

        ident_in = sem("ident_in")
        gain_in = sem("gain_in")
        vec_in = sem("vec_in")
        const_in = sem("const_in")
        x_in = [sem(f"x_in{i}") for i in range(5)]
        rows_in = sem("rows_in")
        resid_in = sem("resid_in")
        w_in_raw = [sem(f"w_landed{i}") for i in range(RAW)]
        w_hi_done = sem("w_hi_done")
        w_split = sem("w_split")
        w_used = sem("w_used")
        n_sq = sem("norm_sq")
        n_dve = sem("norm_dve")
        n_rs = sem("norm_rs")
        n_x = sem("norm_x")
        n_tp = sem("norm_transposed")
        n_hi = sem("norm_hi")
        n_lo = sem("norm_lo")
        vec_tp = sem("vec_tp")
        vec_ok = sem("vec_ok")
        edge = sem("edge_zero")
        in_out = sem("in_out")
        sh_diff = sem("shift_diff")
        shifted = sem("shifted")
        lora_act = sem("lora_act")
        v_tp = sem("v_tp")
        v_out = sem("v_out")
        prep_pe, prep_act, prep_dve, prep_pool = (sem(f"prep_{e}") for e in ("pe", "act", "dve", "pool"))
        bonus_pe = sem("bonus_pe")
        bonus_dve = sem("bonus_dve")
        zero_1 = sem("zero_1")
        tri_ok = sem("tri_ok")
        mix_zero = sem("mix_zero")
        mix_pe, mix_act, mix_dve, mix_pool = (sem(f"mix_{e}") for e in ("pe", "act", "dve", "pool"))
        post_pe, post_act, post_dve, post_pool = (sem(f"post_{e}") for e in ("pe", "act", "dve", "pool"))
        osb_h = sem("osb_h")
        osb_l = sem("osb_l")
        gate_out = sem("gate_out")
        mrg_dve = sem("merge_dve")
        mrg_hi = sem("merge_hi")
        tail_act = sem("tail_act")
        blocks_done = sem("blocks_done")
        eps_ok = sem("eps_ok")
        res_pool = sem("res_pool")
        tail_dve = sem("tail_dve")
        f_sig = sem("ffn_sig")
        stored = sem("stored")

        block = ctx.enter_context(nc.Block())

        def tile_of(w, f):
            return w[:, f * P:(f + 1) * P].rearrange("(k p) n -> p k n", p=P)

        def raw3(u, k=KT):
            return raw[u % RAW][:, 0:k * P].rearrange("p (k n) -> p k n", k=k)

        def load_unit(sp, u):
            if u >= RAW:
                sp.wait_ge(w_split, u - RAW + 1)
            if u < U_MIX:
                sp.dma_start(raw3(u), tile_of(w_in, ORDER[u][1])).then_inc(w_in_raw[u % RAW], 16)
            elif u < U_OUT:
                kind, j = MERGE[u - U_MIX]
                if kind == "branch":
                    half = KT // 2
                    sp.dma_start(raw3(u)[:, 0:half], tile_of(w_sb, j)).then_inc(w_in_raw[u % RAW], 16)
                    sp.dma_start(raw3(u)[:, half:KT], tile_of(w_rw, j)).then_inc(w_in_raw[u % RAW], 16)
                else:
                    f = (GSB if kind == "gate_sb" else GRW) + j
                    sp.dma_start(raw3(u), tile_of(w_in, f)).then_inc(w_in_raw[u % RAW], 16)
            elif u < U_FFN:
                k = u - U_OUT
                sp.dma_start(raw[u % RAW][:], w_out[k * P:(k + 1) * P, :]).then_inc(w_in_raw[u % RAW], 16)
            else:
                k = u - U_DOWN
                sp.dma_start(raw[u % RAW][:], w_d[k * P:(k + 1) * P, :]).then_inc(w_in_raw[u % RAW], 16)

        def landed(u):
            n = sum(1 + (U_MIX <= v < U_OUT and MERGE[v - U_MIX][0] == "branch")
                    for v in range(u % RAW, u + 1, RAW))
            return 16 * n

        def hi_unit(act, u):
            act.wait_ge(w_in_raw[u % RAW], landed(u))
            if u >= SPL:
                act.wait_ge(w_used, u - SPL + 1)
            nc.scalar.activation(w_hi[u % SPL][:], raw[u % RAW][:], ACT.Copy).then_inc(w_hi_done, 1)

        def lo_unit(dve, u):
            dve.wait_ge(w_hi_done, u + 1)
            nc.vector.tensor_sub(w_lo[u % SPL][:], raw[u % RAW][:],
                                 w_hi[u % SPL][:].bitcast(F32)).then_inc(w_split, 1)

        def products(u, w0, outs, xh, xl, kts, last=False):
            hi, lo = w_hi[u % SPL], w_lo[u % SPL]
            n = 0
            total = 3 * len(kts)
            for i, k in enumerate(kts):
                for w, xs in ((hi, xh), (hi, xl), (lo, xh)):
                    for o, (c0, c1) in outs:
                        mm = nc.tensor.matmul(o, w[:, (w0 + i) * P:(w0 + i + 1) * P], xs[:, k, c0:c1],
                                              start=(n == 0), stop=(n == total - 1))
                    n += 1
            return mm

        WIDTH = [SEQ - P * j for j in range(QB)] + [SEQ]
        OFF = [sum(WIDTH[:j]) for j in range(QB + 1)]
        KEYS = [(META + P * j, P) for j in range(QB)] + [(0, META)]
        PART = (slice(0, NS // 2), slice(NS // 2, NS))
        I0, I1 = (0, 2), (1, 3)
        S0, S1 = 4, 5
        CBANK, QBANK = 6, 7

        def cols(c):
            return slice(c * C, (c + 1) * C)

        def top(ap, h):
            return ap[h * C:(h + 1) * C, :, h * C:(h + 1) * C]

        def y_of(p):
            return ar[:, 0, p, C:TP]

        @block.sync
        def _(sp):
            sp.dma_start(xb[4][0:META, :], meta).then_inc(x_in[4], 16)
            sp.dma_start(xb[0][:], x[0:P, :]).then_inc(x_in[0], 16)
            sp.dma_start(g_row[:], g_mix_pre.to_broadcast([P, D])).then_inc(gain_in, 16)
            sp.dma_start(ident, kf[:, K_ID:K_ID + P]).then_inc(ident_in, 16)
            for b in range(1, QB):
                sp.dma_start(xb[b][:], x[b * P:(b + 1) * P, :]).then_inc(x_in[b], 16)
            load_unit(sp, 0)
            sp.dma_start(vrow[:], vecs).then_inc(vec_in, 16)
            load_unit(sp, 1)
            for dst, src in ((masks_f[:], kb), (consts[:, K_TRI:NK], kf[:, K_TRI:NK]), (lora[0:64, :], decay_up),
                             (lora[64:P, :], aaa_up), (gup[:], gate_up)):
                sp.dma_start(dst, src).then_inc(const_in, 16)
            for u in range(2, U_FFN):
                if u == U_OUT + RAW:
                    sp.wait_ge(w_used, U_OUT)
                    for i, g in enumerate((g_mix_post, g_ffn_pre, g_ffn_post)):
                        sp.dma_start(grows[:, i, :], g.to_broadcast([P, D])).then_inc(rows_in, 16)
                    sp.dma_start(resid[:], x.rearrange("(b p) d -> p b d", p=P)).then_inc(resid_in, 16)
                if u == U_MIX + 1:
                    sp.wait_ge(mix_pe, len(MIX_PE))
                load_unit(sp, u)
            with sp.Fori(0, N_FFN_LOOP) as i:
                for s in range(RAW):
                    sp.wait_ge(w_split, i * RAW + (U_FFN + s - RAW + 1))
                    f = i * (RAW // 2) + s // 2
                    w = (w_g, w_u)[s % 2]
                    sl = (U_FFN + s) % RAW
                    sp.dma_start(raw[sl][:, :].rearrange("p (k n) -> p k n", k=KT),
                                 w.rearrange("(k p) n -> p k n", p=P)[:, :, bass.ds(f * P, P)]
                                 ).then_inc(w_in_raw[sl], 16)
            for u in range(U_DOWN, N_UNITS):
                load_unit(sp, u)
            for n, b in enumerate(DOWN_ORDER):
                sp.wait_ge(tail_dve, LAST_AT + TAIL_2.index(f"res{n}") + 1)
                sp.dma_start(out[b * P:(b + 1) * P, :], resid[:, b, :]).then_inc(stored, 16)
            sp.wait_ge(stored, 16 * QB)

        @block.gpsimd
        def _(pool):
            g = nc.gpsimd

            def lo_beside(us):
                for u in us:
                    pool.wait_ge(w_hi_done, u + 1)
                    g.tensor_sub(w_lo[u % SPL][:], raw[u % RAW][:], w_hi[u % SPL][:].bitcast(F32)).then_inc(w_split, 1)

            lo_beside([0])
            pool.wait_ge(const_in, 16 * 5)
            g.tensor_copy(bytes_[:], masks_f[:]).then_inc(edge, 1)
            for t in stage:
                pool.wait_ge(n_x, 5)
                g.memset(t[:, 0:1], 0.0).then_inc(edge, 1)
            for t in (ar[:, 0], ar[:, 1], bt, kt, vv):
                g.memset(t[:, :, 0:PAD], 0.0).then_inc(edge, 1)
            for p in range(PAIRS):
                pool.wait_ge(prep_dve, after(PREP_DVE, p, "csum"))
                if p:
                    pool.wait_ge(prep_act, after(PREP_ACT, p - 1, "exc"))
                    pool.wait_ge(prep_dve, after(PREP_DVE, p - 1, "bneg"))
                g.tensor_sub(csum_x[:], csum[:], sig_w[:]).then_inc(prep_pool, 1)
                pool.wait_ge(shifted, 2 + 3 * p + 2)
                g.tensor_scalar(kkn[:], kp[p % 2][:], vcol[:, V_KK + p:V_KK + p + 1], None,
                                ALU.mult).then_inc(prep_pool, 1)
                pool.wait_ge(prep_act, after(PREP_ACT, p, "inc"))
                g.tensor_copy(pc[:, p, :], p_inc[:, C - 1 - PAD::C]).then_inc(prep_pool, 1)
                g.tensor_tensor(ar[:, 1, p, PAD:TP], rp[p % 2][:], p_inc[:], ALU.mult).then_inc(prep_pool, 1)
                pool.wait_ge(prep_dve, after(PREP_DVE, p, "kmod"))
                pool.wait_ge(prep_act, after(PREP_ACT, p, "inv"))
                g.tensor_tensor(kt[:, p, PAD:TP], kmod[:], p_inv[:], ALU.mult).then_inc(prep_pool, 1)
            pool.wait_ge(prep_pool, PAIRS * len(PREP_POOL))
            pool.wait_ge(bonus_dve, PAIRS)
            pool.wait_ge(prep_act, after(PREP_ACT, PAIRS - 1, "rnorm"))
            pool.wait_ge(v_tp, PAIRS)
            for t in (b_bd, k_bd, a_bd, bh_bd, kh_bd, v_bd, s_bd):
                g.memset(t[:], 0.0).then_inc(mix_zero, 1)
            g.memset(zs[0][:, OFF[4]:NS], 0.0).then_inc(mix_zero, 1)
            pool.wait_ge(mix_zero, N_ZERO)
            steps = 0
            for kind, n, item in MIXING:
                if ITEMS[kind][item][3] and steps:
                    pool.wait_ge(mix_pool, steps)
                steps += sum((kind, n, s) in MIX_POOL for s in ITEMS[kind][item][3])
                c = h = n
                e = c % 2
                if (kind, item) == ("inv", "B"):
                    if c:
                        pool.wait_ge(mix_pe, upto(MIX_PE, "inv", c - 1, "A"))
                    for i in range(2):
                        g.tensor_copy(top(b_bd, i), bt[i * C:(i + 1) * C, :, cols(c)]).then_inc(mix_pool, 1)
                if (kind, item) == ("inv", "A"):
                    if c >= 3:
                        pool.wait_ge(mix_pe, upto(MIX_PE, "seq", c - 3, "SA"))
                    g.tensor_copy(xt_bd[c % 3][:], ident.unsqueeze(1).to_broadcast([P, PAIRS, P])).then_inc(mix_pool, 1)
                if (kind, item) == ("seq", "K"):
                    pcb = pc[:, :, c:c + 1].to_broadcast([P, PAIRS, C])
                    if c:
                        pool.wait_ge(mix_pe, upto(MIX_PE, "seq", c - 1, "Z"))
                    for src, dst in ((kt, k_bd), (ar[:, 0], a_bd)):
                        for i in range(2):
                            g.tensor_copy(top(dst, i), src[i * C:(i + 1) * C, :, cols(c)]).then_inc(mix_pool, 1)
                    if c == LAST_C:
                        continue
                    pool.wait_ge(mix_pool, upto(MIX_POOL, "seq", c, "a1"))
                    g.tensor_tensor(kt[:, :, cols(c)], kt[:, :, cols(c)], pcb, ALU.mult).then_inc(mix_pool, 1)
                    g.tensor_tensor(bt[:, :, cols(c)], bt[:, :, cols(c)], pcb, ALU.mult).then_inc(mix_pool, 1)
                if (kind, n, item) == ("att", 0, "Q4"):
                    pool.wait_ge(w_used, N_IN)
                    g.memset(zs[1][:, OFF[4]:NS], 0.0).then_inc(zero_1, 1)
                    pool.wait_ge(zero_1, 1)
                if kind == "att" and item[0] == "Q" and item != "Q4":
                    j = int(item[1])
                    pool.wait_ge(mix_act, upto(MIX_ACT, "att", h, f"z{j}"))
                    d = zs[h % 2][:, OFF[j]:OFF[j] + P]
                    g.affine_select(out=d, in_=d, compare_op=ALU.is_gt, fill=HIDDEN, base=0,
                                    pattern=[[1, P]], channel_multiplier=-1).then_inc(mix_pool, 1)

            pool.wait_ge(osb_h, 1)
            g.tensor_sub(osb_lo[:], qT[:], osb_hi[:].bitcast(F32)).then_inc(osb_l, 1)
            for item, r in LATE:
                for q in range(2):
                    p = 2 * r + q
                    if item == "gate":
                        y = y_of(p)
                        pool.wait_ge(post_act, upto(POST_ACT, "post", r, f"gain{q}"))
                        g.tensor_add(y, y, bonus[:, p, :]).then_inc(post_pool, 1)
                    if item == "out":
                        pool.wait_ge(post_act, upto(POST_ACT, "post", r, f"hi{q}"))
                        g.tensor_sub(orw_lo[:, p, :], yo[q][:], orw_hi[:, p, :].bitcast(F32)).then_inc(post_pool, 1)

            pool.wait_ge(resid_in, 16)
            for n, b in enumerate(OUT_ORDER[:-1]):
                pool.wait_ge(tail_dve, TAIL_1.index(f"z{n}") + 1)
                g.tensor_add(resid[:, b, :], resid[:, b, :], ztok[b][:]).then_inc(res_pool, 1)

            lo_beside([U_FFN, U_FFN + 1])

        def gate_no(i):
            kind, j = MERGE[i]
            return 2 * j + (kind == "gate_rw")

        def norm_cols(b):
            return (0, META) if b == 4 else (META + P * b, P)

        @block.scalar
        def _(act):
            s_ = nc.scalar

            def norm_hi(n, width, c0, b=None):
                b = n % 4 if b is None else b
                for h in range(2):
                    act.wait_ge(n_tp, n + h + 1)
                    s_.activation(h_hi[:, 4 * h:4 * h + 4, c0:c0 + width], quads(b + h, width),
                                  ACT.Copy).then_inc(n_hi, 1)

            def square(i):
                b = BLOCKS[i]
                n = META if b == 4 else P
                act.wait_ge(x_in[b], 16)
                s_.activation(xn[b][0:n, :], xb[b][0:n, :], ACT.Square,
                              accum_out=small[0:n, b:b + 1]).then_inc(n_sq, 1)

            def root(i):
                b = BLOCKS[i]
                act.wait_ge(n_dve, 2 * i + 3)
                s_.activation(small[:, 24 + b:25 + b], small[:, 16 + b:17 + b], ACT.Sqrt).then_inc(n_rs, 1)

            act.wait_ge(n_dve, 1)
            s_.activation(small[:, 31:32], small[:, 5:6], ACT.Sqrt).then_inc(n_rs, 1)
            square(0)
            for i in range(len(BLOCKS)):
                if i + 1 < len(BLOCKS):
                    square(i + 1)
                root(i)
                if i:
                    norm_hi(2 * i - 2, norm_cols(BLOCKS[i - 1])[1], norm_cols(BLOCKS[i - 1])[0])
            hi_unit(act, 0)
            norm_hi(8, norm_cols(3)[1], norm_cols(3)[0])
            act.wait_ge(vec_tp, 1)
            s_.activation(vcol[:, 0:NVEC], psum[:, 7, 0:NVEC], ACT.Copy).then_inc(vec_ok, 1)
            hi_unit(act, 1)

            n_shift = 0
            for u, (kind, f, p) in enumerate(ORDER):
                act.wait_ge(w_used, u + 1)
                if u == 0:
                    act.wait_ge(edge, 9)
                ps = both(2 * (u % 2))
                if kind in ("xwa", "xg", "r", "k", "v"):
                    if n_shift >= 3:
                        act.wait_ge(shifted, n_shift - 2)
                    s_.activation(halves(stage[n_shift % 3][:, 1:T + 1]), ps, ACT.Copy).then_inc(in_out, 1)
                    n_shift += 1
                elif kind == "sk":
                    s_.activation(halves(kT[:, p, :]), ps, ACT.Copy).then_inc(in_out, 1)
                elif kind == "sv":
                    if p >= 2:
                        act.wait_ge(v_tp, p - 1)
                    s_.activation(halves(vst[p % 2][:]), ps, ACT.Copy).then_inc(in_out, 1)
                else:
                    s_.activation(qT[:, p, :], bank(2 * (u % 2)), ACT.Copy, scale=HD ** -0.5).then_inc(in_out, 1)
                if u + 2 != U_MIX + 1:
                    hi_unit(act, u + 2)
                if u == 1:
                    act.wait_ge(shifted, 1)
                    s_.activation(twx[0:64, :], twx[0:64, :], ACT.Tanh).then_inc(lora_act, 1)
                if u == 2:
                    act.wait_ge(shifted, 2)
                    s_.activation(sg[:], sg[:], ACT.Sigmoid).then_inc(lora_act, 1)
                    act.wait_ge(vec_ok, 2)
                q, step = divmod(u - 5, 4)
                if q in range(PAIRS) and step == 0:
                    act.wait_ge(prep_pe, after(PREP_PE, q, "decay"))
                    if q:
                        act.wait_ge(prep_dve, after(PREP_DVE, q - 1, "k_a"))
                    s_.activation(halves(sig_w[:]), both(4), ACT.Sigmoid,
                                  bias=vcol[:, V_DB + q:V_DB + q + 1]).then_inc(prep_act, 1)
                    act.wait_ge(shifted, 2 + 3 * q + 2)
                    s_.activation(ksq[:], kp[q % 2][:], ACT.Square,
                                  scale=vcol[:, V_KK + q:V_KK + q + 1]).then_inc(prep_act, 1)
                if q in range(PAIRS) and step == 1:
                    act.wait_ge(prep_pe, after(PREP_PE, q, "aaa"))
                    s_.activation(halves(a_gate[:]), both(6), ACT.Sigmoid,
                                  bias=vcol[:, V_AB + q:V_AB + q + 1]).then_inc(prep_act, 1)
                    if q:
                        act.wait_ge(prep_pool, after(PREP_POOL, q - 1, "k"))
                    act.wait_ge(prep_dve, after(PREP_DVE, q, "csum"))
                    s_.activation(p_inc[:], csum[:], ACT.Exp, scale=-DEC).then_inc(prep_act, 1)
                    s_.activation(p_inv[:], csum[:], ACT.Exp, scale=DEC).then_inc(prep_act, 1)
                    act.wait_ge(prep_pool, after(PREP_POOL, q, "csum_x"))
                    s_.activation(p_exc[:], csum_x[:], ACT.Exp, scale=-DEC).then_inc(prep_act, 1)
                if q in range(PAIRS) and step == 2:
                    act.wait_ge(prep_dve, after(PREP_DVE, q, "recip"))
                    s_.activation(rnorm[:], rnorm[:], ACT.Sqrt).then_inc(prep_act, 1)
                if 19 <= u < 23:
                    act.wait_ge(v_tp, u - 18)
                    o = u - 19
                    s_.activation(vtok[:, :, P * o:P * o + P], quads(4, P), ACT.Copy).then_inc(v_out, 1)
                    s_.activation(vmeta[:, P * o:P * o + P], psum[0:META, 5, 0:P], ACT.Copy).then_inc(v_out, 1)

            act.wait_ge(mix_zero, N_ZERO)
            for kind, n, s in MIXING:
                c = h = n
                e = c % 2
                if kind == "inv" and s[0] in "RW":
                    act.wait_ge(mix_pe, upto(MIX_PE, "inv", c, s))
                    dst, bnk = (x_bd[e], I1[e]) if s[0] == "R" else (w_bd[e], I0[e])
                    s_.activation(dst[:], quads(bnk, P), ACT.Copy).then_inc(mix_act, 1)
                if kind == "seq":
                    for name, it, bnk, dst in (("T0", "F", S1, bh_bd), ("T1", "T", S0, kh_bd)):
                        if s == it and c != LAST_C:
                            act.wait_ge(mix_pe, upto(MIX_PE, "seq", c, name))
                            for i in range(2):
                                s_.activation(top(dst, i), quads(bnk, P)[0:C, :, i * C:(i + 1) * C],
                                              ACT.Copy).then_inc(mix_act, 1)
                    for name, bnk, dst in (("Z", S0, z_bd), ("SA", S1, sa_bd)):
                        if s == name:
                            act.wait_ge(mix_pe, upto(MIX_PE, "seq", c, name))
                            s_.activation(dst[:], quads(bnk, P), ACT.Copy).then_inc(mix_act, 1)
                    if s == "S":
                        act.wait_ge(mix_pe, upto(MIX_PE, "seq", c, "OUT"))
                        s_.activation(ar[:, 0, :, cols(c)], quads(S0, C), ACT.Copy).then_inc(mix_act, 1)
                if kind == "att":
                    hp, hr = h // 2, h % 2
                    z_h = zs[h % 2]
                    if s[0] == "Q":
                        j = int(s[1])
                        rows = META if j == 4 else P
                        act.wait_ge(mix_pe, upto(MIX_PE, "att", h, s))
                        if h == 1:
                            act.wait_ge(zero_1, 1)
                        s_.activation(z_h[0:rows, OFF[j]:OFF[j] + WIDTH[j]], psum[0:rows, QBANK, 0:WIDTH[j]],
                                      ACT.Copy).then_inc(mix_act, 1)
                    if s[0] == "E":
                        act.wait_ge(mix_dve, upto(MIX_DVE, "att", h, f"min{s[1]}"))
                        part = sp_[:, PART[int(s[1])]]
                        s_.activation(part, part, ACT.Exp).then_inc(mix_act, 1)
                    if s[0] == "L":
                        act.wait_ge(mix_act, upto(MIX_ACT, "att", h, f"exp{s[1]}"))
                        part = sp_[:, PART[int(s[1])]]
                        s_.activation(part, part, ACT.Ln, bias=1.0).then_inc(mix_act, 1)
                    if s == "V1":
                        act.wait_ge(mix_dve, upto(MIX_DVE, "att", h, "s2"))
                        w = z_h[:, OFF[2]:OFF[4]]
                        s_.activation(w, w, ACT.Exp).then_inc(mix_act, 1)
                    if s == "V0":
                        act.wait_ge(mix_dve, upto(MIX_DVE, "att", h, "s0"))
                        w = z_h[:, 0:OFF[2]]
                        s_.activation(w, w, ACT.Exp).then_inc(mix_act, 1)
                        act.wait_ge(mix_dve, upto(MIX_DVE, "att", h, "s4"))
                        w = z_h[0:META, OFF[4]:NS]
                        s_.activation(w, w, ACT.Exp).then_inc(mix_act, 1)
                    if s == "O":
                        act.wait_ge(mix_pe, upto(MIX_PE, "att", h, "O"))
                        s_.activation(qT[hr * HD:(hr + 1) * HD, hp, :], psum[hr * HD:(hr + 1) * HD, QBANK, :],
                                      ACT.Copy).then_inc(mix_act, 1)

            for kind, i in LATE:
                if kind == "osb":
                    act.wait_ge(mix_act, len(MIX_ACT))
                    act.wait_ge(mix_pool, len(MIX_POOL))
                    act.wait_ge(mix_pe, len(MIX_PE))
                    act.wait_ge(eps_ok, 2)
                    hi_unit(act, U_MIX + 1)
                    s_.activation(osb_hi[:], qT[:], ACT.Copy).then_inc(osb_h, 1)
                if kind == "mean":
                    for q in range(2):
                        act.wait_ge(post_dve, upto(POST_DVE, "post", i, f"centre{q}"))
                        if i:
                            act.wait_ge(post_pe, upto(POST_PE, "post", i - 1, f"var{q}"))
                        s_.activation(ysq[q][:], y_of(2 * i + q), ACT.Square).then_inc(post_act, 1)
                if kind == "var":
                    for q in range(2):
                        act.wait_ge(post_pe, upto(POST_PE, "post", i, f"var{q}"))
                        if i:
                            act.wait_ge(post_dve, upto(POST_DVE, "post", i - 1, f"recip{q}"))
                        s_.activation(yrs[q][:], bank(6 + q), ACT.Sqrt, bias=small[:, 7:8],
                                      scale=1.0 / HD).then_inc(post_act, 1)
                if kind == "gate":
                    for q in range(2):
                        p = 2 * i + q
                        act.wait_ge(post_dve, upto(POST_DVE, "post", i, f"norm{q}"))
                        s_.activation(y_of(p), y_of(p), ACT.Identity, bias=vcol[:, V_LB + p:V_LB + p + 1],
                                      scale=vcol[:, V_LG + p:V_LG + p + 1]).then_inc(post_act, 1)
                if kind == "out":
                    for q in range(2):
                        act.wait_ge(post_dve, upto(POST_DVE, "post", i, f"out{q}"))
                        s_.activation(orw_hi[:, 2 * i + q, :], yo[q][:], ACT.Copy).then_inc(post_act, 1)
                if kind == "unit":
                    u = U_MIX + i
                    what, j = MERGE[i]
                    act.wait_ge(w_used, u + 1)
                    if what == "branch":
                        hi_unit(act, u + 2)
                        act.wait_ge(mrg_dve, 4 * j + 3)
                        s_.activation(mg_hi[:, j, :], mrg_t[0][:], ACT.Copy).then_inc(mrg_hi, 1)
                    else:
                        n = gate_no(i)
                        if j >= AHEAD:
                            act.wait_ge(mrg_dve, 4 * (j - AHEAD) + 2)
                        s_.activation(sig_t[n % (2 * AHEAD)][:], bank(n % 2), ACT.Sigmoid).then_inc(gate_out, 1)
                        hi_unit(act, u + 2)

            for k in range(KT - 2):
                hi_unit(act, U_OUT + k + 2)

            def tail_root(block, count):
                act.wait_ge(tail_act, count)
                s_.activation(small[:, 16 + block:17 + block], small[:, block:block + 1], ACT.Sqrt,
                              bias=small[:, 6:7], scale=1.0 / D).then_inc(tail_act, 1)

            def tail_square(block, t, done, units, count):
                if t < QB - 1:
                    act.wait_ge(blocks_done, done + t + 1)
                else:
                    act.wait_ge(w_used, units)
                s_.activation(ztok[block][:], psum[:, 2 * block:2 * block + 2, :], ACT.Square,
                              accum_out=small[:, block:block + 1]).then_inc(tail_act, 1)
                tail_root(block, count)

            act.wait_ge(eps_ok, 1)
            for t in range(QB + 2):
                if t < QB:
                    tail_square(OUT_ORDER[t], t, 0, U_FFN, TAIL_1_ACT.index(f"sq{t}") + 1)
                if t == QB:
                    hi_unit(act, U_FFN)
                if 0 <= t - 1 < QB:
                    b = OUT_ORDER[t - 1]
                    if t < QB:
                        act.wait_ge(res_pool, t)
                    else:
                        act.wait_ge(tail_dve, TAIL_1.index(f"res{t - 1}") + 1)
                    s_.activation(ztok[b][:], resid[:, b, :], ACT.Square,
                                  accum_out=small[:, b:b + 1]).then_inc(tail_act, 1)
                    tail_root(b, TAIL_1_ACT.index(f"sq_f{t - 1}") + 1)
                if t == QB:
                    hi_unit(act, U_FFN + 1)
                if 0 <= t - 2 < QB:
                    b = OUT_ORDER[t - 2]
                    norm_hi(10 + 2 * (t - 2), P, P * b, 2 * b)

            with act.Fori(0, N_FFN_LOOP) as i:
                for s in range(RAW):
                    u0 = U_FFN + s
                    act.wait_ge(w_used, i * RAW + (u0 + 1))
                    if s % 2 == 0:
                        t = s // 2
                        act.wait_ge(tail_dve, i * (2 * len(TAIL_FFN)) + (FFN_AT + (t - 2) * len(TAIL_FFN) + 1))
                        s_.activation(ffn_t[t][:], bank(2 * t), ACT.Sigmoid).then_inc(f_sig, 1)
                    v = u0 + 2
                    act.wait_ge(w_in_raw[v % RAW], i * 16 + landed(v))
                    s_.activation(w_hi[v % SPL][:], raw[v % RAW][:], ACT.Copy).then_inc(w_hi_done, 1)
            for k in range(2, FT):
                hi_unit(act, U_DOWN + k)
            for t, b in enumerate(DOWN_ORDER):
                tail_square(b, t, QB - 1, N_UNITS, len(TAIL_1_ACT) + TAIL_2_ACT.index(f"sq{t}") + 1)

        @block.vector
        def _(dve):
            v_ = nc.vector

            def norm_lo(n, width, c0, b=None):
                b = n % 4 if b is None else b
                for h in range(2):
                    dve.wait_ge(n_hi, n + h + 1)
                    v_.tensor_sub(h_lo[:, 4 * h:4 * h + 4, c0:c0 + width], quads(b + h, width),
                                  h_hi[:, 4 * h:4 * h + 4, c0:c0 + width].bitcast(F32)).then_inc(n_lo, 1)

            def mean(i):
                b = BLOCKS[i]
                dve.wait_ge(n_sq, i + 1)
                v_.tensor_scalar(small[:, 8 + b:9 + b], small[:, b:b + 1], 1.0 / D, RMS_EPS,
                                 ALU.mult, ALU.add).then_inc(n_dve, 1)
                dve.wait_ge(n_dve, 2 * i + 2)
                v_.reciprocal(small[:, 16 + b:17 + b], small[:, 8 + b:9 + b]).then_inc(n_dve, 1)

            v_.memset(small[:, 6:7], RMS_EPS).then_inc(eps_ok, 1)
            v_.memset(small[:, 7:8], GN_EPS).then_inc(eps_ok, 1)
            v_.memset(small[:, 0:6], 1.0).then_inc(n_dve, 1)
            mean(0)
            for i, b in enumerate(BLOCKS):
                n = META if b == 4 else P
                if i + 1 < len(BLOCKS):
                    mean(i + 1)
                if i == 0:
                    dve.wait_ge(gain_in, 16)
                dve.wait_ge(n_rs, i + 2)
                v_.scalar_tensor_tensor(xn[b][0:n, :], xb[b][0:n, :], small[0:n, 24 + b:25 + b],
                                        g_row[0:n, :], ALU.mult, ALU.mult).then_inc(n_x, 1)
                if i:
                    norm_lo(2 * i - 2, norm_cols(BLOCKS[i - 1])[1], norm_cols(BLOCKS[i - 1])[0])
            norm_lo(8, norm_cols(3)[1], norm_cols(3)[0])
            dve.wait_ge(w_split, 1)
            lo_unit(dve, 1)
            dve.wait_ge(vec_ok, 1)
            v_.tensor_scalar(vcol[:, NVEC:NVEC + PAIRS], vcol[:, V_KA:V_KA + PAIRS], -1.0, 1.0,
                             ALU.mult, ALU.add).then_inc(vec_ok, 1)
            dve.wait_ge(vec_ok, 2)
            dve.wait_ge(edge, 9)

            n_shift = 0
            for u, (kind, f, p) in enumerate(ORDER):
                if kind in ("xwa", "xg", "r", "k", "v"):
                    st = stage[n_shift % 3]
                    dst = {"xwa": twx[:], "xg": sg[:], "r": rp[p % 2][:], "k": kp[p % 2][:],
                           "v": vv[:, p, PAD:TP]}[kind]
                    dve.wait_ge(in_out, u + 1)
                    if n_shift:
                        dve.wait_ge(shifted, n_shift)
                    v_.tensor_sub(diff[:], st[:, 0:T], st[:, 1:T + 1]).then_inc(sh_diff, 1)
                    dve.wait_ge(sh_diff, n_shift + 1)
                    if kind in ("r", "k") and p >= 2:
                        dve.wait_ge(prep_pool, after(PREP_POOL, p - 2, "r"))
                    mu = V_MU + f - RR
                    v_.scalar_tensor_tensor(dst, diff[:], vcol[:, mu:mu + 1], st[:, 1:T + 1],
                                            ALU.mult, ALU.add).then_inc(shifted, 1)
                    n_shift += 1
                if u + 2 != U_MIX + 1:
                    lo_unit(dve, u + 2)
                q, step = divmod(u - 5, 4)
                if q in range(PAIRS) and step == 0:
                    dve.wait_ge(prep_act, after(PREP_ACT, q, "sig"))
                    if q:
                        dve.wait_ge(prep_act, after(PREP_ACT, q - 1, "exc"))
                    v_.tensor_tensor_scan(csum[:], reset, sig_w[:], 0.0, ALU.mult, ALU.add).then_inc(prep_dve, 1)
                if q - 1 in range(PAIRS) and step == 0:
                    dve.wait_ge(bonus_pe, q)
                    m = HALF - META
                    v_.tensor_mul(bonus[:, q - 1, 0:m], psum[:, 6, META:HALF], vv[:, q - 1, C:C + m])
                    v_.tensor_mul(bonus[:, q - 1, m:SEQ], psum[:, 7, 0:HALF], vv[:, q - 1, C + m:TP]).then_inc(bonus_dve, 1)
                if q in range(PAIRS) and step == 1:
                    dve.wait_ge(prep_pe, after(PREP_PE, q, "norm"))
                    v_.tensor_scalar(halves(ksq[:]), both(4), 1e-24, None, ALU.max).then_inc(prep_dve, 1)
                    dve.wait_ge(prep_dve, after(PREP_DVE, q, "max"))
                    v_.reciprocal(rnorm[:], ksq[:]).then_inc(prep_dve, 1)
                if q in range(PAIRS) and step == 2:
                    dve.wait_ge(prep_pool, after(PREP_POOL, q, "kk"))
                    dve.wait_ge(prep_act, after(PREP_ACT, q, "rnorm"))
                    v_.tensor_mul(kkn[:], kkn[:], rnorm[:]).then_inc(prep_dve, 1)
                    dve.wait_ge(prep_dve, after(PREP_DVE, q, "kkn"))
                    v_.tensor_mul(ar[:, 0, q, PAD:TP], kkn[:], p_exc[:]).then_inc(prep_dve, 1)
                    v_.scalar_tensor_tensor(bneg[:], kkn[:], -1.0, a_gate[:], ALU.mult, ALU.mult).then_inc(prep_dve, 1)
                    dve.wait_ge(prep_dve, after(PREP_DVE, q, "bneg"))
                    v_.tensor_mul(bt[:, q, PAD:TP], bneg[:], p_inv[:]).then_inc(prep_dve, 1)
                    if q:
                        dve.wait_ge(prep_pool, after(PREP_POOL, q - 1, "k"))
                        dve.wait_ge(bonus_pe, q)
                    v_.tensor_scalar(kmod[:], a_gate[:], vcol[:, V_KA + q:V_KA + q + 1],
                                     vcol[:, NVEC + q:NVEC + q + 1], ALU.mult, ALU.add).then_inc(prep_dve, 1)
                    dve.wait_ge(prep_dve, after(PREP_DVE, q, "k_a"))
                    v_.tensor_mul(kmod[:], kmod[:], kp[q % 2][:]).then_inc(prep_dve, 1)
                    dve.wait_ge(prep_dve, after(PREP_DVE, q, "kmod"))
                    v_.scalar_tensor_tensor(rkp[:], rp[q % 2][:], vcol[:, V_RK + q:V_RK + q + 1], kmod[:],
                                            ALU.mult, ALU.mult).then_inc(prep_dve, 1)

            dve.wait_ge(mix_zero, N_ZERO)
            dve.wait_ge(w_split, U_MIX + 1)
            v_.tensor_copy(tri_r[:], consts[:, K_TRI:K_TRI + 2 * P]).then_inc(tri_ok, 1)

            def pairs_of(ap):
                return ap.unsqueeze(1).to_broadcast([P, PAIRS, ap.shape[1]])

            def twice(ap):
                return ap.unsqueeze(2).to_broadcast([P, PAIRS, 2, C])

            def bd4(ap):
                return ap.rearrange("p q (h n) -> p q h n", h=2)

            def mask4(ap):
                return ap.rearrange("p (h n) -> p h n", h=2).unsqueeze(1).to_broadcast([P, PAIRS, 2, C])

            for kind, n, s in MIXING:
                c = h = n
                e = c % 2
                if kind == "inv" and s == "A":
                    dve.wait_ge(mix_pe, upto(MIX_PE, "inv", c, "A"))
                    ab, rb = quads(I0[e], P)[:, :, 0:C], quads(I0[e], P)[:, :, C:P]
                    v_.tensor_tensor(bd4(aab_bd[e]), twice(ab), mask4(bd_strict), ALU.mult).then_inc(mix_dve, 1)
                    dve.wait_ge(mix_pool, upto(MIX_POOL, "inv", c, "ixt"))
                    v_.copy_predicated(bd4(xt_bd[c % 3]), mask4(bytes_[:, 0:P]), twice(ab)).then_inc(mix_dve, 1)
                    v_.tensor_tensor(arb[c % 3][:], rb, pairs_of(st_le), ALU.mult).then_inc(mix_dve, 1)
                if kind == "inv" and s[0] == "Y":
                    dve.wait_ge(mix_pe, upto(MIX_PE, "inv", c, s))
                    m = int(s[1]) * P
                    v_.copy_predicated(xt_bd[c % 3][:], pairs_of(bytes_[:, m:m + P]), quads(I1[e], P)).then_inc(mix_dve, 1)
                if kind == "seq" and s == "F":
                    dve.wait_ge(mix_pe, upto(MIX_PE, "seq", c, "F"))
                    ak, rk = quads(S0, P)[:, :, 0:C], quads(S0, P)[:, :, C:P]
                    v_.tensor_tensor(bd4(aak_bd), twice(ak), mask4(bd_strict), ALU.mult).then_inc(mix_dve, 1)
                    v_.tensor_tensor(ark[:], rk, pairs_of(st_le), ALU.mult).then_inc(mix_dve, 1)
                if kind == "seq" and s == "T":
                    dve.wait_ge(mix_pe, upto(MIX_PE, "seq", c, "T2"))
                    for i in range(2):
                        v_.tensor_copy(top(v_bd, i), quads(S1, P)[0:C, :, i * C:(i + 1) * C]).then_inc(mix_dve, 1)
                if kind == "seq" and s == "SA" and c != LAST_C:
                    dve.wait_ge(mix_pe, upto(MIX_PE, "seq", c, "SA"))
                    pcb = pc[:, :, c:c + 1].to_broadcast([P, PAIRS, P])
                    v_.tensor_tensor(z_bd[:], s_bd[:], pcb, ALU.mult).then_inc(mix_dve, 1)
                if kind == "seq" and s == "S" and c != LAST_C:
                    dve.wait_ge(mix_pe, upto(MIX_PE, "seq", c, "S"))
                    dve.wait_ge(mix_dve, upto(MIX_DVE, "seq", c, "decay"))
                    v_.tensor_tensor(s_bd[:], quads(S1, P), z_bd[:], ALU.add).then_inc(mix_dve, 1)
                if kind == "att" and s == "M":
                    dve.wait_ge(mix_act, upto(MIX_ACT, "att", h, "z4"))
                    dve.wait_ge(mix_pool, upto(MIX_POOL, "att", h, "m3"))
                    if h:
                        dve.wait_ge(mix_pe, upto(MIX_PE, "att", h - 1, "C4"))
                    for i in (1, 0):
                        v_.tensor_scalar(sp_[:, PART[i]], zs[h % 2][:, PART[i]], BIG_Z, None,
                                         ALU.min).then_inc(mix_dve, 1)
                if kind == "att" and s[0] == "L":
                    dve.wait_ge(mix_act, upto(MIX_ACT, "att", h, f"ln{s[1]}"))
                    part = PART[int(s[1])]
                    v_.tensor_tensor(sp_[:, part], sp_[:, part], zs[h % 2][:, part], ALU.max).then_inc(mix_dve, 1)
                if kind == "att" and s[0] == "H":
                    part = PART[int(s[1])]
                    dve.wait_ge(mix_dve, upto(MIX_DVE, "att", h, f"max{s[1]}"))
                    v_.tensor_copy(sp_hi[:, part], sp_[:, part]).then_inc(mix_dve, 1)
                    dve.wait_ge(mix_dve, upto(MIX_DVE, "att", h, f"hi{s[1]}"))
                    v_.tensor_sub(sp_lo[:, part], sp_[:, part], sp_hi[:, part].bitcast(F32)).then_inc(mix_dve, 1)
                if kind == "att" and s[0] == "C":
                    j = int(s[1])
                    rows = META if j == 4 else P
                    dve.wait_ge(mix_pe, upto(MIX_PE, "att", h, s))
                    d = zs[h % 2][0:rows, OFF[j]:OFF[j] + WIDTH[j]]
                    v_.tensor_tensor(d, d, psum[0:rows, CBANK, SEQ - WIDTH[j]:SEQ],
                                     ALU.subtract).then_inc(mix_dve, 1)

            for kind, i in LATE:
                if kind == "osb":
                    lo_unit(dve, U_MIX + 1)
                if kind == "mean":
                    for q in range(2):
                        dve.wait_ge(post_pe, upto(POST_PE, "post", i, f"mean{q}"))
                        y = y_of(2 * i + q)
                        v_.scalar_tensor_tensor(y, bank(4 + q), -1.0 / HD, y, ALU.mult, ALU.add).then_inc(post_dve, 1)
                if kind == "var":
                    for q in range(2):
                        dve.wait_ge(post_act, upto(POST_ACT, "post", i, f"root{q}"))
                        v_.reciprocal(yrec[q][:], yrs[q][:]).then_inc(post_dve, 1)
                if kind == "gate":
                    for q in range(2):
                        y = y_of(2 * i + q)
                        dve.wait_ge(post_dve, upto(POST_DVE, "post", i, f"recip{q}"))
                        v_.tensor_mul(y, y, yrec[q][:]).then_inc(post_dve, 1)
                if kind == "out":
                    for q in range(2):
                        dve.wait_ge(post_pool, upto(POST_POOL, "post", i, f"bonus{q}"))
                        dve.wait_ge(post_pe, upto(POST_PE, "post", i, f"gate{q}"))
                        if i:
                            dve.wait_ge(post_pool, upto(POST_POOL, "post", i - 1, f"lo{q}"))
                        v_.tensor_mul(yo[q][:], bank(2 + 2 * i + q), y_of(2 * i + q)).then_inc(post_dve, 1)
                if kind == "unit":
                    u = U_MIX + i
                    what, j = MERGE[i]
                    lo_unit(dve, u + 2)
                    if what == "branch":
                        n = 2 * j
                        dve.wait_ge(w_used, u + 1)
                        dve.wait_ge(gate_out, n + 2)
                        if j:
                            dve.wait_ge(mrg_dve, 4 * j)
                        b = 2 + 2 * (j % 2)
                        v_.tensor_mul(mrg_t[0][:], bank(b), sig_t[n % (2 * AHEAD)][:]).then_inc(mrg_dve, 1)
                        v_.tensor_mul(mrg_t[1][:], bank(b + 1), sig_t[(n + 1) % (2 * AHEAD)][:]).then_inc(mrg_dve, 1)
                        dve.wait_ge(mrg_dve, 4 * j + 2)
                        v_.tensor_add(mrg_t[0][:], mrg_t[0][:], mrg_t[1][:]).then_inc(mrg_dve, 1)
                        dve.wait_ge(mrg_hi, j + 1)
                        v_.tensor_sub(mg_lo[:, j, :], mrg_t[0][:], mg_hi[:, j, :].bitcast(F32)).then_inc(mrg_dve, 1)

            for k in range(KT - 2):
                lo_unit(dve, U_OUT + k + 2)

            def inverse(b, roots):
                dve.wait_ge(tail_act, roots)
                v_.reciprocal(small[:, 24 + b:25 + b], small[:, 16 + b:17 + b]).then_inc(tail_dve, 1)

            def normed(b, row, rec):
                dve.wait_ge(tail_dve, rec)
                v_.scalar_tensor_tensor(ztok[b][:].rearrange("p (a n) -> p a n", a=2), psum[:, 2 * b:2 * b + 2, :],
                                        small[:, 24 + b:25 + b], grows[:, row, :].rearrange("p (a n) -> p a n", a=2),
                                        ALU.mult, ALU.mult).then_inc(tail_dve, 1)

            def add_residual(b, z):
                dve.wait_ge(tail_dve, z)
                v_.tensor_add(resid[:, b, :], resid[:, b, :], ztok[b][:]).then_inc(tail_dve, 1)

            dve.wait_ge(rows_in, 48)
            dve.wait_ge(resid_in, 16)
            for t in range(QB + 2):
                if t < QB:
                    inverse(OUT_ORDER[t], TAIL_1_ACT.index(f"root{t}") + 1)
                    normed(OUT_ORDER[t], 0, TAIL_1.index(f"rec{t}") + 1)
                    if t == QB - 1:
                        add_residual(OUT_ORDER[t], TAIL_1.index(f"z{t}") + 1)
                if 0 <= t - 1 < QB:
                    b = OUT_ORDER[t - 1]
                    inverse(b, TAIL_1_ACT.index(f"root_f{t - 1}") + 1)
                    dve.wait_ge(tail_dve, TAIL_1.index(f"rec_f{t - 1}") + 1)
                    v_.scalar_tensor_tensor(ztok[b][:], resid[:, b, :], small[:, 24 + b:25 + b],
                                            grows[:, 1, :], ALU.mult, ALU.mult).then_inc(tail_dve, 1)
                if 0 <= t - 2 < QB:
                    b = OUT_ORDER[t - 2]
                    norm_lo(10 + 2 * (t - 2), P, P * b, 2 * b)
            dve.wait_ge(w_split, U_FFN + 2)

            with dve.Fori(0, N_FFN_LOOP) as i:
                per = 2 * len(TAIL_FFN)
                for s in range(RAW):
                    u0 = U_FFN + s
                    v = u0 + 2
                    dve.wait_ge(w_hi_done, i * RAW + (v + 1))
                    v_.tensor_sub(w_lo[v % SPL][:], raw[v % RAW][:], w_hi[v % SPL][:].bitcast(F32)).then_inc(w_split, 1)
                    if s % 2 == 1:
                        t = s // 2
                        at = FFN_AT + t * len(TAIL_FFN)
                        dve.wait_ge(f_sig, i * 2 + (t + 1))
                        v_.tensor_mul(ffn_t[t][:], bank(2 * t), ffn_t[t][:]).then_inc(tail_dve, 1)
                        dve.wait_ge(tail_dve, i * per + (at + 1))
                        v_.tensor_mul(ffn_u[t][:], bank(2 * t + 1), ffn_t[t][:]).then_inc(tail_dve, 1)
                        dve.wait_ge(tail_dve, i * per + (at + 2))
                        tile = i * 2 + t
                        v_.tensor_scalar(act_hi[:, bass.ds(tile, 1), :], ffn_u[t][:].unsqueeze(1), 1.0, None,
                                         ALU.mult).then_inc(tail_dve, 1)
                        dve.wait_ge(tail_dve, i * per + (at + 3))
                        v_.tensor_tensor(act_lo[:, bass.ds(tile, 1), :], ffn_u[t][:].unsqueeze(1),
                                         act_hi[:, bass.ds(tile, 1), :].bitcast(F32),
                                         ALU.subtract).then_inc(tail_dve, 1)
            for k in range(2, FT):
                lo_unit(dve, U_DOWN + k)
            for t, b in enumerate(DOWN_ORDER):
                inverse(b, len(TAIL_1_ACT) + TAIL_2_ACT.index(f"root{t}") + 1)
                normed(b, 2, LAST_AT + TAIL_2.index(f"rec{t}") + 1)
                add_residual(b, LAST_AT + TAIL_2.index(f"z{t}") + 1)

        @block.tensor
        def _(pe):
            t_ = nc.tensor

            def norm_transpose(n, src, width, b=None):
                for h in range(2):
                    if b is None and n >= 4:
                        pe.wait_ge(n_lo, n + h - 3)
                    for k in range(4):
                        f = (4 * h + k) * P
                        mm = t_.transpose(quads((n % 4 if b is None else b) + h, width)[:, k, :], src[0:width, f:f + P],
                                          ident[0:width, 0:width])
                    mm.then_inc(n_tp, 1)

            pe.wait_ge(ident_in, 16)
            for i, b in enumerate(BLOCKS):
                pe.wait_ge(n_x, i + 1)
                norm_transpose(2 * i, xn[b][:, :], META if b == 4 else P)
            pe.wait_ge(vec_in, 16)
            t_.transpose(psum[:, 7, 0:NVEC], vrow[:], ident[0:NVEC, 0:NVEC]).then_inc(vec_tp, 1)
            pe.wait_ge(n_lo, 10)
            pe.wait_ge(vec_ok, 1)

            for u, (kind, f, p) in enumerate(ORDER):
                pe.wait_ge(w_split, u + 1)
                if u >= 2:
                    pe.wait_ge(in_out, u - 1)
                b = 2 * (u % 2)
                if kind == "sq":
                    outs = [(bank(b), (META, T))]
                else:
                    outs = [(bank(b, HALF), (0, HALF)), (bank(b + 1, HALF), (HALF, T))]
                products(u, 0, outs, h_hi, h_lo, range(KT)).then_inc(w_used, 1)

                q, step = divmod(u - 5, 4)
                hv = ((0, HALF), (HALF, T))
                if u == 2:
                    pe.wait_ge(const_in, 16 * 5)
                if q in range(PAIRS) and step == 0:
                    pe.wait_ge(lora_act, 1)
                    if q:
                        pe.wait_ge(prep_dve, after(PREP_DVE, q - 1, "max"))
                    for i, (c0, c1) in enumerate(hv):
                        mm = t_.matmul(bank(4 + i, HALF), lora[0:64, q * P:q * P + P], twx[0:64, c0:c1], start=True, stop=True)
                    mm.then_inc(prep_pe, 1)
                if q - 1 in range(PAIRS) and step == 0:
                    pe.wait_ge(prep_dve, after(PREP_DVE, q - 1, "rk"))
                    for i, (c0, c1) in enumerate(hv):
                        mm = t_.matmul(bank(6 + i, HALF), blk, rkp[:, c0:c1], start=True, stop=True)
                    mm.then_inc(bonus_pe, 1)
                if q in range(PAIRS) and step == 1:
                    if q:
                        pe.wait_ge(bonus_dve, q)
                    pe.wait_ge(shifted, 1)
                    for i, (c0, c1) in enumerate(hv):
                        mm = t_.matmul(bank(6 + i, HALF), lora[64:P, q * P:q * P + P], twx[64:P, c0:c1], start=True, stop=True)
                    mm.then_inc(prep_pe, 1)
                    pe.wait_ge(prep_act, after(PREP_ACT, q, "ksq"))
                    for i, (c0, c1) in enumerate(hv):
                        mm = t_.matmul(bank(4 + i, HALF), blk, ksq[:, c0:c1], start=True, stop=True)
                    mm.then_inc(prep_pe, 1)
                if 19 <= u < 23:
                    o = u - 19
                    pe.wait_ge(in_out, u)
                    if o == 0:
                        pe.wait_ge(prep_dve, after(PREP_DVE, PAIRS - 1, "max"))
                    else:
                        pe.wait_ge(v_out, 2 * o)
                    for b4 in range(QB):
                        t_.transpose(quads(4, P)[:, b4, :], vst[o % 2][:, META + P * b4:META + P * b4 + P], ident)
                    t_.transpose(psum[0:META, 5, 0:P], vst[o % 2][:, 0:META], ident).then_inc(v_tp, 1)

            pe.wait_ge(in_out, N_IN - 1)
            pe.wait_ge(v_out, 2 * PAIRS)
            pe.wait_ge(prep_dve, PAIRS * len(PREP_DVE))
            pe.wait_ge(bonus_dve, PAIRS)
            pe.wait_ge(mix_zero, N_ZERO)
            pe.wait_ge(w_split, U_MIX + 1)

            def pairs(outs, terms):
                for p in range(PAIRS):
                    for i, (w, m) in enumerate(terms):
                        mm = t_.matmul(outs[:, p, :], w(p), m(p), start=(i == 0), stop=(i == len(terms) - 1))
                return mm

            def whole(t):
                return lambda p: t[:, p, :]

            LAST = LEVELS - 1
            pe.wait_ge(tri_ok, 1)
            for kind, n, s in MIXING:
                c = h = n
                e = c % 2
                at_c = lambda t: lambda p: t[:, p, cols(c)]
                a_and_r = lambda p: ar[:, :, p, cols(c)]
                if kind == "inv" and s == "A":
                    pe.wait_ge(mix_pool, upto(MIX_POOL, "inv", c, "b1"))
                    if c == 1:
                        pe.wait_ge(in_out, N_IN)
                    if c >= 2:
                        pe.wait_ge(mix_act, upto(MIX_ACT, "inv", c - 2, f"w{LAST}"))
                    pairs(quads(I0[e], P), [(whole(b_bd), a_and_r)]).then_inc(mix_pe, 1)
                if kind == "inv" and s[0] == "R":
                    pe.wait_ge(mix_dve, upto(MIX_DVE, "inv", c, f"xt{s[1]}"))
                    for p in range(PAIRS):
                        mm = t_.transpose(quads(I1[e], P)[:, p, :], xt_bd[c % 3][:, p, :], ident)
                    mm.then_inc(mix_pe, 1)
                if kind == "inv" and s[0] == "W":
                    j = int(s[1])
                    pe.wait_ge(mix_act, upto(MIX_ACT, "inv", c, f"x{j - 1}"))
                    if j == 1:
                        pe.wait_ge(mix_dve, upto(MIX_DVE, "inv", c, "arb"))
                    pairs(quads(I0[e], P), [(whole(aab_bd[e]), whole(x_bd[e]))]).then_inc(mix_pe, 1)
                if kind == "inv" and s[0] == "Y":
                    pe.wait_ge(mix_act, upto(MIX_ACT, "inv", c, f"w{s[1]}"))
                    pairs(quads(I1[e], P), [(whole(w_bd[e]), whole(xt_bd[c % 3]))]).then_inc(mix_pe, 1)
                if kind == "seq" and s in ("F", "T"):
                    if s == "F":
                        pe.wait_ge(mix_pool, upto(MIX_POOL, "seq", c, "k1"))
                        if c:
                            pe.wait_ge(mix_act, upto(MIX_ACT, "seq", c - 1, "out"))
                        pairs(quads(S0, P), [(whole(k_bd), a_and_r)]).then_inc(mix_pe, 1)
                        turns = ((bt, S1),) if c != LAST_C else ()
                        if turns:
                            pe.wait_ge(mix_pool, upto(MIX_POOL, "seq", c, "bh"))
                            if c:
                                pe.wait_ge(mix_dve, upto(MIX_DVE, "seq", c - 1, "s"))
                    else:
                        pe.wait_ge(mix_dve, upto(MIX_DVE, "seq", c, "ark"))
                        turns = ((kt, S0), (vv, S1)) if c != LAST_C else ((vv, S1),)
                    for src, bnk in turns:
                        if src is vv and c != LAST_C:
                            pe.wait_ge(mix_act, upto(MIX_ACT, "seq", c, "bh1"))
                        for p in range(PAIRS):
                            mm = t_.transpose(quads(bnk, P)[0:C, p, :], src[:, p, cols(c)], ident)
                        mm.then_inc(mix_pe, 1)
                if kind == "seq" and s == "Z":
                    if c != LAST_C:
                        pe.wait_ge(mix_act, upto(MIX_ACT, "seq", c, "kh1"))
                    pe.wait_ge(mix_dve, upto(MIX_DVE, "seq", c, "v1"))
                    pe.wait_ge(mix_pool, upto(MIX_POOL, "seq", c, "a1"))
                    pairs(quads(S0, P), [(whole(a_bd), whole(s_bd)), (whole(aak_bd), whole(v_bd))][0 if c else 1:]).then_inc(mix_pe, 1)
                if kind == "seq" and s == "SA":
                    pe.wait_ge(mix_act, upto(MIX_ACT, "seq", c, "z"))
                    pe.wait_ge(mix_dve, upto(MIX_DVE, "inv", c, f"xt{LAST}"))
                    pairs(quads(S1, P), [(whole(xt_bd[c % 3]), whole(z_bd))]).then_inc(mix_pe, 1)
                    if c == LAST_C:
                        products(U_MIX, 0, [(bank(0), (META, T))], h_hi, h_lo, range(KT)).then_inc(w_used, 1)
                if kind == "seq" and s == "S":
                    pe.wait_ge(mix_act, upto(MIX_ACT, "seq", c, "sa"))
                    r_c = lambda p: ar[:, 1, p, cols(c)]
                    pairs(quads(S0, C), [(whole(s_bd), r_c), (whole(v_bd), whole(ark)),
                                         (whole(sa_bd), whole(arb[c % 3]))][0 if c else 1:]).then_inc(mix_pe, 1)
                    if c == LAST_C:
                        continue
                    pairs(quads(S1, P), [(whole(bh_bd), whole(sa_bd)), (whole(kh_bd), whole(v_bd))]).then_inc(mix_pe, 1)
                if kind == "att":
                    hp, hr = h // 2, h % 2
                    rows = slice(hr * HD, (hr + 1) * HD)
                    if s[0] == "Q":
                        j = int(s[1])
                        k0, kn = KEYS[j]
                        if j:
                            pe.wait_ge(mix_act, upto(MIX_ACT, "att", h, f"z{j - 1}"))
                        elif h >= 2:
                            pe.wait_ge(mix_act, upto(MIX_ACT, "att", h - 2, "o"))
                        elif h:
                            pe.wait_ge(mix_act, upto(MIX_ACT, "att", 0, "z4"))
                        t_.matmul(psum[0:kn, QBANK, 0:WIDTH[j]], kT[rows, hp, k0:k0 + kn],
                                  qT[rows, hp, SEQ - WIDTH[j]:SEQ], start=True, stop=True).then_inc(mix_pe, 1)
                    if s[0] == "C":
                        j = int(s[1])
                        kn = KEYS[j][1]
                        if j == 3:
                            pe.wait_ge(mix_dve, upto(MIX_DVE, "att", h, "lo1"))
                        else:
                            i = 0 if j == 4 else j + 1
                            pe.wait_ge(mix_dve, upto(MIX_DVE, "att", h, f"s{i}"))
                            for part in (sp_hi, sp_lo):
                                t_.matmul(psum[:, CBANK, SEQ - WIDTH[i]:SEQ], tri_r[:, P:2 * P],
                                          part[:, OFF[i]:OFF[i] + WIDTH[i]], start=False, stop=False,
                                          skip_group_check=True)
                        for part in (sp_hi, sp_lo):
                            mm = t_.matmul(psum[0:kn, CBANK, SEQ - WIDTH[j]:SEQ], tri_r[0:kn, 0:kn],
                                           part[0:kn, OFF[j]:OFF[j] + WIDTH[j]], start=(j == 3 and part is sp_hi),
                                           stop=(j == 4 and part is sp_lo), skip_group_check=True)
                        mm.then_inc(mix_pe, 1)
                    if s == "O":
                        ps = psum[rows, QBANK, :]
                        z_h = zs[h % 2]
                        pe.wait_ge(mix_act, upto(MIX_ACT, "att", h, "wm"))
                        vc = slice(h * HD, (h + 1) * HD)
                        t_.matmul(ps, vmeta[:, vc], z_h[0:META, OFF[4]:NS], start=True, stop=False)
                        for j in range(QB):
                            mm = t_.matmul(ps[:, SEQ - WIDTH[j]:SEQ], vtok[:, j, vc], z_h[:, OFF[j]:OFF[j] + WIDTH[j]],
                                           start=False, stop=(j == QB - 1))
                        mm.then_inc(mix_pe, 1)

            for kind, i in LATE:
                if kind == "osb":
                    pe.wait_ge(mix_act, len(MIX_ACT))
                    pe.wait_ge(mix_dve, len(MIX_DVE))
                if kind == "mean":
                    for q in range(2):
                        if i:
                            pe.wait_ge(post_dve, upto(POST_DVE, "post", i - 1, f"centre{q}"))
                        t_.matmul(bank(4 + q), blk, y_of(2 * i + q), start=True, stop=True).then_inc(post_pe, 1)
                if kind == "var":
                    for q in range(2):
                        pe.wait_ge(post_act, upto(POST_ACT, "post", i, f"sq{q}"))
                        if i:
                            pe.wait_ge(post_act, upto(POST_ACT, "post", i - 1, f"root{q}"))
                        t_.matmul(bank(6 + q), blk, ysq[q][:], start=True, stop=True).then_inc(post_pe, 1)
                if kind == "gate":
                    for q in range(2):
                        if i:
                            pe.wait_ge(post_dve, upto(POST_DVE, "post", i, f"centre{q}"))
                        f0 = (2 * i + q) * P
                        t_.matmul(bank(2 + 2 * i + q), gup[:, f0:f0 + P], sg[:, META:T], start=True, stop=True).then_inc(post_pe, 1)
                if kind == "unit":
                    u = U_MIX + i
                    what, j = MERGE[i]
                    if i == 0:
                        continue
                    pe.wait_ge(w_split, u + 1)
                    if what == "branch":
                        if j == 0:
                            pe.wait_ge(osb_l, 1)
                        if j >= 2:
                            pe.wait_ge(mrg_dve, 4 * (j - 2) + 2)
                        b = 2 + 2 * (j % 2)
                        products(u, 0, [(bank(b), (0, SEQ))], osb_hi, osb_lo, range(PAIRS))
                        if j == 0:
                            pe.wait_ge(post_dve, len(POST_DVE))
                            pe.wait_ge(post_pool, len(POST_POOL))
                        products(u, PAIRS, [(bank(b + 1), (0, SEQ))], orw_hi, orw_lo, range(PAIRS)).then_inc(w_used, 1)
                    else:
                        n = gate_no(i)
                        if n >= 2:
                            pe.wait_ge(gate_out, n - 1)
                        products(u, 0, [(bank(n % 2), (META, T))], h_hi, h_lo, range(KT)).then_inc(w_used, 1)

            def token_major(u0, n, hi, lo, order, before):
                early, late = order[:2], order[2:]
                turns = [(k, b) for bs in (early, late) for k in range(2) for b in bs] + \
                        [(k, b) for k in range(2, n - 2) for b in order] + \
                        [(k, b) for b in order for k in range(n - 2, n)]
                for k, b in turns:
                    if b == order[0]:
                        pe.wait_ge(w_split, u0 + k + 1)
                    before(k, b)
                    x_w = ((hi, w_hi[(u0 + k) % SPL]), (hi, w_lo[(u0 + k) % SPL]), (lo, w_hi[(u0 + k) % SPL]))
                    for i, (xs, w) in enumerate(x_w):
                        for h in range(2):
                            mm = t_.matmul(bank(2 * b + h), xs[:, k, P * b:P * b + P], w[:, 512 * h:512 * h + 512],
                                           start=(k == 0 and i == 0), stop=(k == n - 1 and i == 2))
                    if b == order[-1]:
                        mm.then_inc(w_used, 1)
                    elif k == n - 1:
                        mm.then_inc(blocks_done, 1)

            def merged(k, b):
                if b == 3:
                    pe.wait_ge(mrg_dve, 4 * (k + 1))
                if k == 0 and b in (1, 2):
                    pe.wait_ge(mrg_dve, 4 * (KT - 3 + b) + 2)

            def activated(k, b):
                if k == 0 and b == 2:
                    pe.wait_ge(tail_dve, FFN_AT + (FT - 2) * len(TAIL_FFN))
                if k == 0 and b == 0:
                    pe.wait_ge(tail_dve, LAST_AT)

            pe.wait_ge(gate_out, 2 * KT)
            token_major(U_OUT, KT, mg_hi, mg_lo, OUT_ORDER, merged)

            for n, b in enumerate(OUT_ORDER):
                pe.wait_ge(tail_dve, TAIL_1.index(f"xn{n}") + 1)
                norm_transpose(10 + 2 * n, ztok[b][:, :], P, 2 * b)
            pe.wait_ge(n_lo, 18)
            with pe.Fori(0, N_FFN_LOOP) as i:
                per = 2 * len(TAIL_FFN)
                for s in range(RAW):
                    u = U_FFN + s
                    t = s // 2
                    pe.wait_ge(w_split, i * RAW + (u + 1))
                    step = 1 + s % 2
                    pe.wait_ge(tail_dve, i * per + (FFN_AT + (t - 2) * len(TAIL_FFN) + step))
                    products(u, 0, [(bank(s), (0, SEQ))], h_hi, h_lo, range(KT)).then_inc(w_used, 1)
            token_major(U_DOWN, FT, act_hi, act_lo, DOWN_ORDER, activated)


def tables():
    import numpy as np

    i = np.arange(P)
    row, col = i[:, None], i[None, :]
    f = np.zeros((P, NK), np.float32)
    f[:, K_ID:K_ID + P] = row == col
    f[:, K_TRI:K_TRI + P] = row >= col
    f[:, K_CTRI:K_CTRI + P] = row < col
    head = row // C == col // C
    f[:, K_BLK:K_BLK + P] = head
    f[:, K_BDS:K_BDS + P] = head & (row < col)
    s, t = i[:, None] % C, np.arange(C)[None, :]
    f[:, K_LE:K_LE + C] = s <= t
    f[:, K_RST:K_RST + T] = (np.arange(T)[None, :] + PAD) % C != 0
    b = np.zeros((P, NB), np.float32)
    for j in range(LEVELS):
        def joins(t, s):
            return (t >> (j + 1) == s >> (j + 1)) & (t >> j & 1 == 1) & (s >> j & 1 == 0)
        b[:, j * P:(j + 1) * P] = head & joins(col % C, row % C)
    return f, b


def kernel(**inputs):
    import numpy as np
    import concourse.bacc as bacc
    from concourse.bass_utils import run_bass_kernel_spmd

    a = {k: np.ascontiguousarray(v) for k, v in inputs.items()}
    vecs = np.concatenate([a[k].reshape(-1, P) for k in (
        "rw_shift_mu", "rw_decay_base", "rw_aaa_base", "rw_k_k", "rw_k_a", "rw_r_k", "rw_ln_gain", "rw_ln_bias")])
    kf, kb = tables()
    arrays = {
        "x": a["x"][0], "meta": a["meta_tokens"], "w_in": a["w_in"][0], "w_sb": a["w_branch_sb"][0],
        "w_rw": a["w_branch_rw"][0], "w_out": a["w_out"][0], "w_g": a["w_ffn_gate"][0],
        "w_u": a["w_ffn_up"][0], "w_d": a["w_ffn_down"][0], "decay_up": a["rw_decay_up"][0],
        "aaa_up": a["rw_aaa_up"][0], "gate_up": a["rw_gate_up"][0], "vecs": vecs,
        "g_mix_pre": a["norm_mix_pre"], "g_mix_post": a["norm_mix_post"],
        "g_ffn_pre": a["norm_ffn_pre"], "g_ffn_post": a["norm_ffn_post"], "kf": kf, "kb": kb,
    }
    nc = bacc.Bacc("TRN2", target_bir_lowering=False, num_devices=1)
    args = [nc.dram_tensor(f"in_{n}", v.shape, mybir.dt.from_np(v.dtype), kind="ExternalInput").ap()
            for n, v in arrays.items()]
    out = nc.dram_tensor("out", (SEQ, D), F32, kind="ExternalOutput").ap()
    build(nc, *args, out)
    r = run_bass_kernel_spmd(nc, [{f"in_{n}": np.ascontiguousarray(v) for n, v in arrays.items()}], core_ids=[0])
    return r.results[0]["out"].reshape(1, SEQ, D)
```
